# Optimizing a Trainium2 kernel written in Bass

```python
import jax
import jax.numpy as jnp
from jax import lax
import numpy as np
import math
import jax, jax.numpy as jnp

D_MODEL = 1024
BATCH = 1
SEQ = 256
DEPTH = 2

CHUNK = 64
EPS = 1e-6
CONV_CH = D_MODEL // 2
CONV_WIDTH = 31
GLA_HEADS = 4
GLA_DK = D_MODEL // 16
GLA_DV = D_MODEL // 8
GLA_GATE_RANK = 16
GLA_GATE_TAU = 16.0
FOX_HEADS = 16
FOX_HD = D_MODEL // FOX_HEADS
Q_BLOCK = 128
PEER_HEADS = 8
PEER_NKEYS = 128
PEER_N = PEER_NKEYS * PEER_NKEYS
PEER_QDIM = 256
PEER_TOPK = 16
PEER_TOKEN_BLOCK = 128

EVEN_IN = 2 * CONV_CH + 2 * GLA_HEADS * GLA_DK + 2 * GLA_HEADS * GLA_DV + GLA_GATE_RANK
ODD_IN = 3 * FOX_HEADS * FOX_HD + FOX_HEADS


def rms_norm(x, g):
    xf = x.astype(jnp.float32)
    y = xf * lax.rsqrt(jnp.mean(xf * xf, axis=-1, keepdims=True) + EPS)
    return (y * g.astype(jnp.float32)).astype(x.dtype)

def layer_norm(x, g, b):
    xf = x.astype(jnp.float32)
    mu = jnp.mean(xf, axis=-1, keepdims=True)
    xc = xf - mu
    y = xc * lax.rsqrt(jnp.mean(xc * xc, axis=-1, keepdims=True) + EPS)
    return (y * g.astype(jnp.float32) + b.astype(jnp.float32)).astype(x.dtype)

def conformer_conv(val, gate, conv_w, conv_b, ln_g, ln_b):
    u = val * jax.nn.sigmoid(gate)
    w = conv_w.astype(u.dtype)[:, None, :]
    y = lax.conv_general_dilated(u, w, window_strides=(1,), padding=[(CONV_WIDTH - 1, 0)],
                                 dimension_numbers=('NWC', 'WIO', 'NWC'),
                                 feature_group_count=u.shape[-1])
    y = y + conv_b.astype(y.dtype)
    return jax.nn.silu(layer_norm(y, ln_g, ln_b))

def gla_chunked(q, k, v, log_a):
    B, S, H, dk = q.shape
    dv = v.shape[-1]
    n = S // CHUNK

    def to_chunks(t):
        return t.reshape(B, n, CHUNK, H, t.shape[-1]).transpose(1, 0, 3, 2, 4)

    qc, kc, vc, gc = to_chunks(q * (dk ** -0.5)), to_chunks(k), to_chunks(v), to_chunks(log_a)
    causal = jnp.tril(jnp.ones((CHUNK, CHUNK), dtype=bool))

    def step(state, inp):
        qi, ki, vi, gi = inp
        b = jnp.cumsum(gi, axis=2)
        b_last = b[:, :, -1:, :]
        o_inter = jnp.einsum('bhtk,bhkv->bhtv', qi * jnp.exp(b), state)
        diff = b[:, :, :, None, :] - b[:, :, None, :, :]
        decay = jnp.exp(jnp.where(causal[:, :, None], diff, -jnp.inf))
        attn = jnp.einsum('bhtk,bhsk,bhtsk->bhts', qi, ki, decay)
        o = o_inter + jnp.einsum('bhts,bhsv->bhtv', attn, vi)
        k_dec = ki * jnp.exp(b_last - b)
        new_state = state * jnp.exp(b_last[:, :, 0, :, None]) + jnp.einsum('bhsk,bhsv->bhkv', k_dec, vi)
        return new_state, o

    s0 = jnp.zeros((B, H, dk, dv), jnp.float32)
    _, o = lax.scan(step, s0, (qc, kc, vc, gc))
    return o.transpose(1, 0, 3, 2, 4).reshape(B, S, H, dv)

def even_mix(h, w_in, conv_w, conv_b, ln_g, ln_b, gate_w2, gate_b, gla_norm_g, w_out):
    B, S, _ = h.shape
    hk = GLA_HEADS * GLA_DK
    hv = GLA_HEADS * GLA_DV
    p = h @ w_in
    cuts = [int(c) for c in np.cumsum([CONV_CH, CONV_CH, hk, hk, hv, hv])]
    a_val, a_gate, q, k, v, r, glr = jnp.split(p, cuts, axis=-1)
    y_a = conformer_conv(a_val, a_gate, conv_w, conv_b, ln_g, ln_b)
    f32 = jnp.float32
    log_a = jax.nn.log_sigmoid((glr @ gate_w2 + gate_b).astype(f32)) / GLA_GATE_TAU
    o = gla_chunked(q.reshape(B, S, GLA_HEADS, GLA_DK).astype(f32),
                    k.reshape(B, S, GLA_HEADS, GLA_DK).astype(f32),
                    v.reshape(B, S, GLA_HEADS, GLA_DV).astype(f32),
                    log_a.reshape(B, S, GLA_HEADS, GLA_DK))
    o = rms_norm(o, gla_norm_g).reshape(B, S, hv).astype(h.dtype)
    y_b = o * jax.nn.silu(r)
    return jnp.concatenate([y_a, y_b], axis=-1) @ w_out

def fox_mix(h, w_in, fgate_b, q_g, k_g, w_out):
    B, S, _ = h.shape
    hd = FOX_HEADS * FOX_HD
    p = h @ w_in
    q, k, v, fz = jnp.split(p, [hd, 2 * hd, 3 * hd], axis=-1)
    q = rms_norm(q.reshape(B, S, FOX_HEADS, FOX_HD), q_g).transpose(0, 2, 1, 3)
    k = rms_norm(k.reshape(B, S, FOX_HEADS, FOX_HD), k_g).transpose(0, 2, 1, 3)
    v = v.reshape(B, S, FOX_HEADS, FOX_HD).transpose(0, 2, 1, 3)
    f32 = jnp.float32
    log_f = jax.nn.log_sigmoid(fz.astype(f32) + fgate_b.astype(f32))
    c = jnp.cumsum(log_f, axis=1).transpose(0, 2, 1)
    scale = FOX_HD ** -0.5
    pos = jnp.arange(S)
    outs = []
    for i in range(S // Q_BLOCK):
        lo, hi = i * Q_BLOCK, (i + 1) * Q_BLOCK
        logits = jnp.einsum('bhqd,bhkd->bhqk', q[:, :, lo:hi], k[:, :, :hi]).astype(f32) * scale
        logits = logits + c[:, :, lo:hi, None] - c[:, :, None, :hi]
        mask = pos[lo:hi, None] >= pos[None, :hi]
        probs = jax.nn.softmax(jnp.where(mask, logits, -jnp.inf), axis=-1)
        outs.append(jnp.einsum('bhqk,bhkd->bhqd', probs.astype(v.dtype), v[:, :, :hi]))
    o = jnp.concatenate(outs, axis=2).transpose(0, 2, 1, 3).reshape(B, S, hd)
    return o @ w_out

def peer_ffn(h, wq, keys, u, v):
    B, S, D = h.shape
    f32 = jnp.float32
    half = PEER_QDIM // 2
    q = (h @ wq).reshape(B, S, PEER_HEADS, 2, half).astype(f32)
    s1 = jnp.einsum('bshd,hnd->bshn', q[..., 0, :], keys[:, 0].astype(f32))
    s2 = jnp.einsum('bshd,hnd->bshn', q[..., 1, :], keys[:, 1].astype(f32))
    v1, i1 = lax.top_k(s1, PEER_TOPK)
    v2, i2 = lax.top_k(s2, PEER_TOPK)
    cand = (v1[..., :, None] + v2[..., None, :]).reshape(B, S, PEER_HEADS, PEER_TOPK * PEER_TOPK)
    sc, j = lax.top_k(cand, PEER_TOPK)
    e1 = jnp.take_along_axis(i1, j // PEER_TOPK, axis=-1)
    e2 = jnp.take_along_axis(i2, j % PEER_TOPK, axis=-1)
    experts = e1 * PEER_NKEYS + e2
    gates = jax.nn.softmax(sc, axis=-1)
    nb = (B * S) // PEER_TOKEN_BLOCK
    ne = PEER_HEADS * PEER_TOPK
    hb = h.reshape(nb, PEER_TOKEN_BLOCK, D)
    eb = experts.reshape(nb, PEER_TOKEN_BLOCK, ne)
    gb = gates.reshape(nb, PEER_TOKEN_BLOCK, ne).astype(h.dtype)

    def block(args):
        ht, et, gt = args
        act = jax.nn.gelu(jnp.einsum('td,ted->te', ht, u[et]), approximate=False)
        return jnp.einsum('te,ted->td', gt * act, v[et])

    out = lax.map(block, (hb, eb, gb))
    return out.reshape(B, S, D)

def first_inputs(seed: int = 0) -> dict:
    key = jax.random.key(seed)
    ks = iter(jax.random.split(key, 32))
    n_even = (DEPTH + 1) // 2
    n_odd = DEPTH // 2
    f32 = jnp.float32
    D = D_MODEL

    def nrm(shape, scale):
        return jax.random.normal(next(ks), shape, f32) * scale

    def gain(shape):
        return 1.0 + 0.05 * jax.random.normal(next(ks), shape, f32)

    return {
        'x': nrm((BATCH, SEQ, D), 1.0),
        'ev_norm_mix': gain((n_even, D)),
        'ev_w_in': nrm((n_even, D, EVEN_IN), D ** -0.5),
        'ev_conv_w': nrm((n_even, CONV_WIDTH, CONV_CH), CONV_WIDTH ** -0.5),
        'ev_conv_b': nrm((n_even, CONV_CH), 0.02),
        'ev_conv_ln_g': gain((n_even, CONV_CH)),
        'ev_conv_ln_b': nrm((n_even, CONV_CH), 0.02),
        'ev_gate_w2': nrm((n_even, GLA_GATE_RANK, GLA_HEADS * GLA_DK), GLA_GATE_RANK ** -0.5),
        'ev_gate_b': nrm((n_even, GLA_HEADS * GLA_DK), 0.1),
        'ev_gla_norm_g': gain((n_even, GLA_DV)),
        'ev_w_out': nrm((n_even, CONV_CH + GLA_HEADS * GLA_DV, D), (CONV_CH + GLA_HEADS * GLA_DV) ** -0.5),
        'od_norm_mix': gain((n_odd, D)),
        'od_w_in': nrm((n_odd, D, ODD_IN), D ** -0.5),
        'od_fgate_b': jax.random.uniform(next(ks), (n_odd, FOX_HEADS), f32, minval=1.0, maxval=4.0),
        'od_q_norm_g': gain((n_odd, FOX_HD)),
        'od_k_norm_g': gain((n_odd, FOX_HD)),
        'od_w_out': nrm((n_odd, FOX_HEADS * FOX_HD, D), (FOX_HEADS * FOX_HD) ** -0.5),
        'ffn_norm': gain((DEPTH, D)),
        'peer_wq': nrm((DEPTH, D, PEER_HEADS * PEER_QDIM), D ** -0.5),
        'peer_keys': nrm((DEPTH, PEER_HEADS, 2, PEER_NKEYS, PEER_QDIM // 2), (PEER_QDIM // 2) ** -0.5),
        'peer_u': nrm((DEPTH, PEER_N, D), D ** -0.5),
        'peer_v': nrm((DEPTH, PEER_N, D), (PEER_HEADS * PEER_TOPK) ** -0.5),
    }

def first_block(x, ev_norm_mix, ev_w_in, ev_conv_w, ev_conv_b, ev_conv_ln_g, ev_conv_ln_b,
              ev_gate_w2, ev_gate_b, ev_gla_norm_g, ev_w_out,
              od_norm_mix, od_w_in, od_fgate_b, od_q_norm_g, od_k_norm_g, od_w_out,
              ffn_norm, peer_wq, peer_keys, peer_u, peer_v):
    for layer in range(DEPTH):
        j = layer // 2
        if layer % 2 == 0:
            h = rms_norm(x, ev_norm_mix[j])
            x = x + even_mix(h, ev_w_in[j], ev_conv_w[j], ev_conv_b[j], ev_conv_ln_g[j], ev_conv_ln_b[j],
                             ev_gate_w2[j], ev_gate_b[j], ev_gla_norm_g[j], ev_w_out[j])
        else:
            h = rms_norm(x, od_norm_mix[j])
            x = x + fox_mix(h, od_w_in[j], od_fgate_b[j], od_q_norm_g[j], od_k_norm_g[j], od_w_out[j])
        h = rms_norm(x, ffn_norm[layer])
        x = x + peer_ffn(h, peer_wq[layer], peer_keys[layer], peer_u[layer], peer_v[layer])
    return x


DEPTH_2 = 1

HEAD_DIM = 64
NSA_HEADS = 8
NSA_KV_HEADS = 2
NSA_GROUP = NSA_HEADS // NSA_KV_HEADS
SB_HEADS = 8
CMP_BLOCK = 32
CMP_STRIDE = 16
CMP_HIDDEN = HEAD_DIM
SEL_BLOCK = 64
SEL_TOPK = 16
WINDOW = 512
NSA_QBLOCK = 64
SB_QBLOCK = 128
N_BUCKETS = 32
MAX_DISTANCE = 128
D_FF = 4 * D_MODEL
FORCED_BONUS = 1e4
NEG_BLOCK = -1e9
NEG_LOGIT = -1e30

Q_A_W = NSA_HEADS * HEAD_DIM
KV_A_W = NSA_KV_HEADS * HEAD_DIM
GATE_A_W = NSA_HEADS * 3
SB_W = SB_HEADS * HEAD_DIM
IN_SPLITS = (Q_A_W, KV_A_W, KV_A_W, KV_A_W, KV_A_W, KV_A_W, KV_A_W, GATE_A_W, SB_W, SB_W, SB_W, D_MODEL, D_MODEL)
IN_WIDTH = Q_A_W + 6 * KV_A_W + GATE_A_W + 3 * SB_W + 2 * D_MODEL


def rms_norm_2(x, g):
    x32 = x.astype(jnp.float32)
    y = x32 * lax.rsqrt(jnp.mean(x32 * x32, axis=-1, keepdims=True) + EPS)
    return (y * g.astype(jnp.float32)).astype(x.dtype)

def rel_bucket(dist):
    n = jnp.maximum(dist, 0)
    max_exact = N_BUCKETS // 2
    nf = jnp.maximum(n, 1).astype(jnp.float32)
    large = max_exact + (jnp.log(nf / max_exact) / math.log(MAX_DISTANCE / max_exact) * (N_BUCKETS - max_exact)).astype(jnp.int32)
    large = jnp.minimum(large, N_BUCKETS - 1)
    return jnp.where(n < max_exact, n, large)

def masked_softmax(logits, mask):
    masked = jnp.where(mask, logits, NEG_LOGIT)
    m = jnp.max(masked, axis=-1, keepdims=True)
    e = jnp.where(mask, jnp.exp(masked - m), 0.0)
    return e / jnp.maximum(jnp.sum(e, axis=-1, keepdims=True), 1e-30)

def compress_blocks(src, pos, w1, w2):
    B, S = src.shape[0], src.shape[1]
    nc = (S - CMP_BLOCK) // CMP_STRIDE + 1
    idx = jnp.arange(nc)[:, None] * CMP_STRIDE + jnp.arange(CMP_BLOCK)[None, :]
    blk = src[:, idx] + pos[None, None, :, None, :]
    blk = blk.transpose(0, 1, 3, 2, 4).reshape(B, nc, NSA_KV_HEADS, CMP_BLOCK * HEAD_DIM)
    return jax.nn.silu(blk @ w1) @ w2

def cmp_to_sel_overlap(nc, nsel):
    c_start = jnp.arange(nc) * CMP_STRIDE
    s_start = jnp.arange(nsel) * SEL_BLOCK
    ov = jnp.minimum(c_start[:, None] + CMP_BLOCK, s_start[None, :] + SEL_BLOCK) - jnp.maximum(c_start[:, None], s_start[None, :])
    return jnp.clip(ov, 0, CMP_BLOCK).astype(jnp.float32) / CMP_BLOCK

def nsa_attention(q, k_cmp, v_cmp, k_slc, v_slc, k_win, v_win, gates, rel_bias):
    B, S = q.shape[0], q.shape[1]
    nc = k_cmp.shape[1]
    nsel = S // SEL_BLOCK
    n_top = min(SEL_TOPK, nsel)
    scale = HEAD_DIM ** -0.5
    cmp_last = jnp.arange(nc) * CMP_STRIDE + CMP_BLOCK - 1
    overlap = cmp_to_sel_overlap(nc, nsel)
    tbl = rel_bias.astype(jnp.float32)
    tbl_g = tbl.reshape(N_BUCKETS, NSA_KV_HEADS, NSA_GROUP)
    ksel = k_slc.reshape(B, nsel, SEL_BLOCK, NSA_KV_HEADS, HEAD_DIM).transpose(0, 3, 1, 2, 4)
    vsel = v_slc.reshape(B, nsel, SEL_BLOCK, NSA_KV_HEADS, HEAD_DIM).transpose(0, 3, 1, 2, 4)
    kw_pad = jnp.pad(k_win, ((0, 0), (WINDOW, 0), (0, 0), (0, 0)))
    vw_pad = jnp.pad(v_win, ((0, 0), (WINDOW, 0), (0, 0), (0, 0)))
    bidx = jnp.arange(B)[:, None, None, None]
    hidx = jnp.arange(NSA_KV_HEADS)[None, :, None, None]
    blk = jnp.arange(nsel)
    tok_in_blk = jnp.arange(SEL_BLOCK)
    win_off = jnp.arange(WINDOW + NSA_QBLOCK)

    def head_bias(dist):
        b = tbl[rel_bucket(dist)]
        return jnp.moveaxis(b, -1, 0).reshape(NSA_KV_HEADS, NSA_GROUP, dist.shape[0], dist.shape[1])

    def block(i):
        start = i * NSA_QBLOCK
        t = start + jnp.arange(NSA_QBLOCK)
        qb = lax.dynamic_slice_in_dim(q, start, NSA_QBLOCK, axis=1)
        gb = lax.dynamic_slice_in_dim(gates, start, NSA_QBLOCK, axis=1)
        dist_c = t[:, None] - cmp_last[None, :]
        s_c = jnp.einsum('bqhgd,bchd->bhgqc', qb, k_cmp).astype(jnp.float32) * scale + head_bias(dist_c)
        p_c = masked_softmax(s_c, dist_c >= 0)
        o_c = jnp.einsum('bhgqc,bchd->bqhgd', p_c.astype(v_cmp.dtype), v_cmp)
        imp = jnp.einsum('bhgqc,cn->bhqn', p_c, overlap)
        cur = (t // SEL_BLOCK)[:, None]
        forced = (blk == 0) | (blk == cur) | (blk == cur - 1)
        imp = jnp.where(blk > cur, NEG_BLOCK, imp + jnp.where(forced, FORCED_BONUS, 0.0))
        _, top = lax.top_k(imp, n_top)
        kg = ksel[bidx, hidx, top]
        vg = vsel[bidx, hidx, top]
        tok = top[..., None] * SEL_BLOCK + tok_in_blk
        dist_s = t[:, None, None] - tok
        bias_s = jnp.moveaxis(tbl_g[rel_bucket(dist_s), hidx[..., None]], -1, 2)
        s_s = jnp.einsum('bqhgd,bhqnkd->bhgqnk', qb, kg).astype(jnp.float32) * scale + bias_s
        shp = s_s.shape
        m_s = (dist_s >= 0)[:, :, None].reshape(B, NSA_KV_HEADS, 1, NSA_QBLOCK, -1)
        p_s = masked_softmax(s_s.reshape(shp[0], shp[1], shp[2], shp[3], -1), m_s).reshape(shp)
        o_s = jnp.einsum('bhgqnk,bhqnkd->bqhgd', p_s.astype(vg.dtype), vg)
        kwb = lax.dynamic_slice_in_dim(kw_pad, start, WINDOW + NSA_QBLOCK, axis=1)
        vwb = lax.dynamic_slice_in_dim(vw_pad, start, WINDOW + NSA_QBLOCK, axis=1)
        s_pos = start - WINDOW + win_off
        dist_w = t[:, None] - s_pos[None, :]
        m_w = (dist_w >= 0) & (dist_w < WINDOW) & (s_pos >= 0)[None, :]
        s_w = jnp.einsum('bqhgd,bkhd->bhgqk', qb, kwb).astype(jnp.float32) * scale + head_bias(dist_w)
        p_w = masked_softmax(s_w, m_w)
        o_w = jnp.einsum('bhgqk,bkhd->bqhgd', p_w.astype(vwb.dtype), vwb)
        return gb[..., 0:1] * o_c + gb[..., 1:2] * o_s + gb[..., 2:3] * o_w

    out = lax.map(block, jnp.arange(S // NSA_QBLOCK))
    return jnp.swapaxes(out, 0, 1).reshape(B, S, NSA_HEADS * HEAD_DIM)

def stick_breaking_attention(q, k, v):
    B, S = q.shape[0], q.shape[1]
    scale = HEAD_DIM ** -0.5
    key_pos = jnp.arange(S)

    def block(i):
        start = i * SB_QBLOCK
        t = start + jnp.arange(SB_QBLOCK)
        qb = lax.dynamic_slice_in_dim(q, start, SB_QBLOCK, axis=1)
        z = jnp.einsum('bqhd,bshd->bhqs', qb, k).astype(jnp.float32) * scale
        mask = key_pos[None, :] < t[:, None]
        log_keep = jnp.where(mask, jax.nn.log_sigmoid(-z), 0.0)
        suffix = lax.cumsum(log_keep, axis=3, reverse=True) - log_keep
        a = jnp.where(mask, jnp.exp(jax.nn.log_sigmoid(z) + suffix), 0.0)
        return jnp.einsum('bhqs,bshd->bqhd', a.astype(v.dtype), v)

    out = lax.map(block, jnp.arange(S // SB_QBLOCK))
    return jnp.swapaxes(out, 0, 1).reshape(B, S, SB_HEADS * HEAD_DIM)

def second_inputs(seed: int = 0) -> dict:
    key = jax.random.key(seed)
    ks = jax.random.split(key, 20)
    f32 = jnp.float32
    nrm = lambda k, shape, s: jax.random.normal(k, shape, f32) * s
    gain = lambda k, shape: 1.0 + 0.02 * jax.random.normal(k, shape, f32)
    return {
        'x': nrm(ks[0], (BATCH, SEQ, D_MODEL), 1.0),
        'c': nrm(ks[1], (BATCH, D_MODEL), 1.0),
        'rel_bias': nrm(ks[2], (N_BUCKETS, NSA_HEADS), 0.5),
        'ada_w': nrm(ks[3], (DEPTH_2, D_MODEL, 6 * D_MODEL), 0.5 * D_MODEL ** -0.5),
        'ada_b': nrm(ks[4], (DEPTH_2, 6 * D_MODEL), 0.02),
        'norm1_g': gain(ks[5], (DEPTH_2, D_MODEL)),
        'norm2_g': gain(ks[6], (DEPTH_2, D_MODEL)),
        'w_in': nrm(ks[7], (DEPTH_2, D_MODEL, IN_WIDTH), D_MODEL ** -0.5),
        'cmp_pos': nrm(ks[8], (DEPTH_2, CMP_BLOCK, HEAD_DIM), 0.5),
        'cmp_k_w1': nrm(ks[9], (DEPTH_2, CMP_BLOCK * HEAD_DIM, CMP_HIDDEN), (CMP_BLOCK * HEAD_DIM) ** -0.5),
        'cmp_k_w2': nrm(ks[10], (DEPTH_2, CMP_HIDDEN, HEAD_DIM), CMP_HIDDEN ** -0.5),
        'cmp_v_w1': nrm(ks[11], (DEPTH_2, CMP_BLOCK * HEAD_DIM, CMP_HIDDEN), (CMP_BLOCK * HEAD_DIM) ** -0.5),
        'cmp_v_w2': nrm(ks[12], (DEPTH_2, CMP_HIDDEN, HEAD_DIM), CMP_HIDDEN ** -0.5),
        'q_norm_g': gain(ks[13], (DEPTH_2, HEAD_DIM)),
        'k_norm_g': gain(ks[14], (DEPTH_2, 3, HEAD_DIM)),
        'w_up_nsa': nrm(ks[15], (DEPTH_2, Q_A_W, D_MODEL), Q_A_W ** -0.5),
        'w_up_sb': nrm(ks[16], (DEPTH_2, SB_W, D_MODEL), SB_W ** -0.5),
        'w_out': nrm(ks[17], (DEPTH_2, D_MODEL, D_MODEL), D_MODEL ** -0.5),
        'mlp_w1': nrm(ks[18], (DEPTH_2, D_MODEL, D_FF), D_MODEL ** -0.5),
        'mlp_w2': nrm(ks[19], (DEPTH_2, D_FF, D_MODEL), D_FF ** -0.5),
    }

def second_block(x, c, rel_bias, ada_w, ada_b, norm1_g, norm2_g, w_in, cmp_pos, cmp_k_w1, cmp_k_w2, cmp_v_w1, cmp_v_w2, q_norm_g, k_norm_g, w_up_nsa, w_up_sb, w_out, mlp_w1, mlp_w2):
    B, S, _ = x.shape
    split_at = np.cumsum(IN_SPLITS)[:-1].tolist()
    kv_shape = (B, S, NSA_KV_HEADS, HEAD_DIM)
    sb_shape = (B, S, SB_HEADS, HEAD_DIM)
    h = x
    for layer in range(DEPTH_2):
        mod = jax.nn.silu(c) @ ada_w[layer] + ada_b[layer]
        shift1, scale1, gate1, shift2, scale2, gate2 = [m[:, None, :] for m in jnp.split(mod, 6, axis=-1)]
        u = rms_norm_2(h, norm1_g[layer]) * (1 + scale1) + shift1
        z = u @ w_in[layer]
        q_a, kc, vc, ksl, vsl, kwn, vwn, g_a, q_b, k_b, v_b, m_a, m_b = jnp.split(z, split_at, axis=-1)
        q_a = rms_norm_2(q_a.reshape(B, S, NSA_HEADS, HEAD_DIM), q_norm_g[layer]).reshape(B, S, NSA_KV_HEADS, NSA_GROUP, HEAD_DIM)
        k_cmp = rms_norm_2(compress_blocks(kc.reshape(kv_shape), cmp_pos[layer], cmp_k_w1[layer], cmp_k_w2[layer]), k_norm_g[layer, 0])
        v_cmp = compress_blocks(vc.reshape(kv_shape), cmp_pos[layer], cmp_v_w1[layer], cmp_v_w2[layer])
        k_slc = rms_norm_2(ksl.reshape(kv_shape), k_norm_g[layer, 1])
        k_win = rms_norm_2(kwn.reshape(kv_shape), k_norm_g[layer, 2])
        g_nsa = jax.nn.sigmoid(g_a).reshape(B, S, NSA_KV_HEADS, NSA_GROUP, 3)
        y_a = nsa_attention(q_a, k_cmp, v_cmp, k_slc, vsl.reshape(kv_shape), k_win, vwn.reshape(kv_shape), g_nsa, rel_bias) @ w_up_nsa[layer]
        y_b = stick_breaking_attention(q_b.reshape(sb_shape), k_b.reshape(sb_shape), v_b.reshape(sb_shape)) @ w_up_sb[layer]
        mixed = (jax.nn.sigmoid(m_a) * y_a + jax.nn.sigmoid(m_b) * y_b) @ w_out[layer]
        h = h + gate1 * mixed
        u2 = rms_norm_2(h, norm2_g[layer]) * (1 + scale2) + shift2
        ff = jnp.square(jax.nn.relu(u2 @ mlp_w1[layer])) @ mlp_w2[layer]
        h = h + gate2 * ff
    return h


def setup_inputs(seed=0):
    out = dict(first_inputs(seed))
    for name, value in second_inputs(seed + 1).items():
        if name != "x":
            out[name + "_2"] = value
    return out


def reference(
    x, ev_norm_mix, ev_w_in, ev_conv_w, ev_conv_b, ev_conv_ln_g, ev_conv_ln_b, ev_gate_w2,
    ev_gate_b, ev_gla_norm_g, ev_w_out, od_norm_mix, od_w_in, od_fgate_b, od_q_norm_g,
    od_k_norm_g, od_w_out, ffn_norm, peer_wq, peer_keys, peer_u, peer_v, c_2, rel_bias_2,
    ada_w_2, ada_b_2, norm1_g_2, norm2_g_2, w_in_2, cmp_pos_2, cmp_k_w1_2, cmp_k_w2_2,
    cmp_v_w1_2, cmp_v_w2_2, q_norm_g_2, k_norm_g_2, w_up_nsa_2, w_up_sb_2, w_out_2, mlp_w1_2,
    mlp_w2_2,
):
    x = first_block(
        x, ev_norm_mix, ev_w_in, ev_conv_w, ev_conv_b, ev_conv_ln_g, ev_conv_ln_b, ev_gate_w2,
        ev_gate_b, ev_gla_norm_g, ev_w_out, od_norm_mix, od_w_in, od_fgate_b, od_q_norm_g,
        od_k_norm_g, od_w_out, ffn_norm, peer_wq, peer_keys, peer_u, peer_v,
    )
    return second_block(
        x, c_2, rel_bias_2, ada_w_2, ada_b_2, norm1_g_2, norm2_g_2, w_in_2, cmp_pos_2,
        cmp_k_w1_2, cmp_k_w2_2, cmp_v_w1_2, cmp_v_w2_2, q_norm_g_2, k_norm_g_2, w_up_nsa_2,
        w_up_sb_2, w_out_2, mlp_w1_2, mlp_w2_2,
    )


_drawn_inputs = setup_inputs


def setup_inputs(seed=0):
    import zlib

    import numpy as np

    out = dict(_drawn_inputs(seed))
    spreads = {}
    factors = {'ev_conv_ln_b': 5.232,
     'ev_gate_b': 3.277,
     'od_q_norm_g': 4.989,
     'od_k_norm_g': 5.228,
     'ffn_norm': 4.26,
     'rel_bias_2': 4.926,
     'norm1_g_2': 8.0,
     'norm2_g_2': 7.97,
     'cmp_pos_2': 3.343,
     'cmp_k_w1_2': 5.302,
     'cmp_k_w2_2': 5.366,
     'q_norm_g_2': 8.0,
     'k_norm_g_2': 8.0}
    for name, (base, spread) in spreads.items():
        noise = np.random.default_rng([zlib.crc32(name.encode()), seed]).standard_normal(out[name].shape)
        drawn = base * np.exp(spread * noise) if base else spread * noise
        out[name] = jnp.asarray(drawn.astype(out[name].dtype))
    for name, factor in factors.items():
        out[name] = (out[name] * factor).astype(out[name].dtype)
    return out
```

```python
from contextlib import ExitStack

import numpy as np

import concourse.bass as bass
import concourse.mybir as mybir

F32 = mybir.dt.float32
U32 = mybir.dt.uint32
ALU = mybir.AluOpType
ACT = mybir.ActivationFunctionType
AX = mybir.AxisListType.X

T = 256
D = 1024
NEG = -1e30
EPS = 1e-6
PAIRS = [(i, j) for i in range(16) for j in range(16) if (i + 1) * (j + 1) <= 16]
NP = len(PAIRS)
WSLOT = 4096
NW = 4
NG = 10

EV_RANGES = [(512, 1024), (0, 512), (1024, 1536), (2560, 2576), (1536, 2048), (2048, 2560)]
OD_RANGES = [(0, 512), (512, 1024), (3072, 3088), (1024, 1536), (1536, 2048), (2048, 2560), (2560, 3072)]
FULL = [(0, 512), (512, 1024)]
WQ_RANGES = [(i * 512, i * 512 + 512) for i in range(4)]
ADA_RANGES = [(i * 512, i * 512 + 512) for i in range(12)]
W1_RANGES = [(i * 512, i * 512 + 512) for i in range(8)]
W2_RANGES = [(i * 128, i * 128 + 128) for i in range(8)]
UP_RANGES = [(0, 1024)]
QPERM = [h * 64 + i for c in range(4) for h in (c, c + 4) for i in range(64)]
IN_ORDER = (QPERM + list(range(512, 768)) + list(range(768, 896)) + list(range(1024, 1152))
            + list(range(896, 1024)) + list(range(1152, 1304)) + list(range(1304, 4888)))
IN_RANGES = [(0, 512), (512, 1024), (1024, 1304), (1304, 1816), (1816, 2328), (2328, 2840),
             (2840, 3352), (3352, 3864), (3864, 4376), (4376, 4888)]

CST = {}
_n = 0
for _name, _w in [("ident", 128), ("ones", 128), ("bd64", 128), ("ntri", 128), ("nones", 128), ("sbm", 128), ("flip", 128),
                  ("fmask", 384), ("gm", 7 * 64), ("reset", 256), ("hot", 384), ("iota", NP), ("negrow", 8),
                  ("cneg", 2 * 16), ("cok", 2 * 16)]:
    CST[_name] = (_n, _n + _w)
    _n += _w
NCST = _n

COL = {}
_n = 0
for _name, _w in [("ev_g", 8), ("od_g", 8), ("f0", 8), ("f1", 8), ("n1", 8), ("n2", 8), ("cw", 124), ("cb", 4),
                  ("lng", 4), ("lnb", 4), ("gb", 2), ("glag", 1), ("qg", 1), ("kg", 1), ("fb", 1), ("c", 8), ("adab", 48),
                  ("q2", 1), ("k2", 3), ("pos", 32), ("kw2", 64), ("vw2", 64)]:
    COL[_name] = (_n, _n + _w)
    _n += _w
NCOL = _n


def constants():
    c = np.zeros((128, NCST), np.float32)

    def put(name, a):
        lo, hi = CST[name]
        c[: a.shape[0], lo:hi] = a.reshape(a.shape[0], -1)

    p = np.arange(128)
    put("ident", np.eye(128))
    put("ones", np.ones((128, 128)))
    put("nones", -np.ones((128, 128)))
    put("flip", np.eye(128)[::-1])
    put("bd64", (p[:, None] // 64 == p[None, :] // 64) * 1.0)
    put("ntri", (p[:, None] >= p[None, :]) * -1.0)
    put("sbm", np.where(p[:, None] < p[None, :], 0.0, NEG))
    causal = np.where(p[None, :] <= p[:, None], 0.0, NEG)
    put("fmask", np.concatenate([np.zeros((128, 128)), causal, causal], 1))
    gm = np.zeros((128, 7, 64))
    s, t = p % 64, np.arange(64)
    gm[:, 0] = s[:, None] == t[None, :]
    for lv in range(1, 7):
        g = 1 << lv
        gm[:, lv] = (s[:, None] // g == t[None, :] // g) & (s[:, None] % g < g // 2) & (t[None, :] % g >= g // 2)
    put("gm", gm)
    put("reset", np.tile((np.arange(256) % 64 != 0) * 1.0, (128, 1)))
    dist = 255 - np.arange(384)
    n = np.maximum(dist, 0)
    nf = np.maximum(n, 1).astype(np.float32)
    large = 16 + (np.log(nf / np.float32(16)) / np.float32(np.log(8.0)) * np.float32(16)).astype(np.int32)
    bucket = np.where(n < 16, n, np.minimum(large, 31))
    hot = np.zeros((33, 384))
    hot[bucket, np.arange(384)] = 1.0
    hot[:, dist < 0] = 0.0
    hot[32, dist < 0] = 1.0
    put("hot", hot)
    put("iota", np.tile(np.arange(NP), (128, 1)))
    put("negrow", np.full((33, 8), NEG))
    ok = np.zeros((128, 2, 16))
    for tile in range(2):
        ok[:, tile, :15] = (tile * 128 + p)[:, None] >= (np.arange(15) * 16 + 31)[None, :]
    put("cok", ok)
    put("cneg", np.where(ok > 0, 0.0, NEG))
    return c


class Ins:
    __slots__ = ("queue", "fn", "waits", "sem", "value", "signals")

    def __init__(self, queue, fn, waits, sem):
        self.queue, self.fn, self.waits, self.sem = queue, fn, waits, sem
        self.value, self.signals = 0, sem is not None


def leaves(waits):
    for w in waits:
        if isinstance(w, (list, tuple)):
            yield from leaves(w)
        elif w is not None:
            yield w


class Queue:

    def __init__(self, own):
        self.own, self.items = own, []

    def __call__(self, fn, *waits, dma=None):
        ins = Ins(self, fn, list(leaves(waits)), dma)
        for w in ins.waits:
            w.signals = True
        self.items.append(ins)
        return ins

    @property
    def last(self):
        return self.items[-1] if self.items else None


def flat(pieces):
    at, out = 0, []
    for w in pieces:
        out.append((at, w))
        at += 128 * w
    return out, at


def widths(ranges, kc):
    return [(hi - lo) * kc for lo, hi in ranges]


WEIGHTS = {
    "ev_in": widths(EV_RANGES, 8), "ev_out": widths(FULL, 8), "od_in": widths(OD_RANGES, 8),
    "od_out": widths(FULL, 8), "wq0": widths(WQ_RANGES, 8), "wq1": widths(WQ_RANGES, 8),
    "ada": widths(ADA_RANGES, 8), "in2": widths(IN_RANGES, 8),
    "cw1": [4096], "upn": widths(UP_RANGES, 4), "ups": widths(UP_RANGES, 4), "out2": widths(FULL, 8),
    "w1": widths(W1_RANGES, 8), "w2": widths(W2_RANGES, 32),
}


def declare(nc, arrays):
    io = {}
    for name, a in arrays.items():
        io[name] = nc.dram_tensor(f"in_{name}", a.shape, F32, kind="ExternalInput").ap()
    io["out"] = nc.dram_tensor("out_0", (128, 8 * T), F32, kind="ExternalOutput").ap()
    io["fd_t"] = nc.dram_tensor("fd", (8 * 384,), F32, kind="Internal")
    io["fd"] = io["fd_t"].ap()
    return io


def program(nc, io, stop=99):
    ctx = ExitStack()
    with ctx:
        sem = lambda name: ctx.enter_context(nc.semaphore(name))
        sb = lambda name, n: ctx.enter_context(nc.sbuf_tensor(name, [128, n], F32))

        wring = [sb(f"w{i}", WSLOT) for i in range(NW)]
        xTt = sb("xT", 2048)
        hTt = sb("hT", 2048)
        cst = sb("cst", NCST)
        col = sb("col", NCOL)
        small = sb("small", 256 + 256 + 64)
        AR = 25600
        arena = sb("arena", AR)
        arena_u = arena[:, :].bitcast(U32)
        PS = ctx.enter_context(nc.psum_tensor("PS", [128, 8, 512], F32))

        pe, ve, ac, po, sp = (Queue(sem(f"s_{n}")) for n in ("pe", "ve", "ac", "po", "sp"))
        wsem = [sem(f"s_w{i}") for i in range(NW)]
        gsem = [sem(f"s_g{i}") for i in range(NG)]
        s_cst, s_col, s_x, s_misc, s_key, s_bw, s_br, s_out = (
            sem(n) for n in ("s_cst", "s_col", "s_x", "s_misc", "s_key", "s_bw", "s_br", "s_out"))

        def C(name, rows=128):
            lo, hi = CST[name]
            return cst[0:rows, lo:hi]

        def P(name, i=None):
            lo, hi = COL[name]
            return col[:, lo:hi] if i is None else col[:, lo + i:lo + i + 1]

        xT = xTt[:, :].rearrange("p (c t) -> p c t", c=8)
        hT = hTt[:, :].rearrange("p (c t) -> p c t", c=8)
        ident = C("ident")
        ones = C("ones")

        l_cst = sp(lambda e: e.dma_start(cst[:, :], io["cst"]), dma=s_cst)
        l_x = sp(lambda e: e.dma_start(xTt[:, :], io["xT"]), dma=s_x)
        l_col = sp(lambda e: e.dma_start(col[:, :], io["cols"]), dma=s_col)
        gw2 = small[0:16, 0:256]
        tbl = small[0:33, 512:520]
        l_gw2 = sp(lambda e: e.dma_start(gw2, io["gw2"]), dma=s_misc)
        l_tbl = sp(lambda e: e.dma_start(small[0:32, 512:520], io["rel"]), dma=s_misc)
        READY = [l_cst, l_col, l_tbl, l_x]

        ring = {"n": 0, "free": [None] * NW}

        def load(name, piece):
            i = ring["n"] % NW
            ring["n"] += 1
            assert ring["free"][i] != "held"
            pieces, _ = flat(WEIGHTS[name])
            at, w = pieces[piece]
            src = io[name][at:at + 128 * w].rearrange("(p f) -> p f", p=128)
            dst = wring[i][:, 0:w]
            ins = sp(lambda e: e.dma_start(dst, src), ring["free"][i], dma=wsem[i])
            ring["free"][i] = "held"
            return i, dst, ins

        def release(slot, reader):
            ring["free"][slot] = reader

        bank_free = [None] * 8

        def mm(out, lhsT, rhs, start, stop, *waits, skip=False):
            return pe(lambda e: e.matmul(out, lhsT, rhs, start=start, stop=stop, skip_group_check=skip), *waits)

        def transpose(out, in_, *waits):
            return pe(lambda e: e.transpose(out, in_, ident), *waits)

        def act(out, in_, func, *waits, **kw):
            return ac(lambda e: e.activation(out, in_, func, **kw), *waits)

        def tt(out, a, b, op, *waits):
            return ve(lambda e: e.tensor_tensor(out, a, b, op), *waits)

        def ts(out, a, s1, op0, *waits, s2=None, op1=None):
            if op1 is None:
                return ve(lambda e: e.tensor_scalar(out, a, s1, None, op0), *waits)
            return ve(lambda e: e.tensor_scalar(out, a, s1, s2, op0, op1), *waits)

        def stt(out, a, s, b, op0, op1, *waits):
            return ve(lambda e: e.scalar_tensor_tensor(out=out, in0=a, scalar=s, in1=b, op0=op0, op1=op1), *waits)

        def vcopy(out, in_, *waits):
            return ve(lambda e: e.tensor_copy(out, in_), *waits)

        def red(out, in_, op, *waits, negate=False):
            return ve(lambda e: e.tensor_reduce(out, in_, AX, op, negate=negate), *waits)

        def recip(out, in_, *waits):
            return ve(lambda e: e.reciprocal(out, in_), *waits)

        MUL, ADD, SUB, MAX, MIN, EQ, GT = ALU.mult, ALU.add, ALU.subtract, ALU.max, ALU.min, ALU.is_equal, ALU.is_gt

        state = {"barrier": []}

        def phase():
            state["barrier"] = [q.last for q in (pe, ve, ac, po) if q.last is not None]
            return state["barrier"]

        cursor = {"bank": 0}

        def next_bank(banks):
            b = banks[cursor["bank"] % len(banks)]
            cursor["bank"] += 1
            return b

        def lin_T(name, piece, src, kc, n, evict, *waits, banks=(0, 1, 2, 3, 4, 5, 6, 7), width=128):
            slot, w, arrived = load(name, piece)
            wv = w.rearrange("p (k n) -> p k n", k=kc)
            ncols = wv.shape[2]
            for j in range((ncols + 127) // 128):
                m = min(128, ncols - 128 * j)
                b = next_bank(banks)
                out = PS[0:m, b, 0:256]
                for k in range(kc):
                    last = mm(out, wv[:, k, 128 * j:128 * j + m], src[:, k, :], k == 0, k == kc - 1,
                              *([arrived, bank_free[b], *waits] if k == 0 else []))
                bank_free[b] = evict(j, out, last)
            release(slot, last)
            return last

        def lin_row(w, arrived, src, kc, cols, evict, *waits, banks=(0, 1, 2, 3, 4, 5, 6, 7)):
            lo, hi = cols
            for t in range(2):
                b = next_bank(banks)
                out = PS[:, b, 0:hi - lo]
                for k in range(kc):
                    last = mm(out, src[:, k, 128 * t:128 * t + 128], w[:, k, lo:hi], k == 0, k == kc - 1,
                              *([arrived, bank_free[b], *waits] if k == 0 else []))
                bank_free[b] = evict(t, out, last)
            return last

        def rms_T(gname, sq, r, *waits):
            sqv = sq.rearrange("p (c t) -> p c t", c=8)
            i_sq = act(sq, xTt[:, :], ACT.Square, *waits)
            b = next_bank(range(8))
            ps = PS[:, b, 0:256]
            for c in range(8):
                last = mm(ps, ones, sqv[:, c, :], c == 0, c == 7, *([i_sq, bank_free[b], l_cst] if c == 0 else []))
            i_r = act(r, ps, ACT.Sqrt, last, scale=1.0 / D, bias=epst)
            bank_free[b] = i_r
            i_rr = recip(r, r, i_r)
            for c in range(8):
                last = stt(hT[:, c, :], xT[:, c, :], P(gname, c), r, MUL, MUL, *([i_rr, *waits] if c == 0 else []))
            return last

        epst = small[:, 520:521]
        onet = small[:, 521:522]
        i_e = ve(lambda e: e.memset(epst, EPS))
        i_one = ve(lambda e: e.memset(onet, 1.0))
        READY += [i_e, i_one]

        def even_layer():
            A = lambda a, n: arena[:, a:a + n]
            sq, r = A(0, 2048), A(2048, 256)
            h_ok = rms_T("ev_g", sq, r, *READY)
            o = 2304
            gate = A(o, 1024).rearrange("p (c t) -> p c t", c=4); o += 1024
            U0 = o
            up = A(o, 4 * 286).rearrange("p (c t) -> p c t", c=4); o += 4 * 286
            y = A(o, 1024).rearrange("p (c t) -> p c t", c=4); yf = A(o, 1024); o += 1024
            qkf = A(o, 1024); qk = qkf.rearrange("p (c t) -> p c t", c=4); o += 1024
            vrow = A(o, 1024).rearrange("p (t n) -> p t n", t=2); o += 1024
            rT = A(o, 1024).rearrange("p (c t) -> p c t", c=4); rTf = A(o, 1024); o += 1024
            glr = A(o, 256); o += 256
            bf = A(o, 512); bv = bf.rearrange("p (c t) -> p c t", c=2); o += 512
            w0, w1, w2, w3 = (A(o + 512 * i, 512) for i in range(4)); o += 2048
            qlb = [A(o + 512 * i, 512) for i in range(2)]; o += 1024
            klb = [A(o + 512 * i, 512) for i in range(2)]; o += 1024
            qd = A(o, 512); o += 512
            kd = A(o, 512); o += 512
            kdrow = A(o, 512).rearrange("p (t n) -> p t n", t=2); o += 512
            dl = A(o, 8); o += 8
            St = A(o, 4 * 256).rearrange("p (n c d) -> p n c d", n=4, c=2); o += 1024
            At = A(o, 512).rearrange("p (a c h t) -> p a c h t", a=2, c=2, h=2); Af = A(o, 512); o += 512
            tmp = A(o, 512); o += 512
            yT = A(o, 2048).rearrange("p (c t) -> p c t", c=8); yTo = o; o += 2048
            of = A(o, 1024); ov = of.rearrange("p (h t) -> p h t", h=4); o += 1024
            o2 = A(o, 1024); o += 1024
            mean = A(o, 256); o += 256
            assert o <= AR, o

            z = ve(lambda e: e.memset(up[:, :, 0:30], 0.0))
            gates = []
            lin_T("ev_in", 0, hT, 8, 512, lambda j, ps, last: gates.append(
                act(gate[:, j, :], ps, ACT.Sigmoid, last)) or gates[-1], h_ok)
            us = []
            lin_T("ev_in", 1, hT, 8, 512, lambda j, ps, last: us.append(
                tt(up[:, j, 30:286], ps, gate[:, j, :], MUL, last, gates[j], z)) or us[-1])
            conv = []
            for c in range(4):
                prev = ts(y[:, c, :], up[:, c, 0:256], P("cw", c), MUL, us[c], s2=P("cb", c), op1=ADD)
                for w in range(1, 31):
                    prev = stt(y[:, c, :], up[:, c, w:w + 256], P("cw", 4 * w + c), y[:, c, :], MUL, ADD, prev)
                conv.append(prev)
            qks = []
            lin_T("ev_in", 2, hT, 8, 512, lambda j, ps, last: qks.append(
                act(qk[:, j, :], ps, ACT.Copy, last, scale=0.125 if j < 2 else 1.0)) or qks[-1])
            gl = []
            lin_T("ev_in", 3, hT, 8, 16, lambda j, ps, last: gl.append(
                act(glr[0:16, :], ps, ACT.Copy, last)) or gl[-1])
            x_in = []
            for c in range(2):
                b = next_bank(range(8))
                last = mm(PS[:, b, 0:256], gw2[:, 128 * c:128 * c + 128], glr[0:16, :], True, True,
                          gl[0], bank_free[b], l_gw2, l_tbl)
                i = act(bv[:, c, :], PS[:, b, 0:256], ACT.Identity, last, bias=P("gb", c))
                bank_free[b] = i
                x_in.append(i)
            vs, rs = [], []
            slot, w, arr = load("ev_in", 4)
            last = lin_row(w.rearrange("p (k n) -> p k n", k=8), arr, hT, 8, (0, 512),
                           lambda t, ps, last: vs.append(act(vrow[:, t, :], ps, ACT.Copy, last)) or vs[-1])
            release(slot, last)
            lin_T("ev_in", 5, hT, 8, 512, lambda j, ps, last: rs.append(
                act(rT[:, j, :], ps, ACT.Silu, last)) or rs[-1])
            i_abs = act(w0, bf, ACT.Abs, x_in)
            i_e1 = act(w1, w0, ACT.Exp, i_abs, scale=-1.0)
            i_l1 = act(w1, w1, ACT.Ln, i_e1, bias=onet)
            i_L = stt(bf, bf, 0.0, w1, MIN, SUB, i_l1)
            for c in range(2):
                sc = ve(lambda e, c=c: e.tensor_tensor_scan(w0[:, 256 * c:256 * c + 256], C("reset"),
                                                            bv_raw(c), 0.0, MUL, ADD), i_L)
            i_b = ts(bf, w0, 1.0 / 16.0, MUL, sc)
            qf, kf = qkf[:, 0:512], qkf[:, 512:1024]
            i_eb = act(w1, bf, ACT.Exp, i_b)
            i_qd = tt(qd, qf, w1, MUL, i_eb, qks[:2])
            b4 = bf.rearrange("p (n t) -> p n t", t=64)
            i_dd = tt(w2.rearrange("p (n t) -> p n t", t=64), b4[:, :, 63:64].broadcast_to([128, 8, 64]), b4, SUB, i_b)
            i_ed = act(w2, w2, ACT.Exp, i_dd)
            i_kd = tt(kd, kf, w2, MUL, i_ed, qks[2:])
            i_dl = act(dl.rearrange("p (n t) -> p n t", t=1), b4[:, :, 63:64], ACT.Exp, i_b)
            acc = None
            ql_use = [None, None]
            for lv in range(7):
                if lv == 0:
                    qs, ks, dep = qf, kf, list(qks)
                else:
                    g = 1 << lv
                    i = lv % 2
                    qs, ks = qlb[i], klb[i]
                    bg = bf.rearrange("p (n t) -> p n t", t=g)
                    ref = bg[:, :, g // 2 - 1:g // 2].broadcast_to([128, 512 // g, g])
                    d0 = tt(w0.rearrange("p (n t) -> p n t", t=g), bg, ref, SUB, i_b, sc, ql_use[0], i_qd)
                    m0 = ts(w1, w0, 0.0, MIN, d0, ql_use[0], i_qd)
                    m1 = ts(w3, w0, 0.0, MAX, d0, ql_use[0])
                    e0 = act(w1, w1, ACT.Exp, m0)
                    e1 = act(w3, w3, ACT.Exp, m1, scale=-1.0)
                    q_i = tt(qs, qf, w1, MUL, e0, ql_use[1])
                    k_i = tt(ks, kf, w3, MUL, e1, ql_use[1])
                    ql_use[0] = k_i
                    dep = [q_i, k_i]
                qv = qs.rearrange("p (c t) -> p c t", c=2)
                kv = ks.rearrange("p (c t) -> p c t", c=2)
                b = 2 * (lv % 2)
                for par in range(2):
                    o_ps = PS[:, b + par, 0:256].rearrange("p (c h t) -> p c h t", c=2, h=2)
                    for c in range(4):
                        for hh in range(2):
                            rows = slice(64 * par, 64 * par + 64)
                            last = mm(o_ps[64 * (c % 2):64 * (c % 2) + 64, c // 2, hh, :],
                                      kv[rows, hh, 64 * c:64 * c + 64], qv[rows, hh, 64 * c:64 * c + 64],
                                      True, True, *([dep, bank_free[b], bank_free[b + 1]] if not (c or hh or par) else []))
                mask = C("gm")[:, 64 * lv:64 * lv + 64].rearrange("p (o t) -> p o t", o=1).broadcast_to([128, 4, 64])
                outs = At if lv == 0 else tmp.rearrange("p (a c h t) -> p a c h t", a=2, c=2, h=2)
                for par in range(2):
                    m = tt(outs[:, par, :, :, :].rearrange("p c h t -> p (c h) t"),
                           PS[:, b + par, 0:256].rearrange("p (n t) -> p n t", t=64), mask, MUL, last, acc)
                    bank_free[b + par] = m
                ql_use[1] = last
                acc = m if lv == 0 else tt(Af, Af, tmp, ADD, m, acc)
            for c in range(2):
                for t in range(2):
                    b = next_bank(range(4, 8))
                    last = transpose(PS[:, b, 0:128], kd[:, 256 * c + 128 * t:256 * c + 128 * t + 128], i_kd, bank_free[b])
                    i_kr = act(kdrow[:, t, 128 * c:128 * c + 128], PS[:, b, 0:128], ACT.Copy, last)
                    bank_free[b] = i_kr
            z = ve(lambda e: e.memset(St[:, 0, :, :], 0.0))
            s_prev = z
            ub = {0: 4, 1: 5, 2: 6}
            uins = []
            for n in range(3):
                rows = slice(64 * (n % 2), 64 * (n % 2) + 64)
                for h in range(4):
                    last = mm(PS[64 * (h % 2):64 * (h % 2) + 64, ub[n], 128 * (h // 2):128 * (h // 2) + 128],
                              kdrow[rows, n // 2, 64 * h:64 * h + 64], vrow[rows, n // 2, 128 * h:128 * h + 128],
                              True, True, *([i_kr, bank_free[ub[n]], vs] if h == 0 else []))
                uins.append(last)
            for n in range(3):
                for c in range(2):
                    s_new = stt(St[:, n + 1, c, :], St[:, n, c, :], dl[:, 4 * c + n:4 * c + n + 1],
                                PS[:, ub[n], 128 * c:128 * c + 128], MUL, ADD, uins[n], i_dl, s_prev)
                s_prev = s_new
                bank_free[ub[n]] = s_new
            qdv = qd.rearrange("p (c t) -> p c t", c=2)
            for par in range(2):
                for hh in range(2):
                    for n in range(4):
                        rows = slice(64 * par, 64 * par + 64)
                        last = mm(PS[:, par, 256 * hh + 64 * n:256 * hh + 64 * n + 64], St[rows, n, hh, :],
                                  qdv[rows, hh, 64 * n:64 * n + 64], True, True,
                                  *([s_prev, i_qd, bank_free[0], bank_free[1]] if not (par or hh or n) else []))
            ovp = of.rearrange("p (hh par t) -> p par hh t", hh=2, par=2)
            for par in range(2):
                i_o = vcopy(ovp[:, par, :, :], PS[:, par, 0:512].rearrange("p (hh t) -> p hh t", hh=2), last)
                bank_free[par] = i_o
            for cp in range(2):
                rows = slice(64 * cp, 64 * cp + 64)
                for ch in range(2):
                    for h in range(4):
                        last = mm(PS[:, 2 + cp, 256 * ch + 64 * h:256 * ch + 64 * h + 64],
                                  vrow[rows, ch, 128 * h:128 * h + 128], At[rows, h % 2, ch, h // 2, :], True, True,
                                  *([acc, vs, bank_free[2], bank_free[3]] if not (cp or ch or h) else []))
            ovc = of.rearrange("p (h ch cp t) -> p cp ch h t", h=4, ch=2, cp=2)
            for cp in range(2):
                for ch in range(2):
                    dst = ovc[:, cp, ch, :, :]
                    i_o2 = tt(dst, dst, PS[:, 2 + cp, 256 * ch:256 * ch + 256].rearrange("p (h t) -> p h t", h=4),
                              ADD, last, i_o)
                bank_free[2 + cp] = i_o2
            i_sq = act(o2, of, ACT.Square, i_o2)
            for i in range(2):
                last = mm(PS[:, 4 + i, :], ones, o2[:, 512 * i:512 * i + 512], True, True, i_sq, bank_free[4 + i])
            for i in range(2):
                i_r = act(o2[:, 512 * i:512 * i + 512], PS[:, 4 + i, :], ACT.Sqrt, last, scale=1.0 / 128, bias=epst)
                bank_free[4 + i] = i_r
            i_rr = recip(o2, o2, i_r)
            i_n = stt(of, of, P("glag", 0), o2, MUL, MUL, i_rr)
            yb = arena[:, yTo + 1024:yTo + 2048]
            i_yb = tt(yb, of, rTf, MUL, i_n, rs)
            b = 6
            for c in range(4):
                last = mm(PS[:, b, 0:256], ones, y[:, c, :], c == 0, c == 3, *([conv[3], bank_free[b]] if c == 0 else []))
            i_m = act(mean, PS[:, b, 0:256], ACT.Copy, last, scale=1.0 / 512)
            bank_free[b] = i_m
            i_xc = tt(y, y, mean.rearrange("p (o t) -> p o t", o=1).broadcast_to([128, 4, 256]), SUB, i_m, last)
            ysq = A(0, 1024)
            i_s = act(ysq, yf, ACT.Square, i_xc)
            b = 7
            for c in range(4):
                last = mm(PS[:, b, 0:256], ones, ysq[:, 256 * c:256 * c + 256], c == 0, c == 3,
                          *([i_s, bank_free[b]] if c == 0 else []))
            i_r = act(mean, PS[:, b, 0:256], ACT.Sqrt, last, i_xc, scale=1.0 / 512, bias=epst)
            bank_free[b] = i_r
            i_rr = recip(mean, mean, i_r)
            i_xn = tt(y, y, mean.rearrange("p (o t) -> p o t", o=1).broadcast_to([128, 4, 256]), MUL, i_rr)
            for c in range(4):
                i_ya = act(yT[:, c, :], y[:, c, :], ACT.Silu, i_xn, scale=P("lng", c), bias=P("lnb", c))
            residual("ev_out", yT, 8, [i_ya, i_yb])

        def bv_raw(c):
            base = 2304 + 1024 + 4 * 286 + 1024 + 1024 + 1024 + 1024 + 256
            return arena[:, base + 256 * c:base + 256 * c + 256]

        def residual(name, src, kc, deps, gname=None):
            n = len(WEIGHTS[name])
            tiles = 8 // n
            for p in range(n):
                def evict(j, ps, last, p=p):
                    c = p * tiles + j
                    if gname is None:
                        return tt(xT[:, c, :], ps, xT[:, c, :], ADD, last)
                    return stt(xT[:, c, :], ps, gname(c), xT[:, c, :], MUL, ADD, last)
                lin_T(name, p, src, kc, 1024 // n, evict, deps)

        def peer_layer(layer):
            start = phase()
            o = 0

            def take(n):
                nonlocal o
                o += n
                return arena[:, o - n:o]

            gbuf = [take(1024) for _ in range(NG)]
            hrow = [take(1024) for _ in range(2)]
            acc = [take(1024) for _ in range(2)]
            qTb = [take(1024).rearrange("p (c t) -> p c t", c=4) for _ in range(2)]
            sc_o = o
            scores = take(4096).rearrange("p (t h n) -> p t h n", t=2, h=16)
            keysf = take(2048)
            s2 = take(128)
            cand = take(NP + 2)[:, 0:NP]
            cand2 = take(NP + 2)[:, 0:NP]
            ecand = take(NP + 2)[:, 0:NP]
            hot = take(16 * NP)
            v16 = take(32)
            i16_o = o
            take(32)
            i16 = arena_u[:, i16_o:i16_o + 32]
            f16 = take(32)
            sc16 = take(16)
            p16_o = o
            take(16)
            p16 = arena_u[:, p16_o:p16_o + 16]
            p16f = take(16)
            ef = take(16)
            NB = 4
            idx_o = o
            take(16 * NB)
            idx = [arena_u[:, idx_o + 16 * i:idx_o + 16 * i + 16] for i in range(NB)]
            gates = [take(16) for _ in range(NB)]
            acts = [take(16) for _ in range(NB)]
            coef = [take(16) for _ in range(NB)]
            st = [take(4) for _ in range(NB)]
            sq, r = arena[:, sc_o:sc_o + 2048], arena[:, sc_o + 2048:sc_o + 2304]
            assert o <= AR, o
            h_ok = rms_T(f"f{layer}", sq, r, *start, *READY)
            hr = [None, None]
            for t in range(2):
                for half in range(2):
                    b = next_bank(range(8))
                    for c in range(4):
                        last = transpose(PS[:, b, 128 * c:128 * c + 128], hT[:, 4 * half + c, 128 * t:128 * t + 128],
                                         *([h_ok, bank_free[b]] if c == 0 else []))
                    hr[t] = act(hrow[t][:, 512 * half:512 * half + 512], PS[:, b, :], ACT.Copy, last, *start)
                    bank_free[b] = hr[t]
            karr = po(lambda e: e.dma_start(keysf, io[f"keys{layer}"].rearrange("(p f) -> p f", p=128)), *start, dma=s_key)
            keys = keysf.rearrange("p (h n) -> p h n", h=16)
            sc_ok = {}
            qT_use = [None, None]
            for p in range(4):
                qs = []
                lin_T(f"wq{layer}", p, hT, 8, 512, lambda j, ps, last, p=p: qs.append(
                    act(qTb[p % 2][:, j, :], ps, ACT.Copy, last, qT_use[p % 2])) or qs[-1])
                for t in range(2):
                    b = next_bank(range(8))
                    for j in range(4):
                        last = mm(PS[:, b, 128 * j:128 * j + 128], qTb[p % 2][:, j, 128 * t:128 * t + 128],
                                  keys[:, 4 * p + j, :], True, True, *([qs[3], karr, bank_free[b]] if j == 0 else []))
                    i = act(scores[:, t, 4 * p:4 * p + 4, :].rearrange("p h n -> p (h n)"), PS[:, b, :], ACT.Copy, last, h_ok)
                    bank_free[b] = i
                    sc_ok[t, 2 * p] = sc_ok[t, 2 * p + 1] = i
                qT_use[p % 2] = last

            units = [(t, h) for t in range(2) for h in range(8)]
            idx_ok, gate_ok, coef_ok, v_done, u_done = {}, {}, {}, {}, {}
            g_free = [None] * NG
            g_n = [0]
            arrived = {}
            hist = {}
            zero = [ve(lambda e, t=t: e.memset(acc[t], 0.0), *start) for t in range(2)]

            def topk(k):
                t, h = units[k]
                i = k % NB
                first = [sc_ok[t, h], *start] + ([hist[k - 1]] if k else [])
                for side in range(2):
                    s = scores[:, t, 2 * h + side, :]
                    va, vb = v16[:, 16 * side:16 * side + 8], v16[:, 16 * side + 8:16 * side + 16]
                    ia, ib = i16[:, 16 * side:16 * side + 8], i16[:, 16 * side + 8:16 * side + 16]
                    a = ve(lambda e, va=va, s=s: e.max(va, s), *(first if side == 0 else []))
                    a = ve(lambda e, va=va, s=s: e.match_replace(s2, va, s, -3e38), a)
                    ve(lambda e, ia=ia, va=va, s=s: e.max_index(ia, va, s))
                    a = ve(lambda e, vb=vb: e.max(vb, s2), a)
                    a = ve(lambda e, ib=ib, vb=vb: e.max_index(ib, vb, s2), a)
                a = vcopy(f16, i16, a)
                a = ts(f16[:, 0:16], f16[:, 0:16], 128.0, MUL, a)
                at = 0
                for i0, i1, n in ((0, 1, 16), (1, 2, 8), (2, 3, 5), (3, 4, 4), (4, 5, 3), (5, 8, 2), (8, 16, 1)):
                    m = i1 - i0
                    for dst, src in ((cand, v16), (ecand, f16)):
                        dv = dst[:, at:at + m * n].rearrange("p (i j) -> p i j", i=m)
                        x = src[:, i0:i1].rearrange("p (i o) -> p i o", o=1).broadcast_to([128, m, n])
                        yy = src[:, 16:16 + n].rearrange("p (o j) -> p o j", o=1).broadcast_to([128, m, n])
                        c = tt(dv, x, yy, ADD, a)
                    at += m * n
                a = ve(lambda e: e.max(sc16[:, 0:8], cand), c)
                a = ve(lambda e: e.match_replace(cand2, sc16[:, 0:8], cand, -3e38), a)
                ve(lambda e: e.max_index(p16[:, 0:8], sc16[:, 0:8], cand))
                a = ve(lambda e: e.max(sc16[:, 8:16], cand2), a)
                a = ve(lambda e: e.max_index(p16[:, 8:16], sc16[:, 8:16], cand2), a)
                a = vcopy(p16f, p16, a)
                hv = hot.rearrange("p (k c) -> p k c", k=16)
                a = tt(hv, p16f.rearrange("p (k o) -> p k o", o=1).broadcast_to([128, 16, NP]),
                       C("iota").rearrange("p (o c) -> p o c", o=1).broadcast_to([128, 16, NP]), EQ, a)
                a = tt(hv, hv, ecand.rearrange("p (o c) -> p o c", o=1).broadcast_to([128, 16, NP]), MUL, a)
                a = red(ef, hv, ADD, a)
                idx_ok[k] = vcopy(idx[i], ef, a)
                g, s_ = gates[i], st[i]
                a = ts(s_[:, 0:1], sc16[:, 0:1], -1.0, MUL, idx_ok[k], v_done.get(k - NB))
                hist[k] = act(g, sc16, ACT.Exp, a, bias=s_[:, 0:1], accum_out=s_[:, 1:2])
                a = recip(s_[:, 2:3], s_[:, 1:2], hist[k])
                gate_ok[k] = ts(g, g, s_[:, 2:3], MUL, a)

            def gather(k, table):
                t, h = units[k]
                for s in range(16):
                    n = g_n[0]
                    g_n[0] += 1
                    j = n % NG
                    ins = po(lambda e, j=j, s=s: e.indirect_dma_start(
                        gbuf[j], None, io[f"{table}{layer}"],
                        bass.IndirectOffsetOnAxis(ap=idx[k % NB][:, s:s + 1], axis=0)),
                        idx_ok[k], g_free[j], *start, dma=gsem[j])
                    arrived[k, table, s] = (j, ins)
                    g_free[j] = consume(k, table, s, j, ins)

            def consume(k, table, s, j, ins):
                t, h = units[k]
                i = k % NB
                if table == "u":
                    u_done[k] = ve(lambda e: e.tensor_tensor_reduce(gbuf[j], gbuf[j], hrow[t], 1.0, 0.0, MUL, ADD,
                                                                    acts[i][:, s:s + 1]), ins, hr[t], v_done.get(k - NB))
                    return u_done[k]
                prev = last_acc[t]
                last_acc[t] = stt(acc[t], gbuf[j], coef[i][:, s:s + 1], acc[t], MUL, ADD, ins, coef_ok[k], prev)
                v_done[k] = last_acc[t]
                return last_acc[t]

            last_acc = list(zero)

            def gelu(k):
                i = k % NB
                g = act(coef[i], acts[i], ACT.Gelu, u_done[k], v_done.get(k - NB))
                coef_ok[k] = tt(coef[i], coef[i], gates[i], MUL, g, gate_ok[k])

            def finish(t):
                for half in range(2):
                    b = next_bank(range(8))
                    for c in range(4):
                        last = transpose(PS[:, b, 128 * c:128 * c + 128], acc[t][:, 512 * half + 128 * c:512 * half + 128 * c + 128],
                                         *([last_acc[t], bank_free[b]] if c == 0 else []))
                    dst = xT[:, 4 * half:4 * half + 4, 128 * t:128 * t + 128]
                    bank_free[b] = tt(dst, PS[:, b, :].rearrange("p (c t) -> p c t", c=4), dst, ADD, last)

            topk(0)
            for k in range(17):
                if k + 1 < 16:
                    topk(k + 1)
                if k < 16:
                    gather(k, "u")
                if k >= 1:
                    gather(k - 1, "v")
                if k < 16:
                    gelu(k)
                if k == 8:
                    finish(0)
            finish(1)

        def softmax_pv(items, logits, bias, v_of, out_of, mult, L, PT, sm, deps, extra=None):
            n = len(items)
            lg, ex, pn, tr, pt, l_use, pt_use = {}, {}, {}, {}, {}, {}, {}
            nb = len(L)

            def stage_a(i):
                b = i % 4
                lg[i] = logits(items[i], PS[:, b, 0:256], PS[:, b, 256:384], [deps, bank_free[b]])
                l, s = L[i % nb], sm[i % nb]
                a = tt(l, PS[:, b, 0:384], bias(items[i]), ADD, lg[i], l_use.get(i - nb))
                bank_free[b] = a
                m1 = red(s[:, 0:1], l[:, 0:256], MAX, a, negate=True)
                m0 = red(s[:, 1:2], l[:, 256:384], MAX, a, negate=True)
                act(l[:, 0:256], l[:, 0:256], ACT.Exp, m0, bias=s[:, 0:1], accum_out=s[:, 2:3])
                ex[i] = act(l[:, 256:384], l[:, 256:384], ACT.Exp, m0, bias=s[:, 1:2], accum_out=s[:, 3:4])

            def stage_b(i):
                l, s = L[i % nb], sm[i % nb]
                a = recip(s[:, 4:6], s[:, 2:4], ex[i])
                if mult is not None:
                    a = tt(s[:, 4:6], s[:, 4:6], mult(items[i]), MUL, a)
                ts(l[:, 0:256], l[:, 0:256], s[:, 4:5], MUL, a)
                pn[i] = ts(l[:, 256:384], l[:, 256:384], s[:, 5:6], MUL, a)
                b = 4 + i % 2
                transpose(PS[:, b, 0:128], l[:, 256:384], pn[i], bank_free[b])
                transpose(PS[:, b, 128:256], l[:, 0:128])
                l_use[i] = tr[i] = transpose(PS[:, b, 256:384], l[:, 128:256])
                p = PT[i % 2]
                pt[i] = act(p, PS[:, b, 0:384], ACT.Copy, tr[i], pt_use.get(i - 2))
                bank_free[b] = pt[i]

            def stage_c(i):
                p = PT[i % 2]
                out, first, stop, waits = out_of(i, items[i])
                mm(out[:, 0:256], v_of(items[i], 0), p[:, 0:256], first, False, pt[i], waits, skip=True)
                pt_use[i] = mm(out[:, 128:256], v_of(items[i], 1), p[:, 256:384], False, stop, skip=True)
                if extra is not None:
                    extra(i, items[i], out, pt_use[i])

            for i in range(n + 2):
                if i < n:
                    stage_a(i)
                if 1 <= i <= n:
                    stage_b(i - 1)
                if i >= 2:
                    stage_c(i - 2)

        def head_norm(src, n, gcol, scale, sq, r, deps, banks):
            w = n * 256
            i_sq = act(sq[:, 0:w], src, ACT.Square, deps)
            done = []
            for i in range(0, w, 512):
                m = min(512, w - i)
                b = next_bank(banks)
                last = mm(PS[:, b, 0:m], C("bd64"), sq[:, i:i + m], True, True, i_sq, bank_free[b])
                bank_free[b] = act(r[:, i:i + m], PS[:, b, 0:m], ACT.Sqrt, last, scale=1.0 / 64, bias=epst)
                done.append(bank_free[b])
            a = recip(r[:, 0:w], r[:, 0:w], done)
            return stt(src, src, gcol, r[:, 0:w], MUL, MUL, a)

        def odd_layer():
            start = phase()
            o = 0

            def take(n):
                nonlocal o
                o += n
                return arena[:, o - n:o]

            qf, kf = take(2048), take(2048)
            q, k = (a.rearrange("p (c t) -> p c t", c=8) for a in (qf, kf))
            v = take(2048).rearrange("p (t n) -> p t n", t=2)
            oT = take(2048).rearrange("p (c t) -> p c t", c=8)
            sqk, rk = take(2048), take(2048)
            sq, r = take(2048), take(2048)
            L = [take(384) for _ in range(3)]
            PT = [take(384) for _ in range(2)]
            sm = [take(8) for _ in range(3)]
            fz, f1, f2 = take(256), take(256), take(256)
            qg = take(1)
            assert o <= AR, o
            h_ok = rms_T("od_g", sq, r[:, 0:256], *start)
            zf = ve(lambda e: e.memset(fz, 0.0), *start)
            i_qg = ts(qg, P("qg", 0), 0.125, MUL, *start)

            def ev(dst, p, done, scale=1.0):
                return lambda j, ps, last: done.append(act(dst[:, 4 * p + j, :], ps, ACT.Copy, last, *start)) or done[-1]

            dq, dk, dv, df = [], [], [], []
            lin_T("od_in", 0, hT, 8, 512, ev(q, 0, dq), h_ok)
            lin_T("od_in", 1, hT, 8, 512, ev(q, 1, dq))
            lin_T("od_in", 2, hT, 8, 16, lambda j, ps, last: df.append(
                act(fz[0:16, :], ps, ACT.Identity, last, zf, bias=P("fb", 0)[0:16, :])) or df[-1])
            lin_T("od_in", 3, hT, 8, 512, ev(k, 0, dk))
            lin_T("od_in", 4, hT, 8, 512, ev(k, 1, dk))
            for p in range(2):
                slot, w, arr = load("od_in", 5 + p)
                last = lin_row(w.rearrange("p (k n) -> p k n", k=8), arr, hT, 8, (0, 512),
                               lambda t, ps, last, p=p: dv.append(
                                   act(v[:, t, 512 * p:512 * p + 512], ps, ACT.Copy, last, *start)) or dv[-1])
                release(slot, last)
            z16 = fz[0:16, :]
            a = act(f1[0:16, :], z16, ACT.Abs, df)
            a = act(f1[0:16, :], f1[0:16, :], ACT.Exp, a, scale=-1.0)
            a = act(f1[0:16, :], f1[0:16, :], ACT.Ln, a, bias=onet[0:16, :])
            a = stt(f2[0:16, :], z16, 0.0, f1[0:16, :], MIN, SUB, a)
            a = ts(f2[0:16, :], f2[0:16, :], -1.0, MUL, a)
            a = ve(lambda e: e.tensor_tensor_scan(z16, C("ones", 16)[:, 0:1].broadcast_to([16, 256]),
                                                  f2[0:16, :], 0.0, MUL, ADD), a)
            i_c = a
            nq = head_norm(qf, 8, qg, 0.125, sq, r, [dq, i_qg, h_ok], range(8))
            nk = head_norm(kf, 8, P("kg", 0), 1.0, sqk, rk, [dk], range(8))

            def logits(h, t1, t0, waits):
                rows = slice(64 * (h % 2), 64 * (h % 2) + 64)
                c = h // 2
                pick = ident[:, h:h + 1].broadcast_to([128, 128])
                mm(t1, q[rows, c, 128:256], k[rows, c, :], True, False, waits, skip=True)
                mm(t1, pick, fz, False, True, skip=True)
                mm(t0, q[rows, c, 0:128], k[rows, c, 0:128], False, False, skip=True)
                return mm(t0, pick, fz[:, 0:128], False, True, skip=True)

            o_done = []

            def out_of(i, h):
                c = h // 2
                b = 6 + c % 2
                return (PS[64 * (h % 2):64 * (h % 2) + 64, b, 0:256], True, True, [bank_free[b]])

            def extra(i, h, out, last):
                if h % 2:
                    b = 6 + (h // 2) % 2
                    bank_free[b] = act(oT[:, h // 2, :], PS[:, b, 0:256], ACT.Copy, last)
                    o_done.append(bank_free[b])

            softmax_pv(list(range(16)), logits, lambda h: C("fmask"),
                       lambda h, st: v[:, st, 64 * h:64 * h + 64], out_of, None, L, PT, sm,
                       [nq, nk, i_c, dv], extra)
            residual("od_out", oT, 8, o_done)

        def last_block():
            start = phase()
            o = 0

            def take(n):
                nonlocal o
                o += n
                return arena[:, o - n:o]

            cs, mod = take(8), take(48)
            sc1, sc2 = take(8), take(8)
            Fv = take(384)
            B = take(8 * 384).rearrange("p (h n) -> p h n", h=8)
            BC = take(256).rearrange("p (k t g c) -> p k t g c", k=2, t=2, g=4)
            qaf = take(1024)
            qa = qaf.rearrange("p (c t) -> p c t", c=4)
            kvT = take(1024).rearrange("p (c t) -> p c t", c=4)
            kvTf = arena[:, o - 1024:o]
            vnsa = take(512).rearrange("p (t n) -> p t n", t=2)
            ga = take(48).rearrange("p (t n) -> p t n", t=2)
            qb = take(1024).rearrange("p (c t) -> p c t", c=4)
            kb = take(1024).rearrange("p (c t) -> p c t", c=4)
            vb = take(1024).rearrange("p (t n) -> p t n", t=2)
            onsa = take(1024).rearrange("p (c t) -> p c t", c=4)
            osb = take(1024).rearrange("p (c t) -> p c t", c=4)
            ma_f, mb_f = take(2048), take(2048)
            ma, mb = (a.rearrange("p (c t) -> p c t", c=8) for a in (ma_f, mb_f))
            sq, r = take(2048), take(1024)
            L = [take(384) for _ in range(3)]
            PT = [take(384) for _ in range(2)]
            sm = [take(8) for _ in range(3)]
            blk = take(2 * 480).rearrange("p (a i c) -> p a i c", a=2, i=32)
            hid = take(32)
            kcT = take(16)
            hrep = take(128)
            vblk = take(512).rearrange("p (k g d) -> p k g d", k=2, g=4)
            Lc = take(256).rearrange("p (k t g c) -> p k t g c", k=2, t=2, g=4)
            Pc = take(512).rearrange("p (k t g c) -> p k t g c", k=2, t=2, g=4)
            PcT = take(512).rearrange("p (k t n) -> p k t n", k=2, t=2)
            cm = take(48)
            qg = take(1)
            assert o <= AR, o

            i_cs = act(cs, P("c"), ACT.Silu, *start)
            for p in range(12):
                slot, w, arr = load("ada", p)
                wv = w.rearrange("p (k n) -> p k n", k=8)
                for j in range(4):
                    n = 4 * p + j
                    for kk in range(8):
                        last = mm(PS[:, 7, n:n + 1], wv[:, kk, 128 * j:128 * j + 128], cs[:, kk:kk + 1], kk == 0, kk == 7,
                                  *([arr, i_cs, bank_free[7]] if kk == 0 else []))
                release(slot, last)
            i_mod = tt(mod, PS[:, 7, 0:48], P("adab"), ADD, last, *start)
            bank_free[7] = i_mod
            i_t = vcopy(tbl[32:33, :], C("negrow", 33)[32:33, :], *start)
            last = mm(PS[0:8, 6, 0:384], tbl, C("hot", 33), True, True, i_t, bank_free[6], *READY)
            i_F = act(Fv[0:8, :], PS[0:8, 6, 0:384], ACT.Copy, last, *start)
            bank_free[6] = i_F
            d_w = sp(lambda e: e.dma_start(io["fd"].rearrange("(h n) -> h n", h=8), Fv[0:8, :]), i_F, dma=s_bw)
            src = bass.AP(io["fd_t"], 0, [[1, 128], [384, 8], [1, 256]])
            d_r1 = sp(lambda e: e.dma_start(ma_f.rearrange("p (h n) -> p h n", h=8), src), d_w, *start, dma=s_br)
            for p in range(4):
                last = mm(PS[:, p, :], C("flip"), ma_f[:, 512 * p:512 * p + 512], True, True, d_r1, bank_free[p])
                i_B = vcopy(B[:, 2 * p:2 * p + 2, 0:256], PS[:, p, :].rearrange("p (h n) -> p h n", h=2), last, *start)
                bank_free[p] = i_B
            i_B = vcopy(B[:, :, 256:384], B[:, :, 128:256], i_B)
            flipped = last

            def modulate(gname, at, scl, tag):
                a = ts(scl, mod[:, 8 + at:16 + at], 1.0, ADD, i_mod, *start)
                h = rms_T(gname, sq, r[:, 0:256], *state["barrier"], a)
                for c in range(8):
                    last = ts(hT[:, c, :], hT[:, c, :], scl[:, c:c + 1], MUL, *([h] if c == 0 else []),
                              s2=mod[:, at + c:at + c + 1], op1=ADD)
                return last

            u_ok = modulate("n1", 0, sc1, 1)
            i_qg = ts(qg, P("q2", 0), 0.125, MUL, *start)

            def cp(dst, done, *ws, func=ACT.Copy, **kw):
                return lambda j, ps, last: done.append(act(dst(j), ps, func, last, *start, *ws, **kw)) or done[-1]

            dqa, dkv, dvn, dga, dqb, dkb, dvb, dma_, dmb = [], [], [], [], [], [], [], [], []
            lin_T("in2", 0, hT, 8, 512, cp(lambda j: qa[:, j, :], dqa), u_ok)
            lin_T("in2", 1, hT, 8, 512, cp(lambda j: kvT[:, j, :], dkv))
            slot, w, arr = load("in2", 2)
            w3 = w.rearrange("p (k n) -> p k n", k=8)
            lin_row(w3, arr, hT, 8, (0, 256), lambda t, ps, last: dvn.append(
                act(vnsa[:, t, :], ps, ACT.Copy, last, *start)) or dvn[-1])
            last = lin_row(w3, arr, hT, 8, (256, 280), lambda t, ps, last: dga.append(
                act(ga[:, t, :], ps, ACT.Sigmoid, last, *start)) or dga[-1])
            release(slot, last)
            lin_T("in2", 3, hT, 8, 512, cp(lambda j: qb[:, j, :], dqb, scale=0.125))
            lin_T("in2", 4, hT, 8, 512, cp(lambda j: kb[:, j, :], dkb))
            slot, w, arr = load("in2", 5)
            last = lin_row(w.rearrange("p (k n) -> p k n", k=8), arr, hT, 8, (0, 512),
                           lambda t, ps, last: dvb.append(act(vb[:, t, :], ps, ACT.Copy, last, *start)) or dvb[-1])
            release(slot, last)
            for p in range(2):
                lin_T("in2", 6 + p, hT, 8, 512, cp(lambda j, p=p: ma[:, 4 * p + j, :], dma_, flipped, func=ACT.Sigmoid))
            for p in range(2):
                u_last = lin_T("in2", 8 + p, hT, 8, 512, cp(lambda j, p=p: mb[:, 4 * p + j, :], dmb, func=ACT.Sigmoid))

            nq = head_norm(qaf, 4, qg, 0.125, sq, r, [dqa, i_qg, u_ok], range(8))
            nk1 = head_norm(kvTf[:, 512:768], 1, P("k2", 1), 1.0, sq, r, [dkv, nq], range(8))
            nk2 = head_norm(kvTf[:, 768:1024], 1, P("k2", 2), 1.0, sq, r, [dkv, nk1], range(8))

            pos = P("pos")
            bl = []
            for a in range(2):
                kview = kvT[:, a, :].rearrange("p (c j) -> p j c", j=16)
                for half in range(2):
                    bl.append(tt(blk[:, a, 16 * half:16 * half + 16, :], kview[:, :, half:half + 15],
                                 pos[:, 16 * half:16 * half + 16].rearrange("p (i o) -> p i o", o=1).broadcast_to([128, 16, 15]),
                                 ADD, dkv, *start))
            slot, w, arr = load("cw1", 0)
            w4 = w.rearrange("p (a i n) -> p a i n", a=2, i=32)
            for a in range(2):
                for hk in range(2):
                    rows = slice(64 * hk, 64 * hk + 64)
                    b = 4 + hk
                    for i in range(32):
                        last = mm(PS[rows, b, 16 * a:16 * a + 15], w4[rows, a, i, :], blk[rows, a, i, :], i == 0, i == 31,
                                  *([arr, bl, bank_free[b]] if i == 0 else []))
            release(slot, last)
            z = ve(lambda e: e.memset(hid, 0.0), *start)
            hv = hid.rearrange("p (a c) -> p a c", a=2)
            for hk in range(2):
                rows = slice(64 * hk, 64 * hk + 64)
                i_h = act(hv[rows, :, 0:15], PS[rows, 4 + hk, 0:32].rearrange("p (a c) -> p a c", a=2)[:, :, 0:15],
                          ACT.Silu, last, z)
                bank_free[4 + hk] = i_h
            z = ve(lambda e: e.memset(hrep, 0.0), *start)
            i_hr = vcopy(hrep.rearrange("p (g c) -> p g c", g=4)[:, :, 0:16],
                         hid[:, 16:32].rearrange("p (o c) -> p o c", o=1).broadcast_to([128, 4, 16]), i_h, z)
            z = ve(lambda e: e.memset(vblk, 0.0), *start)
            for hk in range(2):
                rows = slice(64 * hk, 64 * hk + 64)
                l1 = mm(PS[rows, hk, 0:15], P("kw2")[rows, :], hid[rows, 0:15], True, True, i_h, bank_free[hk])
                l2 = mm(PS[:, 2 + hk, 0:64], hrep[rows, :], P("vw2")[rows, :], True, True, i_hr, bank_free[2 + hk])
                i_k = vcopy(kcT[rows, 0:15], PS[rows, hk, 0:15], l1, *start)
                bank_free[hk] = i_k
                for g in range(4):
                    i_v = vcopy(vblk[32 * g:32 * g + 32, hk, g, :], PS[32 * g:32 * g + 32, 2 + hk, 0:64], l2, z)
                bank_free[2 + hk] = i_v
            a = act(cm[:, 0:15], kcT[:, 0:15], ACT.Square, i_k, *start)
            last = mm(PS[:, 0, 0:15], C("bd64"), cm[:, 0:15], True, True, a, bank_free[0])
            a = act(cm[:, 16:31], PS[:, 0, 0:15], ACT.Sqrt, last, scale=1.0 / 64, bias=epst)
            bank_free[0] = a
            a = recip(cm[:, 16:31], cm[:, 16:31], a)
            i_kc = stt(kcT[:, 0:15], kcT[:, 0:15], P("k2", 0), cm[:, 16:31], MUL, MUL, a)

            cn = C("cneg").rearrange("p (t c) -> p t c", t=2)
            cok = C("cok").rearrange("p (t c) -> p t c", t=2)
            for hk in range(2):
                bh = B[:, 4 * hk:4 * hk + 4, :]
                bi = vcopy(BC[:, hk, 1, :, 0:15], bh[:, :, 31:256:16], i_B)
                for g in range(4):
                    vcopy(BC[:, hk, 0, g, :], cn[:, 0, :])
                bi = vcopy(BC[:, hk, 0, :, 0:6], bh[:, :, 287:287 + 96:16], ve.last)
                bi = vcopy(BC[:, hk, 0, :, 6:7], bh[:, :, 383:384])
            for hk in range(2):
                rows = slice(64 * hk, 64 * hk + 64)
                b = 2 + hk
                for t in range(2):
                    for g in range(4):
                        last = mm(PS[:, b, 64 * t + 16 * g:64 * t + 16 * g + 15], qa[rows, g, 128 * t:128 * t + 128],
                                  kcT[rows, 0:15], True, True, *([nq, i_kc, bank_free[b]] if not (t or g) else []))
            zp = ve(lambda e: e.memset(Pc, 0.0), *start)
            for hk in range(2):
                a = tt(Lc[:, hk, :, :, 0:15].rearrange("p t g c -> p (t g) c"),
                       PS[:, 2 + hk, 0:128].rearrange("p (n c) -> p n c", c=16)[:, :, 0:15],
                       BC[:, hk, :, :, 0:15].rearrange("p t g c -> p (t g) c"), ADD, last, bi)
                bank_free[2 + hk] = a
            L3 = Lc.rearrange("p k t g c -> p (k t g) c")[:, :, 0:15]
            P3 = Pc.rearrange("p k t g c -> p (k t g) c")[:, :, 0:15]
            a = red(cm[:, 0:16], L3, MAX, a)
            a = tt(L3, L3, cm[:, 0:16].rearrange("p (n o) -> p n o", o=1).broadcast_to([128, 16, 15]), SUB, a)
            a = act(L3, L3, ACT.Exp, a)
            for hk in range(2):
                for t in range(2):
                    e1 = tt(Lc[:, hk, t, :, 0:15], Lc[:, hk, t, :, 0:15],
                            cok[:, t:t + 1, 0:15].broadcast_to([128, 4, 15]), MUL, a)
            a = red(cm[:, 0:16], L3, ADD, e1)
            a = ts(cm[:, 0:16], cm[:, 0:16], 1e-30, MAX, a)
            a = recip(cm[:, 16:32], cm[:, 0:16], a)
            g5 = ga.rearrange("p t (h b) -> p t h b", b=3)
            for hk in range(2):
                for t in range(2):
                    n = 8 * hk + 4 * t
                    a2 = tt(cm[:, 16 + n:20 + n], cm[:, 16 + n:20 + n], g5[:, t, 4 * hk:4 * hk + 4, 0], MUL, a, dga)
            i_pc = tt(P3, L3, cm[:, 16:32].rearrange("p (n o) -> p n o", o=1).broadcast_to([128, 16, 15]), MUL, a2, zp)
            for hk in range(2):
                b = 4 + hk
                for t in range(2):
                    last = transpose(PS[:, b, 128 * t:128 * t + 128], Pc[:, hk, t, :, :].rearrange("p g c -> p (g c)"),
                                     i_pc, bank_free[b])
                i_pct = act(PcT[:, hk, :, :].rearrange("p t n -> p (t n)"), PS[:, b, 0:256], ACT.Copy, last, *start)
                bank_free[b] = i_pct

            items = [(c, hk, br) for c in range(4) for br in range(2) for hk in range(2)]

            def logits(it, t1, t0, waits):
                c, hk, br = it
                rows = slice(64 * hk, 64 * hk + 64)
                mm(t1, qa[rows, c, 128:256], kvT[rows, 2 + br, :], True, True, waits, skip=True)
                return mm(t0, qa[rows, c, 0:128], kvT[rows, 2 + br, 0:128], False, True, skip=True)

            def out_of(i, it):
                c, hk, br = it
                b = 6 + c % 2
                return (PS[64 * hk:64 * hk + 64, b, 0:256], br == 0, False, [bank_free[b]])

            o_done = []

            def extra(i, it, out, last):
                c, hk, br = it
                if br == 1:
                    for t in range(2):
                        last = mm(out[:, 128 * t:128 * t + 128], vblk[:, hk, c, :], PcT[:, hk, t, :], False, t == 1,
                                  i_pct, i_v, skip=True)
                    if hk == 1:
                        b = 6 + c % 2
                        bank_free[b] = act(onsa[:, c, :], PS[:, b, 0:256], ACT.Copy, last)
                        o_done.append(bank_free[b])

            def mult(it):
                c, hk, br = it
                return g5[:, ::-1, c + 4 * hk, 1 + br]

            softmax_pv(items, logits, lambda it: B[:, it[0] + 4 * it[1], :],
                       lambda it, st: vnsa[:, st, 128 * it[2] + 64 * it[1]:128 * it[2] + 64 * it[1] + 64],
                       out_of, mult, L, PT, sm, [nq, nk1, nk2, dvn, i_B, dga], extra)

            sb_done = stick(qb, kb, vb, osb, sq, r, L, PT, [dqb, dkb, dvb, nk2])

            ym = hT
            up_ok = {}
            slot1, wn, arr1 = load("upn", 0)
            slot2, wsb, arr2 = load("ups", 0)
            wn = wn.rearrange("p (k n) -> p k n", k=4)
            wsb = wsb.rearrange("p (k n) -> p k n", k=4)
            for c in range(8):
                b = next_bank((0, 1, 2, 3))
                pa, pb = PS[:, b, 0:256], PS[:, b, 256:512]
                for kk in range(4):
                    la = mm(pa, wn[:, kk, 128 * c:128 * c + 128], onsa[:, kk, :], kk == 0, kk == 3,
                            *([arr1, arr2, bank_free[b], o_done, sb_done] if kk == 0 else []))
                for kk in range(4):
                    lb = mm(pb, wsb[:, kk, 128 * c:128 * c + 128], osb[:, kk, :], kk == 0, kk == 3)
                i1 = tt(ma[:, c, :], pa, ma[:, c, :], MUL, lb, dma_)
                i2 = tt(mb[:, c, :], pb, mb[:, c, :], MUL, lb, dmb)
                bank_free[b] = i2
                up_ok[c] = tt(ym[:, c, :], ma[:, c, :], mb[:, c, :], ADD, i1, i2, u_last)
            release(slot1, lb)
            release(slot2, lb)
            residual("out2", ym, 8, [up_ok[c] for c in range(8)], lambda c: mod[:, 16 + c:17 + c])
            phase()
            u2_ok = modulate("n2", 24, sc2, 2)
            hidT = arena[:, 8192:16384].rearrange("p (c t) -> p c t", c=32)
            h_done = []
            rb = [arena[:, 4096 + 256 * i:4352 + 256 * i] for i in range(4)]
            assert AR >= 16384
            for p in range(8):
                def evict(j, ps, last, p=p):
                    i = 4 * p + j
                    rr = act(rb[i % 4], ps, ACT.Relu, last, *state["barrier"], u2_ok,
                             *([h_done[i - 4]] if i >= 4 else []))
                    h_done.append(tt(hidT[:, i, :], rb[i % 4], rb[i % 4], MUL, rr, *state["barrier"]))
                    return rr
                lin_T("w1", p, hT, 8, 512, evict, u2_ok)
            residual("w2", hidT, 32, h_done, lambda c: mod[:, 40 + c:41 + c])

        def stick(qb, kb, vb, osb, sq, r, L, PT, deps):
            n = 8
            lg, p_ok, o_done = {}, {}, []
            cum_ok, a_use, l_use = {}, {}, {}
            A1 = [sq[:, 384 * i:384 * i + 384] for i in range(3)]
            A2 = [sq[:, 1152 + 384 * i:1152 + 384 * i + 384] for i in range(2)] + [r[:, 0:384]]
            def stage_a(i):
                rows = slice(64 * (i % 2), 64 * (i % 2) + 64)
                c, b = i // 2, i % 4
                ps = PS[:, b, 0:384]
                mm(ps[:, 0:256], kb[rows, c, 0:128], qb[rows, c, :], True, False, deps, bank_free[b], skip=True)
                mm(ps[:, 256:384], kb[rows, c, 128:256], qb[rows, c, 128:256], False, False, skip=True)
                mm(ps[:, 0:128], ident, C("sbm"), False, False, skip=True)
                lg[i] = mm(ps[:, 256:384], ident, C("sbm"), False, False, skip=True)
                x, y = A1[i % 3], A2[i % 3]
                a = act(x, ps, ACT.Abs, lg[i], cum_ok.get(i - 3), deps)
                a = act(x, x, ACT.Exp, a, scale=-1.0)
                a = act(x, x, ACT.Ln, a, bias=onet)
                p_ok[i] = stt(x, ps, 0.0, x, MAX, ADD, a)

            def stage_b(i):
                b = i % 4
                ps = PS[:, b, 0:384]
                x, y = A1[i % 3], A2[i % 3]
                mm(ps[:, 0:256], C("ntri"), x[:, 0:256], False, False, p_ok[i], skip=True)
                mm(ps[:, 128:256], C("nones"), x[:, 256:384], False, False, skip=True)
                cum_ok[i] = mm(ps[:, 256:384], C("ntri"), x[:, 256:384], False, True, skip=True)
                a = act(y, ps, ACT.Exp, cum_ok[i], a_use.get(i - 3), deps)
                bank_free[b] = a
                ob = 6 + (i // 2) % 2
                out = PS[64 * (i % 2):64 * (i % 2) + 64, ob, 0:256]
                mm(out, vb[:, 0, 64 * i:64 * i + 64], y[:, 0:256], True, False, a, bank_free[ob], skip=True)
                a_use[i] = mm(out[:, 128:256], vb[:, 1, 64 * i:64 * i + 64], y[:, 256:384], False, True, skip=True)
                if i % 2:
                    bank_free[ob] = act(osb[:, i // 2, :], PS[:, ob, 0:256], ACT.Copy, a_use[i])
                    o_done.append(bank_free[ob])

            for i in range(n + 1):
                if i < n:
                    stage_a(i)
                if i >= 1:
                    stage_b(i - 1)
            return o_done

        steps = [even_layer, lambda: peer_layer(0), odd_layer, lambda: peer_layer(1), last_block]
        for s in steps[:stop]:
            s()
        fin = phase()
        done = sp(lambda e: e.dma_start(io["out"], xTt[:, :]), *fin, dma=s_out)
        sp(lambda e: e.nop(), done)

        counts = {}
        for q in (pe, ve, ac, po, sp):
            n = 0
            for ins in q.items:
                if ins.sem is not None:
                    counts[id(ins.sem)] = ins.value = counts.get(id(ins.sem), 0) + 16
                elif ins.signals:
                    n += 1
                    ins.value = n

        def emit(q, e):
            seen = {}
            for ins in q.items:
                for w in ins.waits:
                    s = w.sem if w.sem is not None else w.queue.own
                    if seen.get(id(s), 0) < w.value:
                        seen[id(s)] = w.value
                        e.wait_ge(s, w.value)
                r = ins.fn(e)
                if ins.sem is not None:
                    r.then_inc(ins.sem, 16)
                elif ins.signals:
                    r.then_inc(q.own, 1)

        block = ctx.enter_context(nc.Block())
        block.sync(lambda e: emit(sp, e))
        block.gpsimd(lambda e: emit(po, e))
        block.scalar(lambda e: emit(ac, e))
        block.vector(lambda e: emit(ve, e))
        block.tensor(lambda e: emit(pe, e))


def pack(w, ranges):
    kc = w.shape[0] // 128
    v = w.reshape(kc, 128, w.shape[1])
    return np.concatenate([np.ascontiguousarray(v[:, :, lo:hi].transpose(1, 0, 2)).reshape(-1) for lo, hi in ranges])


def layout(inputs):
    g = {k: np.asarray(v) for k, v in inputs.items()}
    a = {}
    a["cst"] = constants()
    cols = np.zeros((128, NCOL), np.float32)

    def put(name, m):
        lo, hi = COL[name]
        cols[: m.shape[0], lo:hi] = m

    col = lambda v: v.reshape(-1, 128).T
    twice = lambda v: np.concatenate([v, v], 0)
    put("ev_g", col(g["ev_norm_mix"][0]))
    put("od_g", col(g["od_norm_mix"][0]))
    put("f0", col(g["ffn_norm"][0]))
    put("f1", col(g["ffn_norm"][1]))
    put("n1", col(g["norm1_g_2"][0]))
    put("n2", col(g["norm2_g_2"][0]))
    put("cw", g["ev_conv_w"][0].reshape(31, 4, 128).transpose(2, 0, 1).reshape(128, 124))
    put("cb", col(g["ev_conv_b"][0]))
    put("lng", col(g["ev_conv_ln_g"][0]))
    put("lnb", col(g["ev_conv_ln_b"][0]))
    put("gb", col(g["ev_gate_b"][0]))
    put("glag", col(g["ev_gla_norm_g"][0]))
    put("qg", twice(g["od_q_norm_g"][0])[:, None])
    put("kg", twice(g["od_k_norm_g"][0])[:, None])
    put("fb", g["od_fgate_b"][0][:, None])
    put("c", col(g["c_2"][0]))
    put("adab", col(g["ada_b_2"][0]))
    put("q2", twice(g["q_norm_g_2"][0])[:, None])
    put("k2", twice(g["k_norm_g_2"][0].T))
    put("pos", twice(g["cmp_pos_2"][0].T))
    put("kw2", twice(g["cmp_k_w2_2"][0]))
    put("vw2", twice(g["cmp_v_w2_2"][0]))
    a["cols"] = cols
    a["xT"] = np.ascontiguousarray(g["x"][0].T.reshape(8, 128, T).transpose(1, 0, 2)).reshape(128, 8 * T)
    a["gw2"] = g["ev_gate_w2"][0]
    a["rel"] = g["rel_bias_2"]
    a["ev_in"] = pack(g["ev_w_in"][0], EV_RANGES)
    a["ev_out"] = pack(g["ev_w_out"][0], FULL)
    a["od_in"] = pack(g["od_w_in"][0], OD_RANGES)
    a["od_out"] = pack(g["od_w_out"][0], FULL)
    for i in range(2):
        a[f"wq{i}"] = pack(g["peer_wq"][i], WQ_RANGES)
        a[f"keys{i}"] = np.ascontiguousarray(g["peer_keys"][i].reshape(16, 128, 128).transpose(2, 0, 1)).reshape(-1)
        a[f"u{i}"] = g["peer_u"][i]
        a[f"v{i}"] = g["peer_v"][i]
    a["ada"] = pack(g["ada_w_2"][0], ADA_RANGES)
    a["in2"] = pack(g["w_in_2"][0][:, IN_ORDER], IN_RANGES)
    w1 = [g[n][0].reshape(32, 64, 64).transpose(1, 0, 2).reshape(64, 2048) for n in ("cmp_k_w1_2", "cmp_v_w1_2")]
    a["cw1"] = twice(np.concatenate(w1, 1)).reshape(-1)
    a["upn"] = pack(g["w_up_nsa_2"][0][QPERM], UP_RANGES)
    a["ups"] = pack(g["w_up_sb_2"][0], UP_RANGES)
    a["out2"] = pack(g["w_out_2"][0], FULL)
    a["w1"] = pack(g["mlp_w1_2"][0], W1_RANGES)
    a["w2"] = pack(g["mlp_w2_2"][0], W2_RANGES)
    return {k: np.ascontiguousarray(v) for k, v in a.items()}


def kernel(**inputs):
    import concourse.bacc as _bacc
    from concourse.bass_utils import run_bass_kernel_spmd as _run

    arrays = layout(inputs)
    nc = _bacc.Bacc("TRN2", target_bir_lowering=False, num_devices=1)
    program(nc, declare(nc, arrays))
    r = _run(nc, [{f"in_{k}": v for k, v in arrays.items()}], core_ids=[0])
    out = np.asarray(r.results[0]["out_0"]).reshape(128, 8, T)
    return np.ascontiguousarray(out.transpose(2, 1, 0)).reshape(1, T, D)
```

```python
from contextlib import ExitStack

import numpy as np

import concourse.bass as bass
import concourse.mybir as mybir

F32 = mybir.dt.float32
F32R = mybir.dt.float32r
U32 = mybir.dt.uint32
ALU = mybir.AluOpType
ACT = mybir.ActivationFunctionType
AX = mybir.AxisListType.X

T = 256
D = 1024
NEG = -1e30
EPS = 1e-6
PAIRS = [(i, j) for i in range(16) for j in range(16) if (i + 1) * (j + 1) <= 16]
NP = len(PAIRS)
WSLOT = 4096
NW = 4

EV_RANGES = [(1024, 1536), (2560, 2576), (512, 1024), (0, 512), (1536, 2048), (2048, 2560)]
OD_RANGES = [(0, 512), (3072, 3088), (1024, 1536), (2048, 2560), (512, 1024), (1536, 2048), (2560, 3072)]
FULL = [(0, 512), (512, 1024)]
WQ_RANGES = [(i * 512, i * 512 + 512) for i in range(4)]
ADA_RANGES = [(i * 512, i * 512 + 512) for i in range(12)]
W1_RANGES = [(i * 512, i * 512 + 512) for i in range(8)]
W2_RANGES = [(i * 128, i * 128 + 128) for i in range(8)]
UP_RANGES = [(0, 1024)]
QPERM = [h * 64 + i for c in range(4) for h in (c, c + 4) for i in range(64)]
IN_ORDER = (QPERM + list(range(512, 768)) + list(range(768, 896)) + list(range(1024, 1152))
            + list(range(896, 1024)) + list(range(1152, 1304)) + list(range(1304, 4888)))
IN_RANGES = [(0, 512), (512, 1024), (1024, 1304), (1304, 1816), (1816, 2328), (2328, 2840),
             (2840, 3352), (3352, 3864), (3864, 4376), (4376, 4888)]

CST = {}
_n = 0
for _name, _w in [("ident", 128), ("ones", 128), ("bd64", 128), ("ntri", 128), ("nones", 128), ("sbm", 128), ("flip", 128),
                  ("fmask", 384), ("gm", 7 * 64), ("reset", 256), ("hot", 384), ("iota", 128), ("negrow", 8),
                  ("cneg", 2 * 16), ("cok", 2 * 16)]:
    CST[_name] = (_n, _n + _w)
    _n += _w
NCST = _n

COL = {}
_n = 0
for _name, _w in [("ev_g", 8), ("od_g", 8), ("f0", 8), ("f1", 8), ("n1", 8), ("n2", 8), ("cw", 124), ("cb", 4),
                  ("lng", 4), ("lnb", 4), ("gb", 2), ("glag", 1), ("qg", 1), ("kg", 1), ("fb", 1), ("c", 8), ("adab", 48),
                  ("q2", 1), ("k2", 3), ("pos", 32), ("kw2", 64), ("vw2", 64)]:
    COL[_name] = (_n, _n + _w)
    _n += _w
NCOL = _n


def constants():
    c = np.zeros((128, NCST), np.float32)

    def put(name, a):
        lo, hi = CST[name]
        c[: a.shape[0], lo:hi] = a.reshape(a.shape[0], -1)

    p = np.arange(128)
    put("ident", np.eye(128))
    put("ones", np.ones((128, 128)))
    put("nones", -np.ones((128, 128)))
    put("flip", np.eye(128)[::-1])
    put("bd64", (p[:, None] // 64 == p[None, :] // 64) * 1.0)
    put("ntri", (p[:, None] >= p[None, :]) * -1.0)
    put("sbm", np.where(p[:, None] < p[None, :], 0.0, NEG))
    causal = np.where(p[None, :] <= p[:, None], 0.0, NEG)
    put("fmask", np.concatenate([np.zeros((128, 128)), causal, causal], 1))
    gm = np.zeros((128, 7, 64))
    s, t = p % 64, np.arange(64)
    gm[:, 0] = s[:, None] == t[None, :]
    for lv in range(1, 7):
        g = 1 << lv
        gm[:, lv] = (s[:, None] // g == t[None, :] // g) & (s[:, None] % g < g // 2) & (t[None, :] % g >= g // 2)
    put("gm", gm)
    put("reset", np.tile((np.arange(256) % 64 != 0) * 1.0, (128, 1)))
    dist = 255 - np.arange(384)
    n = np.maximum(dist, 0)
    nf = np.maximum(n, 1).astype(np.float32)
    large = 16 + (np.log(nf / np.float32(16)) / np.float32(np.log(8.0)) * np.float32(16)).astype(np.int32)
    bucket = np.where(n < 16, n, np.minimum(large, 31))
    hot = np.zeros((33, 384))
    hot[bucket, np.arange(384)] = 1.0
    hot[:, dist < 0] = 0.0
    hot[32, dist < 0] = 1.0
    put("hot", hot)
    put("iota", np.tile(np.arange(128), (128, 1)))
    put("negrow", np.full((33, 8), NEG))
    ok = np.zeros((128, 2, 16))
    for tile in range(2):
        ok[:, tile, :15] = (tile * 128 + p)[:, None] >= (np.arange(15) * 16 + 31)[None, :]
    put("cok", ok)
    put("cneg", np.where(ok > 0, 0.0, NEG))
    return c


class Ins:
    __slots__ = ("queue", "fn", "waits", "sem", "value", "signals")

    def __init__(self, queue, fn, waits, sem):
        self.queue, self.fn, self.waits, self.sem = queue, fn, waits, sem
        self.value, self.signals = 0, sem is not None


def leaves(waits):
    for w in waits:
        if isinstance(w, (list, tuple)):
            yield from leaves(w)
        elif w is not None:
            yield w


class Queue:

    def __init__(self, own):
        self.own, self.items = own, []

    def __call__(self, fn, *waits, dma=None):
        ins = Ins(self, fn, list(leaves(waits)), dma)
        for w in ins.waits:
            w.signals = True
        self.items.append(ins)
        return ins

    @property
    def last(self):
        return self.items[-1] if self.items else None


def flat(pieces):
    at, out = 0, []
    for w in pieces:
        out.append((at, w))
        at += 128 * w
    return out, at


def widths(ranges, kc):
    return [(hi - lo) * kc for lo, hi in ranges]


WEIGHTS = {
    "ev_in": widths(EV_RANGES, 8), "ev_out": widths(FULL, 8), "od_in": widths(OD_RANGES, 8),
    "od_out": widths(FULL, 8), "wq0": widths(WQ_RANGES, 8), "wq1": widths(WQ_RANGES, 8),
    "ada": widths(ADA_RANGES, 8), "in2": widths(IN_RANGES, 8),
    "cw1": [4096, 4096], "upn": widths(UP_RANGES, 4), "ups": widths(UP_RANGES, 4), "out2": widths(FULL, 8),
    "w1": widths(W1_RANGES, 8), "w2": widths(W2_RANGES, 32),
}


def declare(nc, arrays):
    io = {}
    for name, a in arrays.items():
        io[name] = nc.dram_tensor(f"in_{name}", a.shape, F32, kind="ExternalInput").ap()
    io["out"] = nc.dram_tensor("out_0", (128, 8 * T), F32, kind="ExternalOutput").ap()
    io["fd_t"] = nc.dram_tensor("fd", (8 * 384,), F32, kind="Internal")
    io["fd"] = io["fd_t"].ap()
    return io


def program(nc, io, stop=99):
    ctx = ExitStack()
    with ctx:
        sem = lambda name: ctx.enter_context(nc.semaphore(name))
        sb = lambda name, n: ctx.enter_context(nc.sbuf_tensor(name, [128, n], F32))

        AR, XR = 22016, 6144
        base = {"hT": (nc.sbuf_base + 31) // 32 * 32}
        hTt = sb("hT", 2048)
        base["mem"] = (nc.sbuf_base + 31) // 32 * 32
        mem = sb("mem", NW * WSLOT + AR + XR)
        wring = [mem[:, 3 * WSLOT + AR + XR:]] + [mem[:, i * WSLOT:(i + 1) * WSLOT] for i in range(3)]
        arena = mem[:, 3 * WSLOT:3 * WSLOT + AR + XR]
        hhi = arena[:, AR:AR + 2048]
        S = [(arena[:, AR + 2048 + 2048 * i:AR + 3072 + 2048 * i], arena[:, AR + 3072 + 2048 * i:AR + 4096 + 2048 * i])
             for i in range(2)]
        xTt = sb("xT", 2048)
        cst = sb("cst", NCST)
        col = sb("col", NCOL)
        small = sb("small", 1024)
        arena_u = arena[:, :].bitcast(U32)
        PS = ctx.enter_context(nc.psum_tensor("PS", [128, 8, 512], F32))

        pe, ve, ac, po, sp = (Queue(sem(f"s_{n}")) for n in ("pe", "ve", "ac", "po", "sp"))
        wsem = [sem(f"s_w{i}") for i in range(NW)]
        gsem = [sem(f"s_g{i}") for i in range(4)]
        s_cst, s_col, s_x, s_misc, s_key, s_bw, s_br, s_out = (
            sem(n) for n in ("s_cst", "s_col", "s_x", "s_misc", "s_key", "s_bw", "s_br", "s_out"))

        def C(name, rows=128):
            lo, hi = CST[name]
            return cst[0:rows, lo:hi]

        def P(name, i=None):
            lo, hi = COL[name]
            return col[:, lo:hi] if i is None else col[:, lo + i:lo + i + 1]

        xT = xTt[:, :].rearrange("p (c t) -> p c t", c=8)
        hT = hTt[:, :].rearrange("p (c t) -> p c t", c=8)
        ident = C("ident")
        ones = C("ones")

        l_cst = sp(lambda e: e.dma_start(cst[:, :], io["cst"]), dma=s_cst)
        l_x = sp(lambda e: e.dma_start(xTt[:, :], io["xT"]), dma=s_x)
        l_col = sp(lambda e: e.dma_start(col[:, :], io["cols"]), dma=s_col)
        gw2 = small[0:16, 0:256]
        rr_ = small[:, 256:512]
        cs, mod = small[:, 528:536], small[:, 536:584]
        tbl = small[0:33, 512:520]
        l_gw2 = sp(lambda e: e.dma_start(gw2, io["gw2"]), dma=s_misc)
        l_tbl = sp(lambda e: e.dma_start(small[0:32, 512:520], io["rel"]), dma=s_misc)
        READY = [l_cst, l_col, l_tbl, l_x]

        ring = {"n": 0, "free": [None] * NW}

        def load(name, piece):
            i = ring["n"] % NW
            ring["n"] += 1
            assert ring["free"][i] != "held"
            pieces, _ = flat(WEIGHTS[name])
            at, w = pieces[piece]
            src = io[name][at:at + 128 * w].rearrange("(p f) -> p f", p=128)
            dst = wring[i][:, 0:w]
            ins = sp(lambda e: e.dma_start(dst, src), ring["free"][i], dma=wsem[i])
            ring["free"][i] = "held"
            return i, dst, ins

        def release(slot, reader):
            ring["free"][slot] = reader

        bank_free = [None] * 8

        def mm(out, lhsT, rhs, start, stop, *waits, skip=False):
            return pe(lambda e: e.matmul(out, lhsT, rhs, start=start, stop=stop, skip_group_check=skip), *waits)

        def transpose(out, in_, *waits):
            return pe(lambda e: e.transpose(out, in_, ident), *waits)

        tables = {"now": None}

        def act(out, in_, func, *waits, **kw):
            need = {ACT.Exp: "natural_log_exp_and_others", ACT.Ln: "natural_log_exp_and_others", ACT.Gelu: "gelu",
                    ACT.Silu: "silu", ACT.Sigmoid: "sigmoid"}.get(func)
            if need and need != tables["now"]:
                tables["now"] = need
                if need == "natural_log_exp_and_others":
                    ac(lambda e: e.preload_act_table_set(need))
            return ac(lambda e: e.activation(out, in_, func, **kw), *waits)

        def tt(out, a, b, op, *waits):
            return ve(lambda e: e.tensor_tensor(out, a, b, op), *waits)

        def ts(out, a, s1, op0, *waits, s2=None, op1=None):
            if op1 is None:
                return ve(lambda e: e.tensor_scalar(out, a, s1, None, op0), *waits)
            return ve(lambda e: e.tensor_scalar(out, a, s1, s2, op0, op1), *waits)

        def stt(out, a, s, b, op0, op1, *waits):
            return ve(lambda e: e.scalar_tensor_tensor(out=out, in0=a, scalar=s, in1=b, op0=op0, op1=op1), *waits)

        def vcopy(out, in_, *waits):
            return ve(lambda e: e.tensor_copy(out, in_), *waits)

        def red(out, in_, op, *waits, negate=False):
            return ve(lambda e: e.tensor_reduce(out, in_, AX, op, negate=negate), *waits)

        def recip(out, in_, *waits):
            return ve(lambda e: e.reciprocal(out, in_), *waits)

        MUL, ADD, SUB, MAX, MIN, EQ, GT = ALU.mult, ALU.add, ALU.subtract, ALU.max, ALU.min, ALU.is_equal, ALU.is_gt

        state = {"barrier": [], "hT": None, "x": [None] * 8, "h": None}

        def phase():
            state["barrier"] = [q.last for q in (pe, ve, ac, po) if q.last is not None]
            return state["barrier"]

        cursor = {"bank": 0}

        def next_bank(banks):
            b = banks[cursor["bank"] % len(banks)]
            cursor["bank"] += 1
            return b

        over = {}

        def rounded(*aps):
            for ap in aps:
                name, lo, n = ap.tensor.name, ap.offset, ap.ap[-1][1]
                t = over.pop((name, lo, lo + n), None)
                over[name, lo, lo + n] = t or nc.alloc_sbuf_tensor_at(
                    f"r_{name}_{lo}_{n}", [128, n], F32R, offset=base[name] + 4 * lo)

        def R(ap):
            end = ap.offset + 1 + sum(s * (n - 1) for s, n in ap.ap[1:])
            for (name, lo, hi), t in reversed(over.items()):
                if name == ap.tensor.name and lo <= ap.offset and end <= hi:
                    return bass.AP(t, ap.offset - lo, [[hi - lo, 128], *ap.ap[1:]])
            raise AssertionError("no float32r tensor there")

        rounded(hTt[:, :], hhi, *[x for pair in S for x in pair])

        def RF(ap):
            return R(ap).bitcast(F32)

        hhiv = R(hhi).rearrange("p (c t) -> p c t", c=8)
        hlov = R(hTt[:, :]).rearrange("p (c t) -> p c t", c=8)
        H3 = (hhiv, hlov)
        sring = {"n": 0, "free": [None] * 2}

        def split(src, *waits):
            i = sring["n"] % 2
            sring["n"] += 1
            assert sring["free"][i] != "held"
            a, n = src.shape[1], src.shape[1] * src.shape[2]
            hi, lo = (x[:, 0:n].rearrange("p (a b) -> p a b", a=a) for x in S[i])
            i_h = act(R(hi), src, ACT.Copy, sring["free"][i], *waits)
            i_l = tt(R(lo), src, RF(hi), SUB, i_h)
            sring["free"][i] = "held"
            return i, R(hi), R(lo), i_h, i_l

        def mm3(out, hi, lo, shi, slo, i_h, i_l, start, stop, *waits, ready=None):
            n = hi.shape[1]
            for k in range(n):
                mm(out, hi[:, k, :], shi[:, k, :], start and k == 0, False, *([i_h, *waits] if k == 0 else []),
                   ready and ready[k][0])
                mm(out, hi[:, k, :], slo[:, k, :], False, False, ready and ready[k][1])
            for k in range(n):
                last = mm(out, lo[:, k, :], shi[:, k, :], False, stop and k == n - 1, *([i_l] if k == 0 else []))
            return last

        def tiles_T(name, piece, src, kc, evict, *waits, banks=(0, 1, 2, 3, 4, 5, 6, 7)):
            slot, w, arrived = load(name, piece)
            wv = w.rearrange("p (k n) -> p k n", k=kc)
            ncols = wv.shape[2]
            pair = isinstance(src, (tuple, list))
            ku = min(kc, 8)
            bank = {}
            for j in range((ncols + 127) // 128):
                m = min(128, ncols - 128 * j)
                for u in range(kc // ku):
                    final = 128 * j + m == ncols and u == kc // ku - 1
                    part = wv[:, ku * u:ku * u + ku, 128 * j:128 * j + m]

                    def prepare(part=part, final=final):
                        if not pair:
                            return None
                        sp_ = split(part, arrived)
                        if final:
                            release(slot, sp_[4])
                        return sp_

                    def run(sp_, part=part, final=final, j=j, m=m, u=u):
                        if u == 0:
                            bank["b"] = next_bank(banks)
                        b = bank["b"]
                        out = PS[0:m, b, 0:256]
                        ks = slice(ku * u, ku * u + ku)
                        ends = u == kc // ku - 1
                        if pair:
                            i, hi, lo, i_h, i_l = sp_
                            shi, slo = src[u] if isinstance(src, list) else (src[0][:, ks, :], src[1][:, ks, :])
                            last = mm3(out, hi, lo, shi, slo, i_h, i_l, u == 0, ends,
                                       *([bank_free[b], waits] if u == 0 else []),
                                       ready=state["h"] if src is H3 and j == 0 else None)
                            sring["free"][i] = last
                        else:
                            for k in range(ku):
                                last = mm(out, part[:, k, :], src[:, ku * u + k, :], u == 0 and k == 0, ends and k == ku - 1,
                                          *([arrived, bank_free[b], waits] if k == 0 else []))
                            if final:
                                release(slot, last)
                        if src is hT or src is H3:
                            state["hT"] = last
                        if ends:
                            bank_free[b] = evict(j, out, last)
                        return last

                    yield prepare, run

        def rows_T(name, piece, evict, *waits, banks=(0, 1, 2, 3, 4, 5, 6, 7), src=None):
            src = src or H3
            slot, w, arrived = load(name, piece)
            wv = w.rearrange("p (k n) -> p k n", k=8)
            n = wv.shape[2]
            bank = []
            for u in range(4):
                part = wv[:, 2 * u:2 * u + 2, :]

                def prepare(part=part, u=u):
                    sp_ = split(part, arrived)
                    if u == 3:
                        release(slot, sp_[4])
                    return sp_

                def run(sp_, u=u):
                    i, hi, lo, i_h, i_l = sp_
                    if u == 0:
                        bank.extend(next_bank(banks) for _ in range(2))
                    for t in range(2):
                        toks = slice(128 * t, 128 * t + 128)
                        ks = slice(2 * u, 2 * u + 2)
                        last = mm3(PS[:, bank[t], 0:n], src[0][:, ks, toks], src[1][:, ks, toks], hi, lo, i_h, i_l,
                                   u == 0, u == 3, *([bank_free[bank[t]], waits] if u == 0 else []), i_l, state["h"])
                        if u == 3:
                            bank_free[bank[t]] = evict(t, PS[:, bank[t], 0:n], last)
                    sring["free"][i] = last
                    state["hT"] = last
                    return last

                yield prepare, run

        def stream(*gens):
            cur = None
            for g in gens:
                for prepare, run in g:
                    nxt = (run, prepare())
                    if cur is not None:
                        yield cur[0](cur[1])
                    cur = nxt
            yield cur[0](cur[1])

        def lin(*gens):
            for last in stream(*gens):
                pass
            return last

        def lin_T(*a, **kw):
            return lin(tiles_T(*a, **kw))

        def rows(name, piece, evict, *waits, banks=(0, 1, 2, 3, 4, 5, 6, 7)):
            slot, w, arrived = load(name, piece)
            w = w.rearrange("p (k n) -> p k n", k=8)
            for t in range(2):
                b = next_bank(banks)
                for k in range(8):
                    last = mm(PS[:, b, :], hT[:, k, 128 * t:128 * t + 128], w[:, k, :], k == 0, k == 7,
                              *([arrived, bank_free[b], *waits] if k == 0 else []))
                bank_free[b] = evict(t, PS[:, b, :], last)
            release(slot, last)
            state["hT"] = last
            return last

        class Filler:

            def __init__(self, *gens):
                self.gens = list(gens)

            def step(self, n=1):
                while n and self.gens:
                    if next(self.gens[0], None) is None:
                        self.gens.pop(0)
                    else:
                        n -= 1

            def drain(self):
                self.step(10 ** 6)

        def rms_T(gain, *waits, shift=None, banks=range(8), parts=True):
            b = next_bank(banks)
            ps = PS[:, b, 0:256]
            for c in range(8):
                i_sq = act(hT[:, c, :], xT[:, c, :], ACT.Square, state["x"][c], state["hT"], *waits)
                last = mm(ps, ones, hT[:, c, :], c == 0, c == 7, i_sq, *([bank_free[b], l_cst] if c == 0 else []))
            i_r = act(rr_, ps, ACT.Ln, last, scale=1.0 / D, bias=epst)
            bank_free[b] = i_r
            i_rr = act(rr_, rr_, ACT.Exp, i_r, scale=-0.5)
            high, state["h"] = [], []

            def low(c):
                return tt(hlov[:, c, :], hT[:, c, :], RF(hhi[:, 256 * c:256 * c + 256]), SUB, high[c])

            for c in range(8):
                last = stt(hT[:, c, :], xT[:, c, :], gain(c), rr_, MUL, MUL, *([i_rr, *waits] if c == 0 else []))
                if shift is not None:
                    last = ts(hT[:, c, :], hT[:, c, :], shift(c), ADD, last)
                if parts:
                    high.append(act(hhiv[:, c, :], hT[:, c, :], ACT.Copy, last, *state["barrier"]))
                    if c >= 1:
                        state["h"].append((high[c - 1], low(c - 1)))
            if not parts:
                return last
            state["h"].append((high[7], low(7)))
            return None

        def parts_of(raw, hi, *waits):
            i_h = act(R(hi), raw, ACT.Copy, *waits)
            return tt(R(raw), raw, RF(hi), SUB, i_h)

        def residual(name, src, kc, deps, gate=None):
            n = len(WEIGHTS[name])
            tiles = 8 // n

            def evict(p):
                def f(j, ps, last):
                    c = p * tiles + j
                    if gate is None:
                        state["x"][c] = tt(xT[:, c, :], ps, xT[:, c, :], ADD, last)
                    else:
                        state["x"][c] = stt(xT[:, c, :], ps, gate(c), xT[:, c, :], MUL, ADD, last)
                    return state["x"][c]
                return f

            return lin(*[tiles_T(name, p, src, kc, evict(p), deps) for p in range(n)])

        epst = small[:, 520:521]
        onet = small[:, 521:522]
        i_e = ve(lambda e: e.memset(epst, EPS))
        i_one = ve(lambda e: e.memset(onet, 1.0))
        READY += [i_e, i_one]

        def even_layer():
            o = 0

            def take(n):
                nonlocal o
                o += n
                return arena[:, o - n:o]

            chunks = lambda a, c: a.rearrange("p (c t) -> p c t", c=c)
            gate, rTf, yf, qkf, of, o2, ysq = (take(1024) for _ in range(7))
            gate, rT, y = chunks(gate, 4), chunks(rTf, 4), chunks(yf, 4)
            qk = chunks(qkf, 4)
            up = chunks(take(4 * 286), 4)
            vrow = chunks(take(1024), 2)
            glr, mean = take(256), take(256)
            bf, w0, w1, w2, qd, kd = (take(512) for _ in range(6))
            qlb = [take(512) for _ in range(6)]
            klb = [take(512) for _ in range(6)]
            kdrow = chunks(take(512), 2)
            dl = take(8)
            Stf, Atf = take(1024), take(1024)
            St = Stf.rearrange("p (n c d) -> p n c d", n=4, c=2)
            At = Atf.rearrange("p (a n t) -> p a n t", a=2, n=4)
            yTf = take(2048)
            yT = chunks(yTf, 8)
            assert o <= AR + XR, o

            zups = [po(lambda e: e.memset(up[:, :, 0:30], 0.0))]
            zl = [po(lambda e, a=a: e.memset(a, 0.0)) for a in qlb + klb]
            zA = po(lambda e: e.memset(Atf, 0.0))
            zS = po(lambda e: e.memset(St[:, 0, :, :], 0.0))
            state["cs"] = act(cs, P("c"), ACT.Silu, READY)
            h_ok = rms_T(lambda c: P("ev_g", c), READY, parts=False)
            qks = []
            lin_T("ev_in", 0, hT, 8, lambda j, ps, last: qks.append(
                act(qk[:, j, :], ps, ACT.Copy, last, scale=0.125 if j < 2 else 1.0)) or qks[-1], h_ok)
            gl = []
            lin_T("ev_in", 1, hT, 8, lambda j, ps, last: gl.append(act(glr[0:16, :], ps, ACT.Copy, last)) or gl[-1])
            x_in = []
            for c in range(2):
                b = next_bank(range(8))
                last = mm(PS[:, b, 0:256], gw2[:, 128 * c:128 * c + 128], glr[0:16, :], True, True,
                          gl[0], bank_free[b], l_gw2, l_tbl)
                i = act(bf[:, 256 * c:256 * c + 256], PS[:, b, 0:256], ACT.Identity, last, bias=P("gb", c))
                bank_free[b] = i
                x_in.append(i)
            i_abs = act(w0, bf, ACT.Abs, x_in)
            i_e1 = act(w1, w0, ACT.Exp, i_abs, scale=-1.0)
            i_l1 = act(w1, w1, ACT.Ln, i_e1, bias=onet)
            i_L = stt(bf, bf, 0.0, w1, MIN, SUB, i_l1)
            for c in range(2):
                sc = ve(lambda e, c=c: e.tensor_tensor_scan(w0[:, 256 * c:256 * c + 256], C("reset"),
                                                            bf[:, 256 * c:256 * c + 256], 0.0, MUL, ADD), i_L)
            i_b = ts(bf, w0, 1.0 / 16.0, MUL, sc)
            qf, kf = qkf[:, 0:512], qkf[:, 512:1024]
            level = {}
            for lv in range(6, 0, -1):
                g = 1 << lv
                h = g // 2
                bg = bf.rearrange("p (n t) -> p n t", t=g)
                ref = bg[:, :, h - 1:h].broadcast_to([128, 512 // g, h])
                qs, ks = (a[lv - 1].rearrange("p (n t) -> p n t", t=g)[:, :, h:g] for a in (qlb, klb))
                ks = klb[lv - 1].rearrange("p (n t) -> p n t", t=g)[:, :, 0:h]
                d0 = tt(qs, bg[:, :, h:g], ref, SUB, i_b, zl)
                d1 = tt(ks, ref, bg[:, :, 0:h], SUB)
                e0 = act(qs, qs, ACT.Exp, d0)
                e1 = act(ks, ks, ACT.Exp, d1)
                level[lv] = [qs, ks, e0, e1]
            b4 = bf.rearrange("p (n t) -> p n t", t=64)
            i_dd = tt(w2.rearrange("p (n t) -> p n t", t=64), b4[:, :, 63:64].broadcast_to([128, 8, 64]), b4, SUB, i_b)
            i_eb = act(w1, bf, ACT.Exp, i_b)
            i_ed = act(w2, w2, ACT.Exp, i_dd)
            i_dl = act(dl.rearrange("p (n t) -> p n t", t=1), b4[:, :, 63:64], ACT.Exp, i_b)
            for lv in range(6, 0, -1):
                g = 1 << lv
                h = g // 2
                qs, ks, e0, e1 = level[lv]
                i0 = tt(qs, qf.rearrange("p (n t) -> p n t", t=g)[:, :, h:g], qs, MUL, e0, qks)
                i1 = tt(ks, kf.rearrange("p (n t) -> p n t", t=g)[:, :, 0:h], ks, MUL, e1, qks)
                level[lv] = [i0, i1]
            i_qd = tt(qd, qf, w1, MUL, i_eb, qks)
            i_kd = tt(kd, kf, w2, MUL, i_ed, qks)

            gates, us, vs, rs = [], [], [], []
            lin_T("ev_in", 2, hT, 8, lambda j, ps, last: gates.append(
                act(gate[:, j, :], ps, ACT.Sigmoid, last)) or gates[-1])
            lin_T("ev_in", 3, hT, 8, lambda j, ps, last: us.append(
                tt(up[:, j, 30:286], ps, gate[:, j, :], MUL, last, gates[j], zups)) or us[-1])
            conv = [None] * 4

            def taps():
                for w in range(31):
                    for c in range(4):
                        if w == 0:
                            conv[c] = ts(y[:, c, :], up[:, c, 0:256], P("cw", c), MUL, us[c], s2=P("cb", c), op1=ADD)
                        else:
                            conv[c] = stt(y[:, c, :], up[:, c, w:w + 256], P("cw", 4 * w + c), y[:, c, :], MUL, ADD, conv[c])
                        yield conv[c]

            taps = Filler(taps())
            copied = {}
            for lv in range(7):
                qs, ks, dep = (qf, kf, qks) if lv == 0 else (qlb[lv - 1], klb[lv - 1], level[lv])
                qv, kv = chunks(qs, 2), chunks(ks, 2)
                b = 2 * (lv % 4)
                for par in range(2):
                    rows_ = slice(64 * par, 64 * par + 64)
                    for cp in range(2):
                        for hh in range(2):
                            n = 2 * cp + hh
                            last = mm(PS[:, b + par, 128 * n:128 * n + 128], kv[rows_, hh, 128 * cp:128 * cp + 128],
                                      qv[rows_, hh, 128 * cp:128 * cp + 128], True, True,
                                      *([dep, bank_free[b], bank_free[b + 1]] if not (par or n) else []))
                for half in range(2):
                    rows_ = slice(64 * half, 64 * half + 64)
                    mask = C("gm")[rows_, 64 * lv:64 * lv + 64].rearrange("p (o t) -> p o t", o=1)
                    for par in range(2):
                        src = PS[rows_, b + par, :].rearrange("p (n t) -> p n t", n=4)[:, :, 64 * half:64 * half + 64]
                        dst = At[rows_, par, :, 64 * half:64 * half + 64]
                        m = ve(lambda e, dst=dst, src=src, mask=mask: e.copy_predicated(
                            dst, mask.bitcast(U32).broadcast_to([64, 4, 64]), src), last, copied.get((par, half), zA))
                        copied[par, half] = m
                bank_free[b] = bank_free[b + 1] = m
                taps.step(4)
            for c in range(2):
                for t in range(2):
                    b = next_bank(range(8))
                    last = transpose(PS[:, b, 0:128], kd[:, 256 * c + 128 * t:256 * c + 128 * t + 128], i_kd, bank_free[b])
                    i_kr = act(kdrow[:, t, 128 * c:128 * c + 128], PS[:, b, 0:128], ACT.Copy, last)
                    bank_free[b] = i_kr
            rows("ev_in", 4, lambda t, ps, last: vs.append(act(vrow[:, t, :], ps, ACT.Copy, last)) or vs[-1])
            ub = {0: 4, 1: 5, 2: 6}
            uins = []
            for n in range(3):
                rows_ = slice(64 * (n % 2), 64 * (n % 2) + 64)
                for h in range(4):
                    last = mm(PS[64 * (h % 2):64 * (h % 2) + 64, ub[n], 128 * (h // 2):128 * (h // 2) + 128],
                              kdrow[rows_, n // 2, 64 * h:64 * h + 64], vrow[rows_, n // 2, 128 * h:128 * h + 128],
                              True, True, *([i_kr, bank_free[ub[n]], vs] if h == 0 else []))
                uins.append(last)
            lin_T("ev_in", 5, hT, 8, lambda j, ps, last: rs.append(act(rT[:, j, :], ps, ACT.Silu, last)) or rs[-1],
                  banks=(0, 1, 2, 3))
            taps.step(48)
            s_prev = zS
            for n in range(3):
                for c in range(2):
                    s_new = stt(St[:, n + 1, c, :], St[:, n, c, :], dl[:, 4 * c + n:4 * c + n + 1],
                                PS[:, ub[n], 128 * c:128 * c + 128], MUL, ADD, uins[n], i_dl, s_prev)
                s_prev = s_new
                bank_free[ub[n]] = s_new
            qdv = chunks(qd, 2)
            for par in range(2):
                rows_ = slice(64 * par, 64 * par + 64)
                b = 6 + par
                for hh in range(2):
                    for n in range(4):
                        last = mm(PS[:, b, 256 * hh + 64 * n:256 * hh + 64 * n + 64], St[rows_, n, hh, :],
                                  qdv[rows_, hh, 64 * n:64 * n + 64], hh == 0 and n == 0, False,
                                  *([s_prev, i_qd, bank_free[b]] if not (hh or n) else []), skip=True)
                for hh in range(2):
                    for cp in range(2):
                        h = 2 * hh + par
                        last = mm(PS[:, b, 256 * hh + 128 * cp:256 * hh + 128 * cp + 128],
                                  vrow[:, cp, 128 * h:128 * h + 128], At[:, par, 2 * cp + hh, :], False, True,
                                  *([copied[par, 0], copied[par, 1], vs] if not (hh or cp) else []), skip=True)
                i_o = act(of.rearrange("p (hh par t) -> p par hh t", hh=2, par=2)[:, par, :, :],
                          PS[:, b, :].rearrange("p (hh t) -> p hh t", hh=2), ACT.Copy, last)
                bank_free[b] = i_o
            taps.drain()
            i_sq = act(o2, of, ACT.Square, i_o)
            done = []
            for i in range(2):
                last = mm(PS[:, 4 + i, :], ones, o2[:, 512 * i:512 * i + 512], True, True, i_sq, bank_free[4 + i])
            for i in range(2):
                bank_free[4 + i] = act(o2[:, 512 * i:512 * i + 512], PS[:, 4 + i, :], ACT.Ln, last, scale=1.0 / 128, bias=epst)
                done.append(bank_free[4 + i])
            i_r = act(o2, o2, ACT.Exp, done, scale=-0.5)
            i_n = stt(of, of, P("glag", 0), o2, MUL, MUL, i_r)
            i_yb = tt(yTf[:, 1024:2048], of, rTf, MUL, i_n, rs)
            mean4 = mean.rearrange("p (o t) -> p o t", o=1).broadcast_to([128, 4, 256])
            for c in range(4):
                last = mm(PS[:, 2, 0:256], ones, y[:, c, :], c == 0, c == 3, conv[c], *([bank_free[2]] if c == 0 else []))
            i_m = act(mean, PS[:, 2, 0:256], ACT.Copy, last, scale=1.0 / 512)
            bank_free[2] = i_m
            i_xc = tt(y, y, mean4, SUB, i_m, last)
            i_s = act(ysq, yf, ACT.Square, i_xc)
            for c in range(4):
                last = mm(PS[:, 3, 0:256], ones, ysq[:, 256 * c:256 * c + 256], c == 0, c == 3,
                          *([i_s, bank_free[3]] if c == 0 else []))
            i_r = act(mean, PS[:, 3, 0:256], ACT.Ln, last, i_xc, scale=1.0 / 512, bias=epst)
            bank_free[3] = i_r
            i_r = act(mean, mean, ACT.Exp, i_r, scale=-0.5)
            i_xn = tt(y, y, mean4, MUL, i_r)
            ya = []
            for c in range(4):
                ya.append(act(yT[:, c, :], y[:, c, :], ACT.Silu, i_xn, scale=P("lng", c), bias=P("lnb", c)))
            loads = [load("ev_out", p) for p in range(2)]
            for half in (1, 0):
                for n in range(8):
                    slot, w, arrived = loads[n // 4]
                    wv = chunks(w, 8)
                    for k in range(4 * half, 4 * half + 4):
                        last = mm(PS[:, n, 0:256], wv[:, k, 128 * (n % 4):128 * (n % 4) + 128], yT[:, k, :],
                                  k == 4, k == 3, *([arrived, bank_free[n], i_yb] if k == 4 else []),
                                  *([ya[k]] if half == 0 else []))
                    if half == 0:
                        bank_free[n] = state["x"][n] = tt(xT[:, n, :], PS[:, n, 0:256], xT[:, n, :], ADD, last)
            for slot, _, _ in loads:
                release(slot, last)

        def peer_layer(layer):
            start = phase()
            if layer == 0:
                sring["free"] = [start, start]
            at = {"o": 0}

            def take(n):
                at["o"] += n
                return arena[:, at["o"] - n:at["o"]]

            av = mem[:, 0:32768].rearrange("p (j t) -> p j t", j=128)
            A0 = 32768 - 3 * WSLOT
            LATE = 4096 + 6 * 256 + 1500
            at["o"] = A0 - LATE - 4096
            keysb = take(2048)
            qTb = [take(1024).rearrange("p (c t) -> p c t", c=4) for _ in range(2)]
            late = at["o"]
            j_early, j_late = (3 * WSLOT + late - 4096) // 256, (3 * WSLOT + late) // 256
            scores = take(4096).rearrange("p (t h n) -> p t h n", t=2, h=16)
            SC, EF, GT, E1, E2 = (take(256) for _ in range(5))
            EI = arena_u[:, at["o"]:at["o"] + 256]
            take(256)
            s2 = take(128)
            cand, cand2, ecand = (take(NP + 2)[:, 0:NP] for _ in range(3))
            hot = take(16 * NP)
            v16 = take(32)
            i16 = arena_u[:, at["o"]:at["o"] + 32]
            take(32)
            f16 = take(32)
            p16 = arena_u[:, at["o"]:at["o"] + 16]
            take(16)
            p16f = take(16)
            st = take(16)
            assert at["o"] <= A0, at["o"]
            at["o"] = A0
            cbuf = take(1536)
            assert at["o"] <= AR, at["o"]
            eT = [cbuf[:, 256 * i:256 * i + 256] for i in range(4)]
            CS = [(cbuf[:, 512 * i:512 * i + 256], cbuf[:, 512 * i + 256:512 * i + 512]) for i in range(3)]
            rounded(*[x for pair in CS for x in pair])
            raw = [wring[0][:, 1024 * i:1024 * i + 1024] for i in range(4)]

            h_ok = rms_T(lambda c: P(f"f{layer}", c), READY)
            sc_ok = {}
            qT_use = [None, None]

            def queries(p):
                def evict(j, ps, last):
                    qs[p].append(act(qTb[p % 2][:, j, :], ps, ACT.Copy, last, qT_use[p % 2], *start))
                    if j == 3 and p >= 1:
                        score(p - 1)
                    return qs[p][-1]
                return tiles_T(f"wq{layer}", p, H3, 8, evict, h_ok, banks=(0, 1, 2, 3))

            def score(p):
                for t in range(2):
                    b = next_bank((4, 5, 6, 7))
                    for j in range(4):
                        last = mm(PS[:, b, 128 * j:128 * j + 128], qTb[p % 2][:, j, 128 * t:128 * t + 128],
                                  keys[:, 4 * p + j, :], True, True, *([qs[p][3], karr, bank_free[b]] if j == 0 else []))
                    i = act(scores[:, t, 4 * p:4 * p + 4, :].rearrange("p h n -> p (h n)"), PS[:, b, :], ACT.Copy, last, *start)
                    bank_free[b] = i
                    sc_ok[t, 2 * p] = sc_ok[t, 2 * p + 1] = i
                qT_use[p % 2] = last
                return last

            qs = [[] for _ in range(4)]
            karr = sp(lambda e: e.dma_start(keysb[:, :], io[f"keys{layer}"].rearrange("(p f) -> p f", p=128)), *start, dma=s_key)
            keys = keysb.rearrange("p (h n) -> p h n", h=16)
            lin(*[queries(p) for p in range(4)])
            ring_was = list(ring["free"])

            n_raw = {"n": 0}
            raw_free = [ring_was[0]] * 4

            def tile(table, j):
                n = n_raw["n"]
                n_raw["n"] += 1
                r = raw[n % 4]
                src = io[f"{table}{layer}"][131072 * j:131072 * j + 131072].rearrange("(p f) -> p f", p=128)
                arrived = sp(lambda e: e.dma_start(r, src), raw_free[n % 4], dma=gsem[n % 4])
                got = split(r.rearrange("p (c e) -> p c e", c=8), arrived, *start)
                raw_free[n % 4] = got[4]
                return got

            def topk(t, h):
                sc16, ef = SC[:, 128 * t + 16 * h:128 * t + 16 * h + 16], EF[:, 128 * t + 16 * h:128 * t + 16 * h + 16]
                first = [sc_ok[t, h], *start]
                for side in range(2):
                    s = scores[:, t, 2 * h + side, :]
                    va, vb = v16[:, 16 * side:16 * side + 8], v16[:, 16 * side + 8:16 * side + 16]
                    ia, ib = i16[:, 16 * side:16 * side + 8], i16[:, 16 * side + 8:16 * side + 16]
                    a = ve(lambda e, va=va, s=s: e.max(va, s), *(first if side == 0 else []))
                    a = ve(lambda e, va=va, s=s: e.match_replace(s2, va, s, -3e38), a)
                    ve(lambda e, ia=ia, va=va, s=s: e.max_index(ia, va, s))
                    a = ve(lambda e, vb=vb: e.max(vb, s2), a)
                    a = ve(lambda e, ib=ib, vb=vb: e.max_index(ib, vb, s2), a)
                    yield a
                a = vcopy(f16, i16, a)
                a = ts(f16[:, 0:16], f16[:, 0:16], 128.0, MUL, a)
                off = 0
                for i0, i1, n in ((0, 1, 16), (1, 2, 8), (2, 3, 5), (3, 4, 4), (4, 5, 3), (5, 8, 2), (8, 16, 1)):
                    m = i1 - i0
                    for dst, src in ((cand, v16), (ecand, f16)):
                        dv = dst[:, off:off + m * n].rearrange("p (i j) -> p i j", i=m)
                        x = src[:, i0:i1].rearrange("p (i o) -> p i o", o=1).broadcast_to([128, m, n])
                        yy = src[:, 16:16 + n].rearrange("p (o j) -> p o j", o=1).broadcast_to([128, m, n])
                        c = tt(dv, x, yy, ADD, a)
                    off += m * n
                yield c
                a = ve(lambda e: e.max(sc16[:, 0:8], cand), c)
                a = ve(lambda e: e.match_replace(cand2, sc16[:, 0:8], cand, -3e38), a)
                ve(lambda e: e.max_index(p16[:, 0:8], sc16[:, 0:8], cand))
                a = ve(lambda e: e.max(sc16[:, 8:16], cand2), a)
                a = ve(lambda e: e.max_index(p16[:, 8:16], sc16[:, 8:16], cand2), a)
                a = vcopy(p16f, p16, a)
                yield a
                hv = hot.rearrange("p (k c) -> p k c", k=16)
                a = tt(hv, p16f.rearrange("p (k o) -> p k o", o=1).broadcast_to([128, 16, NP]),
                       C("iota")[:, 0:NP].rearrange("p (o c) -> p o c", o=1).broadcast_to([128, 16, NP]), EQ, a)
                yield a
                a = tt(hv, hv, ecand.rearrange("p (o c) -> p o c", o=1).broadcast_to([128, 16, NP]), MUL, a)
                yield a
                yield red(ef, hv, ADD, a)

            e_ok = []

            def choices():
                for t in range(2):
                    for h in range(8):
                        for a in topk(t, h):
                            yield a
                    w = slice(128 * t, 128 * t + 128)
                    g = GT[:, w].rearrange("p (h k) -> p h k", h=8)
                    s = SC[:, w].rearrange("p (h k) -> p h k", h=8)
                    st8 = st[:, 0:8].rearrange("p (h o) -> p h o", o=1)
                    x = tt(g, s, s[:, :, 0:1].broadcast_to([128, 8, 16]), SUB, a)
                    x = act(GT[:, w], GT[:, w], ACT.Exp, x)
                    a = vcopy(EI[:, w], EF[:, w], a)
                    b1 = ts(E2[:, w].bitcast(U32), EI[:, w], 127, ALU.bitwise_and, a)
                    b2 = ts(E1[:, w].bitcast(U32), EI[:, w], 7, ALU.logical_shift_right, a)
                    b1 = vcopy(E2[:, w], E2[:, w].bitcast(U32), b1)
                    b2 = vcopy(E1[:, w], E1[:, w].bitcast(U32), b2)
                    yield b2
                    a = red(st[:, 0:8], g, ADD, x)
                    a = recip(st[:, 8:16], st[:, 0:8], a)
                    a = tt(g, g, st[:, 8:16].rearrange("p (h o) -> p h o", o=1).broadcast_to([128, 8, 16]), MUL, a)
                    yield a
                    yield a
                    b = next_bank((0, 1, 2, 3))
                    for i, m in enumerate((E1, E2, GT)):
                        last = transpose(PS[:, b, 128 * i:128 * i + 128], m[:, w], a, bank_free[b])
                    for i in range(3):
                        bank_free[b] = act(eT[i][:, w], PS[:, b, 128 * i:128 * i + 128], ACT.Copy, last, *start)
                    bank_free[b] = act(eT[3][:, w], PS[:, b, 0:128], ACT.Copy, last, *start, scale=-1.0)
                    e_ok.append(bank_free[b])
                    yield last

            picks = Filler(choices())
            cur = tile("u", 0)
            q_done = score(3)
            gelu = None
            for j in range(128):
                nxt = tile("u" if j < 127 else "v", (j + 1) % 128)
                picks.step(2 if j % 4 == 3 else 1)
                if j == j_late - 2:
                    picks.drain()
                sl, hi, lo, i_h, i_l = cur
                b = next_bank((0, 1, 2, 3))
                out = PS[:, b, 0:256]
                last = mm3(out, hi, lo, hhiv, hlov, i_h, i_l, True, True, bank_free[b])
                sring["free"][sl] = last
                before = [ring_was[1 + j // 16]] if j < 48 else [q_done] if j < j_late else [e_ok]
                assert j < j_early or j >= 48
                gelu = act(av[:, j, :], out, ACT.Gelu, last, before, *start)
                bank_free[b] = gelu
                cur = nxt
            state["hT"] = last

            oneA = hhi.rearrange("p (n e) -> p n e", n=16)
            oneB = hTt[:, :].rearrange("p (n e) -> p n e", n=16)
            iota = C("iota")
            prod = {}

            def one_hots(g):
                s = 4 * (g % 4)
                w = [e_ok, last, prod.get(g - 4)]
                done = []
                for i in range(4):
                    n, o = 4 * g + i, oneA[:, s + i, :]
                    if i == 0 and g % 2:
                        done.append(ve(lambda e, n=n, o=o: e.tensor_scalar(o, iota, eT[0][:, n:n + 1], eT[2][:, n:n + 1], EQ, MUL), *w))
                    elif i <= 1:
                        done.append(po(lambda e, n=n, o=o: e.tensor_scalar(o, iota, eT[0][:, n:n + 1], eT[2][:, n:n + 1], EQ, MUL), *w))
                    else:
                        x = act(o, iota, ACT.Abs, *w, bias=eT[3][:, n:n + 1])
                        done.append(act(o, o, ACT.Relu, x, scale=-2.0, bias=eT[2][:, n:n + 1]))
                done.append(tt(oneB[:, s:s + 4, :], iota.rearrange("p (o e) -> p o e", o=1).broadcast_to([128, 4, 128]),
                               eT[1][:, 4 * g:4 * g + 4].rearrange("p (t o) -> p t o", o=1).broadcast_to([128, 4, 128]), EQ, *w))
                return done

            hots = [one_hots(g) for g in range(2)]
            for g in range(64):
                b = next_bank((0, 1, 2, 3))
                for i in range(4):
                    prod[g] = mm(PS[:, b, 128 * i:128 * i + 128], oneA[:, 4 * (g % 4) + i, :], oneB[:, 4 * (g % 4) + i, :],
                                 True, True, *([hots[g], bank_free[b]] if i == 0 else []))
                if g < 62:
                    hots.append(one_hots(g + 2))
                m = av[:, :, 4 * g:4 * g + 4]
                a_ok = bank_free[b] = tt(m, m, PS[:, b, :].rearrange("p (t j) -> p j t", t=4), MUL, prod[g], gelu)

            state["hT"] = prod[63]

            c_free, freed = [None] * 3, {}

            def coef(j):
                hi, lo = CS[j % 3]
                i_h = act(R(hi), av[:, j, :], ACT.Copy, a_ok, c_free[j % 3])
                freed[j] = tt(R(lo), av[:, j, :], RF(hi), SUB, i_h)
                return R(hi), R(lo), i_h, freed[j]

            ada_sum, ada_got = small[:, 0:512], {"use": state["barrier"], "sum": None}

            def modulation(j):
                piece, i = (j - 4) // 10, (j - 4) % 10
                if j < 4 or piece >= 12 or i % 2:
                    return
                q = i // 2
                if q < 4:
                    n = n_raw["n"]
                    n_raw["n"] += 1
                    r = raw[n % 4]
                    p0, w = flat(WEIGHTS["ada"])[0][piece]
                    src = io["ada"][p0:p0 + 128 * w].rearrange("(p f) -> p f", p=128)[:, 1024 * q:1024 * q + 1024]
                    arrived = sp(lambda e: e.dma_start(r, src), raw_free[n % 4], dma=gsem[n % 4])
                    k = 2 * q
                    if q == 0:
                        a = ts(ada_sum, r[:, 0:512], cs[:, 0:1], MUL, arrived, state["cs"], ada_got["use"])
                    else:
                        a = stt(ada_sum, r[:, 0:512], cs[:, k:k + 1], ada_sum, MUL, ADD, arrived, ada_got["sum"])
                    ada_got["sum"] = raw_free[n % 4] = stt(ada_sum, r[:, 512:1024], cs[:, k + 1:k + 2], ada_sum, MUL, ADD, a)
                else:
                    b = next_bank((0, 1, 2, 3))
                    for m in range(4):
                        last = mm(PS[:, b, m:m + 1], ada_sum[:, 128 * m:128 * m + 128], ones[:, 0:1], True, True,
                                  *([ada_got["sum"], bank_free[b]] if m == 0 else []))
                    ada_got["use"] = last
                    bank_free[b] = state["mod"] = tt(mod[:, 4 * piece:4 * piece + 4], PS[:, b, 0:4],
                                                     P("adab")[:, 4 * piece:4 * piece + 4], ADD, last)

            ccur = coef(0)
            for j in range(128):
                if j < 127:
                    cnxt, nxt = coef(j + 1), tile("v", j + 1)
                sl, hi, lo, i_h, i_l = cur
                chi, clo, j_h, j_l = ccur
                outs = [PS[:, 4 + c // 2, 256 * (c % 2):256 * (c % 2) + 256] for c in range(8)]
                for c in range(8):
                    mm(outs[c], hi[:, c, :], chi, j == 0 and c % 2 == 0, False,
                       *([i_h, j_h] + [bank_free[4 + i] for i in range(4) if j == 0] if c == 0 else []), skip=True)
                    mm(outs[c], hi[:, c, :], clo, False, False, *([j_l] if c == 0 else []), skip=True)
                for c in range(8):
                    last = mm(outs[c], lo[:, c, :], chi, False, j == 127, *([i_l] if c == 0 else []), skip=True)
                sring["free"][sl] = c_free[j % 3] = last
                if layer == 0:
                    modulation(j)
                cur, ccur = nxt, cnxt
            for c in range(8):
                state["x"][c] = tt(xT[:, c, :], PS[:, 4 + c // 2, 256 * (c % 2):256 * (c % 2) + 256], xT[:, c, :], ADD, last)
                bank_free[4 + c // 2] = state["x"][c]
            ring["free"] = [raw_free] + [freed[16 * i + 15] for i in range(3)]
            ring["n"] = 1

        def softmax_pv(items, logits, bias, v_of, out_of, mult, L, PT, sm, deps, extra, fill):
            n = len(items)
            lg, ex, pn, tr, pt, l_use, pt_use = {}, {}, {}, {}, {}, {}, {}
            filler, rate = fill
            nb = len(L)

            def stage_a(i):
                b = i % 2
                lg[i] = logits(items[i], PS[:, b, 0:256], PS[:, b, 256:384], [deps, bank_free[b]])
                l, s = L[i % nb], sm[i % nb]
                a = tt(l, PS[:, b, 0:384], bias(items[i]), ADD, lg[i], l_use.get(i - nb))
                bank_free[b] = a
                m1 = red(s[:, 0:1], l[:, 0:256], MAX, a, negate=True)
                m0 = red(s[:, 1:2], l[:, 256:384], MAX, a, negate=True)
                act(l[:, 0:256], l[:, 0:256], ACT.Exp, m0, bias=s[:, 0:1], accum_out=s[:, 2:3])
                ex[i] = act(l[:, 256:384], l[:, 256:384], ACT.Exp, m0, bias=s[:, 1:2], accum_out=s[:, 3:4])

            def scale(i):
                l, s = L[i % nb], sm[i % nb]
                a = recip(s[:, 4:6], s[:, 2:4], ex[i])
                if mult is not None:
                    a = tt(s[:, 4:6], s[:, 4:6], mult(items[i]), MUL, a)
                ts(l[:, 0:256], l[:, 0:256], s[:, 4:5], MUL, a)
                pn[i] = ts(l[:, 256:384], l[:, 256:384], s[:, 5:6], MUL, a)

            def stage_b(i):
                l = L[i % nb]
                b = 2 + i % 2
                transpose(PS[:, b, 0:128], l[:, 256:384], pn[i], bank_free[b])
                transpose(PS[:, b, 128:256], l[:, 0:128])
                l_use[i] = tr[i] = transpose(PS[:, b, 256:384], l[:, 128:256])
                p = PT[i % 2]
                pt[i] = act(p, PS[:, b, 0:384], ACT.Copy, tr[i], pt_use.get(i - 2))
                bank_free[b] = pt[i]

            def stage_c(i):
                p = PT[i % 2]
                out, first, stop, waits = out_of(i, items[i])
                mm(out[:, 0:256], v_of(items[i], 0), p[:, 0:256], first, False, pt[i], waits, skip=True)
                pt_use[i] = mm(out[:, 128:256], v_of(items[i], 1), p[:, 256:384], False, stop, skip=True)
                extra(i, items[i], out, pt_use[i])

            for i in range(n + 3):
                if 2 <= i < n + 2:
                    scale(i - 2)
                if i < n:
                    stage_a(i)
                filler.step(rate)
                if 2 <= i < n + 2:
                    stage_b(i - 2)
                if i >= 3:
                    stage_c(i - 3)

        def head_norm(src, n, gcol, sq, r, deps, banks):
            w = n * 256
            i_sq = act(sq[:, 0:w], src, ACT.Square, deps)
            done = []
            for i in range(0, w, 512):
                m = min(512, w - i)
                b = next_bank(banks)
                last = mm(PS[:, b, 0:m], C("bd64"), sq[:, i:i + m], True, True, i_sq, bank_free[b])
                bank_free[b] = act(r[:, i:i + m], PS[:, b, 0:m], ACT.Ln, last, scale=1.0 / 64, bias=epst)
                done.append(bank_free[b])
            a = act(r[:, 0:w], r[:, 0:w], ACT.Exp, done, scale=-0.5)
            return stt(src, src, gcol, r[:, 0:w], MUL, MUL, a)

        def odd_layer():
            start = phase()
            o = 0

            def take(n):
                nonlocal o
                o += n
                return arena[:, o - n:o]

            qf, kf = take(2048), take(2048)
            q, k = (a.rearrange("p (c t) -> p c t", c=8) for a in (qf, kf))
            v = take(2048).rearrange("p (t n) -> p t n", t=2)
            oTf = take(2048)
            rounded(oTf)
            oT = oTf.rearrange("p (c t) -> p c t", c=8)
            sqk, rk, sq, r = (take(1024) for _ in range(4))
            L = [take(384) for _ in range(3)]
            PT = [take(384) for _ in range(2)]
            sm = [take(8) for _ in range(3)]
            fz, f1, f2 = take(256), take(256), take(256)
            qg = take(1)
            assert o <= AR, o
            zf = po(lambda e: e.memset(fz, 0.0), *start)
            h_ok = rms_T(lambda c: P("od_g", c))
            i_qg = ts(qg, P("qg", 0), 0.125, MUL, *start)
            dq, dk, dv, df = [], [], [], []

            def ev(dst, p, done):
                return lambda j, ps, last: done.append(act(dst[:, 4 * p + j, :], ps, ACT.Copy, last, *start)) or done[-1]

            def proj(p, **kw):
                yield from tiles_T("od_in", 4 * p, H3, 8, ev(q, p, dq), h_ok, **kw)
                if p == 0:
                    yield from tiles_T("od_in", 1, H3, 8, lambda j, ps, last: df.append(
                        act(fz[0:16, :], ps, ACT.Identity, last, zf, bias=P("fb", 0)[0:16, :])) or df[-1], **kw)
                yield from tiles_T("od_in", 2 + 3 * p, H3, 8, ev(k, p, dk), **kw)
                yield from rows_T("od_in", 3 + 3 * p, lambda t, ps, last: dv.append(
                    act(v[:, t, 512 * p:512 * p + 512], ps, ACT.Copy, last, *start)) or dv[-1], **kw)

            lin(proj(0))
            z16 = fz[0:16, :]
            a = act(f1[0:16, :], z16, ACT.Abs, df)
            a = act(f1[0:16, :], f1[0:16, :], ACT.Exp, a, scale=-1.0)
            a = act(f1[0:16, :], f1[0:16, :], ACT.Ln, a, bias=onet[0:16, :])
            a = stt(f2[0:16, :], z16, 0.0, f1[0:16, :], MIN, SUB, a)
            a = ts(f2[0:16, :], f2[0:16, :], -1.0, MUL, a)
            i_c = ve(lambda e: e.tensor_tensor_scan(z16, C("ones", 16)[:, 0:1].broadcast_to([16, 256]),
                                                    f2[0:16, :], 0.0, MUL, ADD), a)
            o_done = []

            def logits(h, t1, t0, waits):
                rows_ = slice(64 * (h % 2), 64 * (h % 2) + 64)
                c = h // 2
                pick = ident[:, h:h + 1].broadcast_to([128, 128])
                mm(t1, q[rows_, c, 128:256], k[rows_, c, :], True, False, waits, skip=True)
                mm(t1, pick, fz, False, True, skip=True)
                mm(t0, q[rows_, c, 0:128], k[rows_, c, 0:128], False, False, skip=True)
                return mm(t0, pick, fz[:, 0:128], False, True, skip=True)

            def out_of(i, h):
                b = 4 + (h // 2) % 2
                return (PS[64 * (h % 2):64 * (h % 2) + 64, b, 0:256], True, True, [bank_free[b]])

            def extra(i, h, out, last):
                if h % 2:
                    b = 4 + (h // 2) % 2
                    bank_free[b] = act(oT[:, h // 2, :], PS[:, b, 0:256], ACT.Copy, last, *start)
                    o_done.append(bank_free[b])

            fill = Filler(stream(proj(1, banks=(6, 7))))
            for p in range(2):
                w = slice(1024 * p, 1024 * p + 1024)
                nq = head_norm(qf[:, w], 4, qg, sq, r, [dq, i_qg, *start], range(8))
                fill.step(2)
                nk = head_norm(kf[:, w], 4, P("kg", 0), sqk, rk, [dk, *start], range(8))
                softmax_pv(list(range(8 * p, 8 * p + 8)), logits, lambda h: C("fmask"),
                           lambda h, st: v[:, st, 64 * h:64 * h + 64], out_of, None, L, PT, sm,
                           [nq, nk, i_c, dv, *start], extra, (fill, 1))
                fill.drain()
            o_ok = [parts_of(oT[:, c, :], hhi[:, 256 * c:256 * c + 256], o_done[c], state["hT"]) for c in range(8)]
            state["hT"] = residual("od_out", (hhiv, R(oT)), 8, o_ok)

        def last_block():
            start = phase()
            o = 0

            def take(n):
                nonlocal o
                o += n
                return arena[:, o - n:o]

            gs1, gs2 = take(8), take(8)
            B = take(8 * 384).rearrange("p (h n) -> p h n", h=8)
            qaf = take(1024)
            qa = qaf.rearrange("p (c t) -> p c t", c=4)
            kvT = take(1024).rearrange("p (c t) -> p c t", c=4)
            kvTf = arena[:, o - 1024:o]
            vnsa = take(512).rearrange("p (t n) -> p t n", t=2)
            ga = take(48).rearrange("p (t n) -> p t n", t=2)
            qb = take(1024).rearrange("p (c t) -> p c t", c=4)
            kb = take(1024).rearrange("p (c t) -> p c t", c=4)
            vb = take(1024).rearrange("p (t n) -> p t n", t=2)
            onsaf = take(1024)
            onsa = onsaf.rearrange("p (c t) -> p c t", c=4)
            osbf = take(1024)
            osb = osbf.rearrange("p (c t) -> p c t", c=4)
            ma_f, mb_f = take(2048), take(2048)
            ma, mb = (a.rearrange("p (c t) -> p c t", c=8) for a in (ma_f, mb_f))
            sq, r = take(2048), take(1536)
            L = [take(384) for _ in range(3)]
            PT = [take(384) for _ in range(2)]
            sm = [take(8) for _ in range(3)]
            Fv = L[0]
            blk = osbf[:, 0:960].rearrange("p (a i c) -> p a i c", a=2, i=32)
            hid15 = PT[0][:, 0:256]
            hid = take(32)
            kcT = take(16)
            hrep = take(128)
            vblk = take(512).rearrange("p (k g d) -> p k g d", k=2, g=4)
            Lc = r[:, 384:640].rearrange("p (k t g c) -> p k t g c", k=2, t=2, g=4)
            BC = r[:, 640:896].rearrange("p (k t g c) -> p k t g c", k=2, t=2, g=4)
            Pc = r[:, 896:1408].rearrange("p (k t g c) -> p k t g c", k=2, t=2, g=4)
            PcT = take(512).rearrange("p (k t n) -> p k t n", k=2, t=2)
            cm = take(48)
            qg = take(1)
            assert o <= AR, o

            i_g = stt(gs1, mod[:, 8:16], 1.0, P("n1"), ADD, MUL, state["mod"], *start)
            i_g2 = stt(gs2, mod[:, 32:40], 1.0, P("n2"), ADD, MUL)
            i_t = vcopy(tbl[32:33, :], C("negrow", 33)[32:33, :], *start)
            last = mm(PS[0:8, 6, 0:384], tbl, C("hot", 33), True, True, i_t, bank_free[6], *READY)
            i_F = act(Fv[0:8, :], PS[0:8, 6, 0:384], ACT.Copy, last, *start)
            bank_free[6] = i_F
            d_w = sp(lambda e: e.dma_start(io["fd"].rearrange("(h n) -> h n", h=8), Fv[0:8, :]), i_F, dma=s_bw)
            src = bass.AP(io["fd_t"], 0, [[1, 128], [384, 8], [1, 256]])
            d_r1 = sp(lambda e: e.dma_start(ma_f.rearrange("p (h n) -> p h n", h=8), src), d_w, *start, dma=s_br)

            u_ok = rms_T(lambda c: gs1[:, c:c + 1], i_g, shift=lambda c: mod[:, c:c + 1])
            i_qg = ts(qg, P("q2", 0), 0.125, MUL, *start)

            def cp(dst, done, *ws, func=ACT.Copy, **kw):
                return lambda j, ps, last: done.append(act(dst(j), ps, func, last, *start, *ws, **kw)) or done[-1]

            dqa, dkv, dvn, dga, dqb, dkb, dvb, dma_, dmb = [], [], [], [], [], [], [], [], []
            def vg(t, ps, last):
                dvn.append(act(vnsa[:, t, :], ps[:, 0:256], ACT.Copy, last, *start))
                dga.append(act(ga[:, t, :], ps[:, 256:280], ACT.Sigmoid, last, *start))
                return dga[-1]

            lin(tiles_T("in2", 1, H3, 8, cp(lambda j: kvT[:, j, :], dkv), u_ok),
                tiles_T("in2", 0, H3, 8, cp(lambda j: qa[:, j, :], dqa)),
                rows_T("in2", 2, vg))
            fb = (6, 7)
            pos = P("pos")
            bl = []
            for a in range(2):
                kview = kvT[:, a, :].rearrange("p (c j) -> p j c", j=16)
                for half in range(2):
                    bl.append(tt(blk[:, a, 16 * half:16 * half + 16, :], kview[:, :, half:half + 15],
                                 pos[:, 16 * half:16 * half + 16].rearrange("p (i o) -> p i o", o=1).broadcast_to([128, 16, 15]),
                                 ADD, dkv, *start))
            hid_ok = []
            for a in range(2):
                slot, w, arr = load("cw1", a)
                wi = w.rearrange("p (i n) -> p i n", i=32)
                for i in range(32):
                    last = mm(PS[0:15, a, 0:128], blk[:, a, i, :], wi[:, i, :], i == 0, i == 31,
                              *([arr, bl, bank_free[a]] if i == 0 else []))
                release(slot, last)
                i_h = act(hid15[0:15, 128 * a:128 * a + 128], PS[0:15, a, 0:128], ACT.Silu, last, *start)
                bank_free[a] = i_h
                hid_ok.append(i_h)
            nq = head_norm(qaf, 4, qg, sq, r, [dqa, i_qg, *start], (2, 3, 4, 5))
            nk1 = head_norm(kvTf[:, 512:768], 1, P("k2", 1), sq[:, 1024:1280], r[:, 1024:1280], [dkv, *start], (2, 3, 4, 5))
            nk2 = head_norm(kvTf[:, 768:1024], 1, P("k2", 2), sq[:, 1280:1536], r[:, 1280:1536], [dkv, *start], (2, 3, 4, 5))
            for p in range(4):
                b = 2 + p
                flipped = mm(PS[:, b, :], C("flip"), ma_f[:, 512 * p:512 * p + 512], True, True, d_r1, bank_free[b])
                i_B = vcopy(B[:, 2 * p:2 * p + 2, 0:256], PS[:, b, :].rearrange("p (h n) -> p h n", h=2), flipped, *start)
                bank_free[b] = i_B
            i_B = vcopy(B[:, :, 256:384], B[:, :, 128:256], i_B)
            fill = Filler(stream(
                tiles_T("in2", 3, H3, 8, cp(lambda j: qb[:, j, :], dqb, scale=0.125), banks=fb),
                tiles_T("in2", 4, H3, 8, cp(lambda j: kb[:, j, :], dkb), banks=fb),
                rows_T("in2", 5, lambda t, ps, last: dvb.append(act(vb[:, t, :], ps, ACT.Copy, last, *start)) or dvb[-1], banks=fb),
                *[tiles_T("in2", 6 + p, H3, 8, cp(lambda j, p=p: ma[:, 4 * p + j, :], dma_, flipped), banks=fb)
                  for p in range(2)],
                *[tiles_T("in2", 8 + p, H3, 8, cp(lambda j, p=p: mb[:, 4 * p + j, :], dmb), banks=fb)
                  for p in range(2)]))
            z = ve(lambda e: e.memset(hid, 0.0), *start)
            hv = hid.rearrange("p (a c) -> p a c", a=2)
            for a in range(2):
                last = mm(PS[:, a, 0:15], hid15[0:15, 128 * a:128 * a + 128], ident[0:15, 0:15], True, True,
                          hid_ok[a], bank_free[a])
                i_h = vcopy(hv[:, a, 0:15], PS[:, a, 0:15], last, z)
                bank_free[a] = i_h
            fill.step(1)
            z = ve(lambda e: e.memset(hrep, 0.0), *start)
            i_hr = vcopy(hrep.rearrange("p (g c) -> p g c", g=4)[:, :, 0:16],
                         hid[:, 16:32].rearrange("p (o c) -> p o c", o=1).broadcast_to([128, 4, 16]), i_h, z)
            z = ve(lambda e: e.memset(vblk, 0.0), *start)
            for hk in range(2):
                rows = slice(64 * hk, 64 * hk + 64)
                l1 = mm(PS[rows, hk, 0:15], P("kw2")[rows, :], hid[rows, 0:15], True, True, i_h, bank_free[hk])
                l2 = mm(PS[:, 2 + hk, 0:64], hrep[rows, :], P("vw2")[rows, :], True, True, i_hr, bank_free[2 + hk])
                i_k = vcopy(kcT[rows, 0:15], PS[rows, hk, 0:15], l1, *start)
                bank_free[hk] = i_k
                for g in range(4):
                    i_v = vcopy(vblk[32 * g:32 * g + 32, hk, g, :], PS[32 * g:32 * g + 32, 2 + hk, 0:64], l2, z)
                bank_free[2 + hk] = i_v
            a = act(cm[:, 0:15], kcT[:, 0:15], ACT.Square, i_k, *start)
            last = mm(PS[:, 0, 0:15], C("bd64"), cm[:, 0:15], True, True, a, bank_free[0])
            a = act(cm[:, 16:31], PS[:, 0, 0:15], ACT.Ln, last, scale=1.0 / 64, bias=epst)
            bank_free[0] = a
            a = act(cm[:, 16:31], cm[:, 16:31], ACT.Exp, a, scale=-0.5)
            fill.step(1)
            i_kc = stt(kcT[:, 0:15], kcT[:, 0:15], P("k2", 0), cm[:, 16:31], MUL, MUL, a)

            cn = C("cneg").rearrange("p (t c) -> p t c", t=2)
            cok = C("cok").rearrange("p (t c) -> p t c", t=2)
            for hk in range(2):
                bh = B[:, 4 * hk:4 * hk + 4, :]
                bi = vcopy(BC[:, hk, 1, :, 0:15], bh[:, :, 31:256:16], i_B)
                for g in range(4):
                    vcopy(BC[:, hk, 0, g, :], cn[:, 0, :])
                bi = vcopy(BC[:, hk, 0, :, 0:6], bh[:, :, 287:287 + 96:16], ve.last)
                bi = vcopy(BC[:, hk, 0, :, 6:7], bh[:, :, 383:384])
            for hk in range(2):
                rows = slice(64 * hk, 64 * hk + 64)
                b = 2 + hk
                for t in range(2):
                    for g in range(4):
                        last = mm(PS[:, b, 64 * t + 16 * g:64 * t + 16 * g + 15], qa[rows, g, 128 * t:128 * t + 128],
                                  kcT[rows, 0:15], True, True, *([nq, i_kc, bank_free[b]] if not (t or g) else []))
            fill.step(5)
            zp = ve(lambda e: e.memset(Pc, 0.0), *start)
            for hk in range(2):
                a = tt(Lc[:, hk, :, :, 0:15].rearrange("p t g c -> p (t g) c"),
                       PS[:, 2 + hk, 0:128].rearrange("p (n c) -> p n c", c=16)[:, :, 0:15],
                       BC[:, hk, :, :, 0:15].rearrange("p t g c -> p (t g) c"), ADD, last, bi)
                bank_free[2 + hk] = a
            L3 = Lc.rearrange("p k t g c -> p (k t g) c")[:, :, 0:15]
            P3 = Pc.rearrange("p k t g c -> p (k t g) c")[:, :, 0:15]
            a = red(cm[:, 0:16], L3, MAX, a)
            a = tt(L3, L3, cm[:, 0:16].rearrange("p (n o) -> p n o", o=1).broadcast_to([128, 16, 15]), SUB, a)
            a = act(L3, L3, ACT.Exp, a)
            for hk in range(2):
                for t in range(2):
                    e1 = tt(Lc[:, hk, t, :, 0:15], Lc[:, hk, t, :, 0:15],
                            cok[:, t:t + 1, 0:15].broadcast_to([128, 4, 15]), MUL, a)
            a = red(cm[:, 0:16], L3, ADD, e1)
            a = ts(cm[:, 0:16], cm[:, 0:16], 1e-30, MAX, a)
            a = recip(cm[:, 16:32], cm[:, 0:16], a)
            g5 = ga.rearrange("p t (h b) -> p t h b", b=3)
            for hk in range(2):
                for t in range(2):
                    n = 8 * hk + 4 * t
                    a2 = tt(cm[:, 16 + n:20 + n], cm[:, 16 + n:20 + n], g5[:, t, 4 * hk:4 * hk + 4, 0], MUL, a, dga)
            i_pc = tt(P3, L3, cm[:, 16:32].rearrange("p (n o) -> p n o", o=1).broadcast_to([128, 16, 15]), MUL, a2, zp)
            for hk in range(2):
                b = 4 + hk
                for t in range(2):
                    last = transpose(PS[:, b, 128 * t:128 * t + 128], Pc[:, hk, t, :, :].rearrange("p g c -> p (g c)"),
                                     i_pc, bank_free[b])
                i_pct = act(PcT[:, hk, :, :].rearrange("p t n -> p (t n)"), PS[:, b, 0:256], ACT.Copy, last, *start)
                bank_free[b] = i_pct

            items = [(c, hk, br) for c in range(4) for br in range(2) for hk in range(2)]

            def logits(it, t1, t0, waits):
                c, hk, br = it
                rows = slice(64 * hk, 64 * hk + 64)
                mm(t1, qa[rows, c, 128:256], kvT[rows, 2 + br, :], True, True, waits, skip=True)
                return mm(t0, qa[rows, c, 0:128], kvT[rows, 2 + br, 0:128], False, True, skip=True)

            def out_of(i, it):
                c, hk, br = it
                b = 4 + c % 2
                return (PS[64 * hk:64 * hk + 64, b, 0:256], br == 0, False, [bank_free[b]])

            o_done = []

            def extra(i, it, out, last):
                c, hk, br = it
                if br == 1:
                    for t in range(2):
                        last = mm(out[:, 128 * t:128 * t + 128], vblk[:, hk, c, :], PcT[:, hk, t, :], False, t == 1,
                                  i_pct, i_v, skip=True)
                    if hk == 1:
                        b = 4 + c % 2
                        bank_free[b] = act(onsa[:, c, :], PS[:, b, 0:256], ACT.Copy, last)
                        o_done.append(bank_free[b])

            def mult(it):
                c, hk, br = it
                return g5[:, ::-1, c + 4 * hk, 1 + br]

            softmax_pv(items, logits, lambda it: B[:, it[0] + 4 * it[1], :],
                       lambda it, st: vnsa[:, st, 128 * it[2] + 64 * it[1]:128 * it[2] + 64 * it[1] + 64],
                       out_of, mult, L, PT, sm, [nq, nk1, nk2, dvn, i_B, dga], extra, (fill, 1))

            onsa_hi = kvTf
            rounded(kvTf, qaf, onsaf, osbf)
            n_ok = [parts_of(onsa[:, c, :], onsa_hi[:, 256 * c:256 * c + 256], o_done) for c in range(4)]
            sb_done = stick(qb, kb, vb, osb, sq, r, [dqb, dkb, dvb, nq, nk1, nk2], fill)
            fill.drain()

            b_ok = [parts_of(osb[:, c, :], qaf[:, 256 * c:256 * c + 256], sb_done[c]) for c in range(4)]
            for i in range(4):
                w = slice(512 * i, 512 * i + 512)
                dma_[2 * i + 1] = dma_[2 * i] = act(ma_f[:, w], ma_f[:, w], ACT.Sigmoid, dma_[2 * i + 1])
                dmb[2 * i + 1] = dmb[2 * i] = act(mb_f[:, w], mb_f[:, w], ACT.Sigmoid, dmb[2 * i + 1])
            u_read = state["hT"]
            n3, s3 = ((R(h_).rearrange("p (c t) -> p c t", c=4), R(l_)) for h_, l_ in ((onsa_hi, onsa), (qaf, osb)))
            gated, up_ok = {}, {}

            def up_n(j, ps, last):
                gated[j] = tt(ma[:, j, :], ps, ma[:, j, :], MUL, last, dma_[j])
                return gated[j]

            def up_s(j, ps, last):
                i2 = tt(mb[:, j, :], ps, mb[:, j, :], MUL, last, dmb[j])
                i3 = tt(hT[:, j, :], ma[:, j, :], mb[:, j, :], ADD, gated[j], i2, u_read)
                up_ok[j] = parts_of(hT[:, j, :], hhi[:, 256 * j:256 * j + 256], i3, u_read)
                return i2

            def by_turns(a, b):
                for x, y in zip(a, b):
                    yield x
                    yield y

            lin(by_turns(tiles_T("upn", 0, n3, 4, up_n, n_ok, banks=(0, 1, 2, 3)),
                         tiles_T("ups", 0, s3, 4, up_s, b_ok, banks=(4, 5, 6, 7))))
            residual("out2", H3, 8, [up_ok[c] for c in range(8)], lambda c: mod[:, 16 + c:17 + c])
            phase()
            u2_ok = rms_T(lambda c: gs2[:, c:c + 1], i_g2, shift=lambda c: mod[:, 24 + c:25 + c])
            hid_hi, hid_lo = arena[:, 1024:9216], arena[:, 9216:17408]
            rounded(*[x[:, 2048 * i:2048 * i + 2048] for x in (hid_hi, hid_lo) for i in range(4)])
            rb = [arena[:, 17408 + 256 * i:17664 + 256 * i] for i in range(4)]
            h_done, squared = [], []

            def hidden(p):
                def evict(j, ps, last):
                    i = 4 * p + j
                    w = slice(256 * i, 256 * i + 256)
                    if squared:
                        n, sq_ = squared.pop()
                        h_done.append(parts_of(hid_lo[:, n], hid_hi[:, n], sq_))
                    rr = act(rb[i % 4], ps, ACT.Relu, last, *state["barrier"], used.get(i - 4))
                    used[i] = tt(hid_lo[:, w], rb[i % 4], rb[i % 4], MUL, rr, *state["barrier"])
                    squared.append((w, used[i]))
                    return rr
                return tiles_T("w1", p, H3, 8, evict, u2_ok)

            used = {}
            lin(*[hidden(p) for p in range(8)])
            n, sq_ = squared.pop()
            h_done.append(parts_of(hid_lo[:, n], hid_hi[:, n], sq_))
            hid3 = [tuple(R(x[:, 2048 * i:2048 * i + 2048]).rearrange("p (c t) -> p c t", c=8) for x in (hid_hi, hid_lo))
                    for i in range(4)]
            residual("w2", hid3, 32, h_done, lambda c: mod[:, 40 + c:41 + c])

        def stick(qb, kb, vb, osb, sq, r, deps, fill):
            n = 8
            lg, p_ok, o_done = {}, {}, []
            cum_ok, a_use, y_ok = {}, {}, {}
            A1 = [sq[:, 384 * i:384 * i + 384] for i in range(3)]
            A2 = [sq[:, 1152 + 384 * i:1152 + 384 * i + 384] for i in range(2)] + [r[:, 0:384]]
            def stage_a(i):
                rows = slice(64 * (i % 2), 64 * (i % 2) + 64)
                c, b = i // 2, i % 4
                ps = PS[:, b, 0:384]
                mm(ps[:, 0:256], kb[rows, c, 0:128], qb[rows, c, :], True, False, deps, bank_free[b], skip=True)
                mm(ps[:, 256:384], kb[rows, c, 128:256], qb[rows, c, 128:256], False, False, skip=True)
                mm(ps[:, 0:128], ident, C("sbm"), False, False, skip=True)
                lg[i] = mm(ps[:, 256:384], ident, C("sbm"), False, False, skip=True)
                x, y = A1[i % 3], A2[i % 3]
                a = act(x, ps, ACT.Abs, lg[i], cum_ok.get(i - 3), deps)
                a = act(x, x, ACT.Exp, a, scale=-1.0)
                a = act(x, x, ACT.Ln, a, bias=onet)
                p_ok[i] = stt(x, ps, 0.0, x, MAX, ADD, a)

            def stage_b(i):
                b = i % 4
                ps = PS[:, b, 0:384]
                x, y = A1[i % 3], A2[i % 3]
                mm(ps[:, 0:256], C("ntri"), x[:, 0:256], False, False, p_ok[i], skip=True)
                mm(ps[:, 128:256], C("nones"), x[:, 256:384], False, False, skip=True)
                cum_ok[i] = mm(ps[:, 256:384], C("ntri"), x[:, 256:384], False, True, skip=True)
                y_ok[i] = bank_free[b] = act(y, ps, ACT.Exp, cum_ok[i], a_use.get(i - 3), deps)

            def stage_c(i):
                y = A2[i % 3]
                ob = 4 + (i // 2) % 2
                out = PS[64 * (i % 2):64 * (i % 2) + 64, ob, 0:256]
                mm(out, vb[:, 0, 64 * i:64 * i + 64], y[:, 0:256], True, False, y_ok[i], bank_free[ob], skip=True)
                a_use[i] = mm(out[:, 128:256], vb[:, 1, 64 * i:64 * i + 64], y[:, 256:384], False, True, skip=True)
                if i % 2:
                    bank_free[ob] = act(osb[:, i // 2, :], PS[:, ob, 0:256], ACT.Copy, a_use[i])
                    o_done.append(bank_free[ob])

            for i in range(n + 3):
                if i < n:
                    stage_a(i)
                fill.step(1)
                if 2 <= i < n + 2:
                    stage_b(i - 2)
                if i >= 3:
                    stage_c(i - 3)
            return o_done

        steps = [even_layer, lambda: peer_layer(0), odd_layer, lambda: peer_layer(1), last_block]
        for s in steps[:stop]:
            s()
        fin = phase()
        done = sp(lambda e: e.dma_start(io["out"], xTt[:, :]), *fin, dma=s_out)
        sp(lambda e: e.nop(), done)

        counts = {}
        for q in (pe, ve, ac, po, sp):
            n = 0
            for ins in q.items:
                if ins.sem is not None:
                    counts[id(ins.sem)] = ins.value = counts.get(id(ins.sem), 0) + 16
                elif ins.signals:
                    n += 1
                    ins.value = n

        def emit(q, e):
            seen = {}
            for ins in q.items:
                for w in ins.waits:
                    s = w.sem if w.sem is not None else w.queue.own
                    if seen.get(id(s), 0) < w.value:
                        seen[id(s)] = w.value
                        e.wait_ge(s, w.value)
                r = ins.fn(e)
                if ins.sem is not None:
                    r.then_inc(ins.sem, 16)
                elif ins.signals:
                    r.then_inc(q.own, 1)

        block = ctx.enter_context(nc.Block())
        block.sync(lambda e: emit(sp, e))
        block.gpsimd(lambda e: emit(po, e))
        block.scalar(lambda e: emit(ac, e))
        block.vector(lambda e: emit(ve, e))
        block.tensor(lambda e: emit(pe, e))


def pack(w, ranges):
    kc = w.shape[0] // 128
    v = w.reshape(kc, 128, w.shape[1])
    return np.concatenate([np.ascontiguousarray(v[:, :, lo:hi].transpose(1, 0, 2)).reshape(-1) for lo, hi in ranges])


def layout(inputs):
    g = {k: np.asarray(v) for k, v in inputs.items()}
    a = {}
    a["cst"] = constants()
    cols = np.zeros((128, NCOL), np.float32)

    def put(name, m):
        lo, hi = COL[name]
        cols[: m.shape[0], lo:hi] = m

    col = lambda v: v.reshape(-1, 128).T
    twice = lambda v: np.concatenate([v, v], 0)
    put("ev_g", col(g["ev_norm_mix"][0]))
    put("od_g", col(g["od_norm_mix"][0]))
    put("f0", col(g["ffn_norm"][0]))
    put("f1", col(g["ffn_norm"][1]))
    put("n1", col(g["norm1_g_2"][0]))
    put("n2", col(g["norm2_g_2"][0]))
    put("cw", g["ev_conv_w"][0].reshape(31, 4, 128).transpose(2, 0, 1).reshape(128, 124))
    put("cb", col(g["ev_conv_b"][0]))
    put("lng", col(g["ev_conv_ln_g"][0]))
    put("lnb", col(g["ev_conv_ln_b"][0]))
    put("gb", col(g["ev_gate_b"][0]))
    put("glag", col(g["ev_gla_norm_g"][0]))
    put("qg", twice(g["od_q_norm_g"][0])[:, None])
    put("kg", twice(g["od_k_norm_g"][0])[:, None])
    put("fb", g["od_fgate_b"][0][:, None])
    put("c", col(g["c_2"][0]))
    put("adab", col(g["ada_b_2"][0]))
    put("q2", twice(g["q_norm_g_2"][0])[:, None])
    put("k2", twice(g["k_norm_g_2"][0].T))
    put("pos", twice(g["cmp_pos_2"][0].T))
    put("kw2", twice(g["cmp_k_w2_2"][0]))
    put("vw2", twice(g["cmp_v_w2_2"][0]))
    a["cols"] = cols
    a["xT"] = np.ascontiguousarray(g["x"][0].T.reshape(8, 128, T).transpose(1, 0, 2)).reshape(128, 8 * T)
    a["gw2"] = g["ev_gate_w2"][0]
    a["rel"] = g["rel_bias_2"]
    a["ev_in"] = pack(g["ev_w_in"][0], EV_RANGES)
    a["ev_out"] = pack(g["ev_w_out"][0], FULL)
    a["od_in"] = pack(g["od_w_in"][0], OD_RANGES)
    a["od_out"] = pack(g["od_w_out"][0], FULL)
    for i in range(2):
        a[f"wq{i}"] = pack(g["peer_wq"][i], WQ_RANGES)
        a[f"keys{i}"] = np.ascontiguousarray(g["peer_keys"][i].reshape(16, 128, 128).transpose(2, 0, 1)).reshape(-1)
        a[f"u{i}"] = np.ascontiguousarray(g["peer_u"][i].reshape(128, 128, 8, 128).transpose(1, 3, 2, 0)).reshape(-1)
        a[f"v{i}"] = np.ascontiguousarray(g["peer_v"][i].reshape(128, 128, 1024).transpose(1, 0, 2)).reshape(-1)
    a["ada"] = pack(g["ada_w_2"][0], ADA_RANGES)
    a["in2"] = pack(g["w_in_2"][0][:, IN_ORDER], IN_RANGES)
    w1 = [g[n][0].reshape(32, 64, 64).transpose(1, 0, 2).reshape(64, 2048) for n in ("cmp_k_w1_2", "cmp_v_w1_2")]
    blocks = np.zeros((2, 2, 64, 32, 2, 64), np.float32)
    for i in range(2):
        for h in range(2):
            blocks[i, h, :, :, h, :] = w1[i].reshape(64, 32, 64)
    a["cw1"] = blocks.reshape(-1)
    a["upn"] = pack(g["w_up_nsa_2"][0][QPERM], UP_RANGES)
    a["ups"] = pack(g["w_up_sb_2"][0], UP_RANGES)
    a["out2"] = pack(g["w_out_2"][0], FULL)
    a["w1"] = pack(g["mlp_w1_2"][0], W1_RANGES)
    a["w2"] = pack(g["mlp_w2_2"][0], W2_RANGES)
    return {k: np.ascontiguousarray(v) for k, v in a.items()}


def kernel(**inputs):
    import concourse.bacc as _bacc
    from concourse.bass_utils import run_bass_kernel_spmd as _run

    arrays = layout(inputs)
    nc = _bacc.Bacc("TRN2", target_bir_lowering=False, num_devices=1)
    program(nc, declare(nc, arrays))
    r = _run(nc, [{f"in_{k}": v for k, v in arrays.items()}], core_ids=[0])
    out = np.asarray(r.results[0]["out_0"]).reshape(128, 8, T)
    return np.ascontiguousarray(out.transpose(2, 1, 0)).reshape(1, T, D)
```

```python
from contextlib import ExitStack

import numpy as np

import concourse.bass as bass
import concourse.mybir as mybir

F32 = mybir.dt.float32
F32R = mybir.dt.float32r
U32 = mybir.dt.uint32
ALU = mybir.AluOpType
ACT = mybir.ActivationFunctionType
AX = mybir.AxisListType.X

T = 256
D = 1024
NEG = -1e30
EPS = 1e-6
PAIRS = [(i, j) for i in range(16) for j in range(16) if (i + 1) * (j + 1) <= 16]
NP = len(PAIRS)
WSLOT = 4096
NW = 4

EV_RANGES = [(512, 1024), (0, 512), (1024, 1536), (2560, 2576), (1536, 2048), (2048, 2560)]
OD_RANGES = [(0, 512), (3072, 3088), (1024, 1536), (2048, 2560), (512, 1024), (1536, 2048), (2560, 3072)]
FULL = [(0, 512), (512, 1024)]
WQ_RANGES = [(i * 512, i * 512 + 512) for i in range(4)]
ADA_RANGES = [(i * 512, i * 512 + 512) for i in range(12)]
W1_RANGES = [(i * 512, i * 512 + 512) for i in range(8)]
W2_RANGES = [(i * 128, i * 128 + 128) for i in range(8)]
UP_RANGES = [(0, 1024)]
QPERM = [h * 64 + i for c in range(4) for h in (c, c + 4) for i in range(64)]
IN_ORDER = (QPERM + list(range(512, 768)) + list(range(768, 896)) + list(range(1024, 1152))
            + list(range(896, 1024)) + list(range(1152, 1304)) + list(range(1304, 4888)))
IN_RANGES = [(0, 512), (512, 1024), (1024, 1304), (1304, 1816), (1816, 2328), (2328, 2840),
             (2840, 3352), (3352, 3864), (3864, 4376), (4376, 4888)]

CST = {}
_n = 0
for _name, _w in [("ident", 128), ("ones", 128), ("bd64", 128), ("ntri", 128), ("nones", 128), ("sbm", 128), ("flip", 128),
                  ("fmask", 384), ("gm", 7 * 64), ("reset", 256), ("hot", 384), ("iota", 128), ("negrow", 8),
                  ("cneg", 2 * 16), ("cok", 2 * 16)]:
    CST[_name] = (_n, _n + _w)
    _n += _w
NCST = _n

COL = {}
_n = 0
for _name, _w in [("ev_g", 8), ("od_g", 8), ("f0", 8), ("f1", 8), ("n1", 8), ("n2", 8), ("cw", 124), ("cb", 4),
                  ("lng", 4), ("lnb", 4), ("gb", 2), ("glag", 1), ("qg", 1), ("kg", 1), ("fb", 1), ("c", 8), ("adab", 48),
                  ("q2", 1), ("k2", 3), ("pos", 32), ("kw2", 64), ("vw2", 64)]:
    COL[_name] = (_n, _n + _w)
    _n += _w
NCOL = _n


def constants():
    c = np.zeros((128, NCST), np.float32)

    def put(name, a):
        lo, hi = CST[name]
        c[: a.shape[0], lo:hi] = a.reshape(a.shape[0], -1)

    p = np.arange(128)
    put("ident", np.eye(128))
    put("ones", np.ones((128, 128)))
    put("nones", -np.ones((128, 128)))
    put("flip", np.eye(128)[::-1])
    put("bd64", (p[:, None] // 64 == p[None, :] // 64) * 1.0)
    put("ntri", (p[:, None] >= p[None, :]) * -1.0)
    put("sbm", np.where(p[:, None] < p[None, :], 0.0, NEG))
    causal = np.where(p[None, :] <= p[:, None], 0.0, NEG)
    put("fmask", np.concatenate([np.zeros((128, 128)), causal, causal], 1))
    gm = np.zeros((128, 7, 64))
    s, t = p % 64, np.arange(64)
    gm[:, 0] = s[:, None] == t[None, :]
    for lv in range(1, 7):
        g = 1 << lv
        gm[:, lv] = (s[:, None] // g == t[None, :] // g) & (s[:, None] % g < g // 2) & (t[None, :] % g >= g // 2)
    put("gm", gm)
    put("reset", np.tile((np.arange(256) % 64 != 0) * 1.0, (128, 1)))
    dist = 255 - np.arange(384)
    n = np.maximum(dist, 0)
    nf = np.maximum(n, 1).astype(np.float32)
    large = 16 + (np.log(nf / np.float32(16)) / np.float32(np.log(8.0)) * np.float32(16)).astype(np.int32)
    bucket = np.where(n < 16, n, np.minimum(large, 31))
    hot = np.zeros((33, 384))
    hot[bucket, np.arange(384)] = 1.0
    hot[:, dist < 0] = 0.0
    hot[32, dist < 0] = 1.0
    put("hot", hot)
    put("iota", np.tile(np.arange(128), (128, 1)))
    put("negrow", np.full((33, 8), NEG))
    ok = np.zeros((128, 2, 16))
    for tile in range(2):
        ok[:, tile, :15] = (tile * 128 + p)[:, None] >= (np.arange(15) * 16 + 31)[None, :]
    put("cok", ok)
    put("cneg", np.where(ok > 0, 0.0, NEG))
    return c


class Ins:
    __slots__ = ("queue", "fn", "waits", "sem", "value", "signals")

    def __init__(self, queue, fn, waits, sem):
        self.queue, self.fn, self.waits, self.sem = queue, fn, waits, sem
        self.value, self.signals = 0, sem is not None


def leaves(waits):
    for w in waits:
        if isinstance(w, (list, tuple)):
            yield from leaves(w)
        elif w is not None:
            yield w


class Queue:

    def __init__(self, own):
        self.own, self.items = own, []

    def __call__(self, fn, *waits, dma=None):
        ins = Ins(self, fn, list(leaves(waits)), dma)
        for w in ins.waits:
            w.signals = True
        self.items.append(ins)
        return ins

    @property
    def last(self):
        return self.items[-1] if self.items else None


def flat(pieces):
    at, out = 0, []
    for w in pieces:
        out.append((at, w))
        at += 128 * w
    return out, at


def widths(ranges, kc):
    return [(hi - lo) * kc for lo, hi in ranges]


WEIGHTS = {
    "ev_in": widths(EV_RANGES, 8), "ev_out": widths(FULL, 8), "od_in": widths(OD_RANGES, 8),
    "od_out": widths(FULL, 8), "wq0": widths(WQ_RANGES, 8), "wq1": widths(WQ_RANGES, 8),
    "ada": widths(ADA_RANGES, 8), "in2": widths(IN_RANGES, 8),
    "cw1": [4096, 4096], "upn": widths(UP_RANGES, 4), "ups": widths(UP_RANGES, 4), "out2": widths(FULL, 8),
    "w1": widths(W1_RANGES, 8), "w2": widths(W2_RANGES, 32),
}


def declare(nc, arrays):
    io = {}
    for name, a in arrays.items():
        io[name] = nc.dram_tensor(f"in_{name}", a.shape, F32, kind="ExternalInput").ap()
    io["out"] = nc.dram_tensor("out_0", (128, 8 * T), F32, kind="ExternalOutput").ap()
    io["fd_t"] = nc.dram_tensor("fd", (8 * 384,), F32, kind="Internal")
    io["fd"] = io["fd_t"].ap()
    return io


def program(nc, io, stop=99):
    ctx = ExitStack()
    with ctx:
        sem = lambda name: ctx.enter_context(nc.semaphore(name))
        sb = lambda name, n: ctx.enter_context(nc.sbuf_tensor(name, [128, n], F32))

        AR, XR = 22016, 6144
        base = {"hT": (nc.sbuf_base + 31) // 32 * 32}
        hTt = sb("hT", 2048)
        base["mem"] = (nc.sbuf_base + 31) // 32 * 32
        mem = sb("mem", NW * WSLOT + AR + XR)
        wring = [mem[:, 3 * WSLOT + AR + XR:]] + [mem[:, i * WSLOT:(i + 1) * WSLOT] for i in range(3)]
        arena = mem[:, 3 * WSLOT:3 * WSLOT + AR + XR]
        hhi = arena[:, AR:AR + 2048]
        S = [(arena[:, AR + 2048 + 2048 * i:AR + 3072 + 2048 * i], arena[:, AR + 3072 + 2048 * i:AR + 4096 + 2048 * i])
             for i in range(2)]
        xTt = sb("xT", 2048)
        cst = sb("cst", NCST)
        col = sb("col", NCOL)
        small = sb("small", 1024)
        arena_u = arena[:, :].bitcast(U32)
        PS = ctx.enter_context(nc.psum_tensor("PS", [128, 8, 512], F32))

        pe, ve, ac, po, sp = (Queue(sem(f"s_{n}")) for n in ("pe", "ve", "ac", "po", "sp"))
        wsem = [sem(f"s_w{i}") for i in range(NW)]
        gsem = [sem(f"s_g{i}") for i in range(4)]
        s_xs = [sem(f"s_x{i}") for i in range(4)]
        s_cst, s_one, s_col, s_misc, s_key, s_bw, s_br, s_out = (
            sem(n) for n in ("s_cst", "s_one", "s_col", "s_misc", "s_key", "s_bw", "s_br", "s_out"))

        def C(name, rows=128):
            lo, hi = CST[name]
            return cst[0:rows, lo:hi]

        def P(name, i=None):
            lo, hi = COL[name]
            return col[:, lo:hi] if i is None else col[:, lo + i:lo + i + 1]

        xT = xTt[:, :].rearrange("p (c t) -> p c t", c=8)
        hT = hTt[:, :].rearrange("p (c t) -> p c t", c=8)
        ident = C("ident")
        ones = C("ones")

        l_x = [sp(lambda e, i=i: e.dma_start(xTt[:, 512 * i:512 * i + 512], io["xT"][:, 512 * i:512 * i + 512]), dma=s_xs[i])
               for i in range(4)]
        l_one = sp(lambda e: e.dma_start(cst[:, 0:256], io["cst"][:, 0:256]), dma=s_one)
        l_col = sp(lambda e: e.dma_start(col[:, :], io["cols"]), dma=s_col)
        l_cst = sp(lambda e: e.dma_start(cst[:, 256:], io["cst"][:, 256:]), dma=s_cst)
        gw2 = small[0:16, 0:256]
        rr_ = small[:, 256:512]
        cs, mod = small[:, 528:536], small[:, 536:584]
        tbl = small[0:33, 512:520]
        l_gw2 = sp(lambda e: e.dma_start(gw2, io["gw2"]), dma=s_misc)
        l_tbl = sp(lambda e: e.dma_start(small[0:32, 512:520], io["rel"]), dma=s_misc)
        READY = [l_one, l_cst, l_col, l_tbl, *l_x]

        ring = {"n": 0, "free": [None] * NW}

        def load(name, piece):
            i = ring["n"] % NW
            ring["n"] += 1
            assert ring["free"][i] != "held"
            pieces, _ = flat(WEIGHTS[name])
            at, w = pieces[piece]
            src = io[name][at:at + 128 * w].rearrange("(p f) -> p f", p=128)
            dst = wring[i][:, 0:w]
            ins = sp(lambda e: e.dma_start(dst, src), ring["free"][i], dma=wsem[i])
            ring["free"][i] = "held"
            return i, dst, ins

        def release(slot, reader):
            ring["free"][slot] = reader

        bank_free = [None] * 8

        def mm(out, lhsT, rhs, start, stop, *waits, skip=False):
            return pe(lambda e: e.matmul(out, lhsT, rhs, start=start, stop=stop, skip_group_check=skip), *waits)

        def transpose(out, in_, *waits):
            return pe(lambda e: e.transpose(out, in_, ident), *waits)

        tables = {"now": None}

        def act(out, in_, func, *waits, **kw):
            need = {ACT.Exp: "natural_log_exp_and_others", ACT.Ln: "natural_log_exp_and_others", ACT.Gelu: "gelu",
                    ACT.Silu: "silu", ACT.Sigmoid: "sigmoid"}.get(func)
            if need and need != tables["now"]:
                tables["now"] = need
                if need == "natural_log_exp_and_others":
                    ac(lambda e: e.preload_act_table_set(need))
            return ac(lambda e: e.activation(out, in_, func, **kw), *waits)

        def tt(out, a, b, op, *waits):
            return ve(lambda e: e.tensor_tensor(out, a, b, op), *waits)

        def ts(out, a, s1, op0, *waits, s2=None, op1=None):
            if op1 is None:
                return ve(lambda e: e.tensor_scalar(out, a, s1, None, op0), *waits)
            return ve(lambda e: e.tensor_scalar(out, a, s1, s2, op0, op1), *waits)

        def stt(out, a, s, b, op0, op1, *waits):
            return ve(lambda e: e.scalar_tensor_tensor(out=out, in0=a, scalar=s, in1=b, op0=op0, op1=op1), *waits)

        def vcopy(out, in_, *waits):
            return ve(lambda e: e.tensor_copy(out, in_), *waits)

        def red(out, in_, op, *waits, negate=False):
            return ve(lambda e: e.tensor_reduce(out, in_, AX, op, negate=negate), *waits)

        def recip(out, in_, *waits):
            return ve(lambda e: e.reciprocal(out, in_), *waits)

        MUL, ADD, SUB, MAX, MIN, EQ, GT = ALU.mult, ALU.add, ALU.subtract, ALU.max, ALU.min, ALU.is_equal, ALU.is_gt

        state = {"barrier": [], "hT": None, "x": [None] * 8, "h": None}

        def phase():
            state["barrier"] = [q.last for q in (pe, ve, ac, po) if q.last is not None]
            return state["barrier"]

        cursor = {"bank": 0}

        def next_bank(banks):
            b = banks[cursor["bank"] % len(banks)]
            cursor["bank"] += 1
            return b

        over = {}

        def rounded(*aps):
            for ap in aps:
                name, lo, n = ap.tensor.name, ap.offset, ap.ap[-1][1]
                t = over.pop((name, lo, lo + n), None)
                over[name, lo, lo + n] = t or nc.alloc_sbuf_tensor_at(
                    f"r_{name}_{lo}_{n}", [128, n], F32R, offset=base[name] + 4 * lo)

        def R(ap):
            end = ap.offset + 1 + sum(s * (n - 1) for s, n in ap.ap[1:])
            for (name, lo, hi), t in reversed(over.items()):
                if name == ap.tensor.name and lo <= ap.offset and end <= hi:
                    return bass.AP(t, ap.offset - lo, [[hi - lo, 128], *ap.ap[1:]])
            raise AssertionError("no float32r tensor there")

        rounded(hTt[:, :], hhi, *[x for pair in S for x in pair])

        def RF(ap):
            return R(ap).bitcast(F32)

        hhiv = R(hhi).rearrange("p (c t) -> p c t", c=8)
        hlov = R(hTt[:, :]).rearrange("p (c t) -> p c t", c=8)
        H3 = (hhiv, hlov)
        sring = {"n": 0, "free": [None] * 2}

        def split(src, *waits):
            i = sring["n"] % 2
            sring["n"] += 1
            assert sring["free"][i] != "held"
            a, n = src.shape[1], src.shape[1] * src.shape[2]
            hi, lo = (x[:, 0:n].rearrange("p (a b) -> p a b", a=a) for x in S[i])
            i_h = act(R(hi), src, ACT.Copy, sring["free"][i], *waits)
            i_l = tt(R(lo), src, RF(hi), SUB, i_h)
            sring["free"][i] = "held"
            return i, R(hi), R(lo), i_h, i_l

        def mm3(out, hi, lo, shi, slo, i_h, i_l, start, stop, *waits, ready=None):
            n = hi.shape[1]
            for k in range(n):
                mm(out, hi[:, k, :], shi[:, k, :], start and k == 0, False, *([i_h, *waits] if k == 0 else []),
                   ready and ready[k][0])
                mm(out, hi[:, k, :], slo[:, k, :], False, False, ready and ready[k][1])
            for k in range(n):
                last = mm(out, lo[:, k, :], shi[:, k, :], False, stop and k == n - 1, *([i_l] if k == 0 else []))
            return last

        def tiles_T(name, piece, src, kc, evict, *waits, banks=(0, 1, 2, 3, 4, 5, 6, 7), loaded=None):
            slot, w, arrived = loaded or load(name, piece)
            wv = w.rearrange("p (k n) -> p k n", k=kc)
            ncols = wv.shape[2]
            pair = isinstance(src, (tuple, list))
            ku = min(kc, 8)
            bank = {}
            for j in range((ncols + 127) // 128):
                m = min(128, ncols - 128 * j)
                for u in range(kc // ku):
                    final = 128 * j + m == ncols and u == kc // ku - 1
                    part = wv[:, ku * u:ku * u + ku, 128 * j:128 * j + m]

                    def prepare(part=part, final=final):
                        if not pair:
                            return None
                        sp_ = split(part, arrived)
                        if final:
                            release(slot, sp_[4])
                        return sp_

                    def run(sp_, part=part, final=final, j=j, m=m, u=u):
                        if u == 0:
                            bank["b"] = next_bank(banks)
                        b = bank["b"]
                        out = PS[0:m, b, 0:256]
                        ks = slice(ku * u, ku * u + ku)
                        ends = u == kc // ku - 1
                        if pair:
                            i, hi, lo, i_h, i_l = sp_
                            shi, slo = src[u] if isinstance(src, list) else (src[0][:, ks, :], src[1][:, ks, :])
                            last = mm3(out, hi, lo, shi, slo, i_h, i_l, u == 0, ends,
                                       *([bank_free[b], waits] if u == 0 else []),
                                       ready=state["h"] if src is H3 and j == 0 else None)
                            sring["free"][i] = last
                        else:
                            for k in range(ku):
                                last = mm(out, part[:, k, :], src[:, ku * u + k, :], u == 0 and k == 0, ends and k == ku - 1,
                                          *([arrived, bank_free[b], waits] if k == 0 else []))
                            if final:
                                release(slot, last)
                        if src is hT or src is H3:
                            state["hT"] = last
                        if ends:
                            bank_free[b] = evict(j, out, last)
                        return last

                    yield prepare, run

        def rows_T(name, piece, evict, *waits, banks=(0, 1, 2, 3, 4, 5, 6, 7), src=None, loaded=None):
            src = src or H3
            slot, w, arrived = loaded or load(name, piece)
            wv = w.rearrange("p (k n) -> p k n", k=8)
            n = wv.shape[2]
            bank = []
            for u in range(4):
                part = wv[:, 2 * u:2 * u + 2, :]

                def prepare(part=part, u=u):
                    sp_ = split(part, arrived)
                    if u == 3:
                        release(slot, sp_[4])
                    return sp_

                def run(sp_, u=u):
                    i, hi, lo, i_h, i_l = sp_
                    if u == 0:
                        bank.extend(next_bank(banks) for _ in range(2))
                    for t in range(2):
                        toks = slice(128 * t, 128 * t + 128)
                        ks = slice(2 * u, 2 * u + 2)
                        last = mm3(PS[:, bank[t], 0:n], src[0][:, ks, toks], src[1][:, ks, toks], hi, lo, i_h, i_l,
                                   u == 0, u == 3, *([bank_free[bank[t]], waits] if u == 0 else []), i_l, state["h"])
                        if u == 3:
                            bank_free[bank[t]] = evict(t, PS[:, bank[t], 0:n], last)
                    sring["free"][i] = last
                    state["hT"] = last
                    return last

                yield prepare, run

        class stream:

            def __init__(self, *gens):
                self.items = (item for g in gens for item in g)
                self.next = None

            def prime(self):
                item = next(self.items, None) if self.next is None else None
                if item is not None:
                    self.next = (item[1], item[0]())

            def __iter__(self):
                return self

            def __next__(self):
                self.prime()
                if self.next is None:
                    raise StopIteration
                (run, ready), self.next = self.next, None
                self.prime()
                return run(ready)

        def lin(*gens):
            return run_all(stream(*gens))

        def run_all(st):
            for last in st:
                pass
            return last

        def lin_T(*a, **kw):
            return lin(tiles_T(*a, **kw))

        def rows(name, piece, evict, *waits, banks=(0, 1, 2, 3, 4, 5, 6, 7)):
            slot, w, arrived = load(name, piece)
            w = w.rearrange("p (k n) -> p k n", k=8)
            for t in range(2):
                b = next_bank(banks)
                for k in range(8):
                    last = mm(PS[:, b, :], hT[:, k, 128 * t:128 * t + 128], w[:, k, :], k == 0, k == 7,
                              *([arrived, bank_free[b], *waits] if k == 0 else []))
                bank_free[b] = evict(t, PS[:, b, :], last)
            release(slot, last)
            state["hT"] = last
            return last

        class Filler:

            def __init__(self, *gens):
                self.gens = list(gens)

            def step(self, n=1):
                while n and self.gens:
                    if next(self.gens[0], None) is None:
                        self.gens.pop(0)
                    else:
                        n -= 1

            def drain(self):
                self.step(10 ** 6)

        def rms_T(gain, *waits, first, shift=None):
            b = next_bank(range(8))
            ps = PS[:, b, 0:256]
            for c in range(8):
                i_sq = act(hT[:, c, :], xT[:, c, :], ACT.Square, state["x"][c], state["hT"], *waits)
                last = mm(ps, ones, hT[:, c, :], c == 0, c == 7, i_sq, *([bank_free[b], l_one] if c == 0 else []))
            i_r = act(rr_, ps, ACT.Ln, last, scale=1.0 / D, bias=epst)
            bank_free[b] = i_r
            i_rr = act(rr_, rr_, ACT.Exp, i_r, scale=-0.5)
            first.prime()
            state["h"] = []
            for c in range(8):
                q = ve if c % 4 != 3 else po
                h = hT[:, c, :]
                if q is ve:
                    i_h = stt(h, xT[:, c, :], gain(c), rr_, MUL, MUL, i_rr, *waits)
                    if shift is not None:
                        i_h = ts(h, h, shift(c), ADD, i_h)
                else:
                    i_h = po(lambda e, h=h, c=c: e.tensor_tensor(h, xT[:, c, :], rr_, MUL), i_rr, *waits)
                    i_h = po(lambda e, h=h, c=c: e.tensor_scalar(h, h, gain(c), None if shift is None else shift(c), MUL,
                                                                 *([] if shift is None else [ADD])), i_h)
                i_hi = act(hhiv[:, c, :], h, ACT.Copy, i_h, *state["barrier"])
                state["h"].append([i_hi, (q, h, c)])
            for p in state["h"]:
                q, h, c = p[1]
                p[1] = q(lambda e, h=h, c=c: e.tensor_tensor(hlov[:, c, :], h, RF(hhi[:, 256 * c:256 * c + 256]), SUB), p[0])

        def parts_of(raw, hi, *waits, q=None):
            i_h = act(R(hi), raw, ACT.Copy, *waits)
            low, high = R(raw), RF(hi)
            return (q or ve)(lambda e: e.tensor_tensor(low, raw, high, SUB), i_h)

        def residual(name, src, kc, deps, gate=None):
            n = len(WEIGHTS[name])
            tiles = 8 // n

            def evict(p):
                def f(j, ps, last):
                    c = p * tiles + j
                    if gate is None:
                        state["x"][c] = tt(xT[:, c, :], ps, xT[:, c, :], ADD, last)
                    else:
                        state["x"][c] = stt(xT[:, c, :], ps, gate(c), xT[:, c, :], MUL, ADD, last)
                    return state["x"][c]
                return f

            return lin(*[tiles_T(name, p, src, kc, evict(p), deps) for p in range(n)])

        epst = small[:, 520:521]
        onet = small[:, 521:522]
        i_e = ve(lambda e: e.memset(epst, EPS))
        i_one = ve(lambda e: e.memset(onet, 1.0))
        READY += [i_e, i_one]
        state["x"] = [[l_x[c // 2], l_col, i_e] for c in range(8)]

        def even_layer():
            o = 0

            def take(n):
                nonlocal o
                o += n
                return arena[:, o - n:o]

            chunks = lambda a, c: a.rearrange("p (c t) -> p c t", c=c)
            gate, rTf, yf, qkf, of, o2 = (take(1024) for _ in range(6))
            ysq = o2
            gate, rT, y = chunks(gate, 4), chunks(rTf, 4), chunks(yf, 4)
            qk = chunks(qkf, 4)
            up = chunks(take(4 * 286), 4)
            vrow = chunks(take(1024), 2)
            glr = take(256)
            mean = glr
            bf, w0, w1, w2, qd, kd = (take(512) for _ in range(6))
            qlb = [take(512) for _ in range(6)]
            klb = [take(512) for _ in range(6)]
            kdrow = chunks(w0, 2)
            dl = take(8)
            Stf, Atf = take(1024), take(1024)
            St = Stf.rearrange("p (n c d) -> p n c d", n=4, c=2)
            At = Atf.rearrange("p (a n t) -> p a n t", a=2, n=4)
            yTf = take(2048)
            yT = chunks(yTf, 8)
            assert o <= AR, o
            rounded(yTf)

            zups = [po(lambda e: e.memset(up[:, :, 0:30], 0.0))]
            zl = [po(lambda e, a=a: e.memset(a, 0.0)) for a in qlb + klb]
            zA = po(lambda e: e.memset(Atf, 0.0))
            zS = po(lambda e: e.memset(St[:, 0, :, :], 0.0))
            state["cs"] = act(cs, P("c"), ACT.Silu, READY)
            gates, us, vs, rs, qks, gl = [], [], [], [], [], []
            st = stream(
                tiles_T("ev_in", 0, H3, 8, lambda j, ps, last: gates.append(act(gate[:, j, :], ps, ACT.Sigmoid, last)) or gates[-1]),
                tiles_T("ev_in", 1, H3, 8, lambda j, ps, last: us.append(
                    tt(up[:, j, 30:286], ps, gate[:, j, :], MUL, last, gates[j], zups)) or us[-1]),
                tiles_T("ev_in", 2, H3, 8, lambda j, ps, last: qks.append(
                    act(qk[:, j, :], ps, ACT.Copy, last, scale=0.125 if j < 2 else 1.0)) or qks[-1]),
                tiles_T("ev_in", 3, H3, 8, lambda j, ps, last: gl.append(act(glr[0:16, :], ps, ACT.Copy, last)) or gl[-1]),
                rows_T("ev_in", 4, lambda t, ps, last: vs.append(act(vrow[:, t, :], ps, ACT.Copy, last)) or vs[-1]),
                tiles_T("ev_in", 5, H3, 8, lambda j, ps, last: rs.append(act(rT[:, j, :], ps, ACT.Copy, last)) or rs[-1]))
            rms_T(lambda c: P("ev_g", c), first=st)
            proj = Filler(st)
            conv = [None] * 4
            taps = chunks(o2, 4)
            on_pool = slice(2, 4)

            dve_w = iter(range(31))

            def taps_on_dve(n):
                for _, w in zip(range(n), dve_w):
                    for c in range(2):
                        if w == 0:
                            conv[c] = ts(y[:, c, :], up[:, c, 0:256], P("cw", c), MUL, us[c], s2=P("cb", c), op1=ADD)
                        else:
                            conv[c] = stt(y[:, c, :], up[:, c, w:w + 256], P("cw", 4 * w + c), y[:, c, :], MUL, ADD, conv[c])

            proj.step(8)
            for w in range(31):
                if w == 0:
                    for c in range(2, 4):
                        conv[c] = po(lambda e, c=c: e.tensor_scalar(y[:, c, :], up[:, c, 0:256], P("cw", c), P("cb", c), MUL, ADD), us[c])
                    continue
                tap = taps[:, 2 * (w % 2):2 * (w % 2) + 2, :]
                cw = P("cw")[:, 4 * w + 2:4 * w + 4].rearrange("p (c o) -> p c o", o=1).broadcast_to([128, 2, 256])
                i_t = po(lambda e, w=w, t=tap, cw=cw: e.tensor_tensor(t, up[:, on_pool, w:w + 256], cw, MUL), conv[2], conv[3])
                conv[2] = conv[3] = po(lambda e, t=tap: e.tensor_tensor(y[:, on_pool, :], y[:, on_pool, :], t, ADD), i_t)
            proj.step(6)
            x_in = []
            for c in range(2):
                b = next_bank(range(8))
                last = mm(PS[:, b, 0:256], gw2[:, 128 * c:128 * c + 128], glr[0:16, :], True, True,
                          gl[0], bank_free[b], l_gw2, l_tbl)
                i = act(bf[:, 256 * c:256 * c + 256], PS[:, b, 0:256], ACT.Identity, last, bias=P("gb", c))
                bank_free[b] = i
                x_in.append(i)
            i_abs = act(w0, bf, ACT.Abs, x_in)
            i_e1 = act(w1, w0, ACT.Exp, i_abs, scale=-1.0)
            i_l1 = act(w1, w1, ACT.Ln, i_e1, bias=onet)
            proj.step(3)
            taps_on_dve(8)
            i_L = stt(bf, bf, 0.0, w1, MIN, SUB, i_l1)
            for c in range(2):
                sc = ve(lambda e, c=c: e.tensor_tensor_scan(w0[:, 256 * c:256 * c + 256], C("reset"),
                                                            bf[:, 256 * c:256 * c + 256], 0.0, MUL, ADD), i_L)
            i_b = ts(bf, w0, 1.0 / 16.0, MUL, sc)
            qf, kf = qkf[:, 0:512], qkf[:, 512:1024]
            level = {}
            for lv in range(6, 0, -1):
                g = 1 << lv
                h = g // 2
                bg = bf.rearrange("p (n t) -> p n t", t=g)
                ref = bg[:, :, h - 1:h].broadcast_to([128, 512 // g, h])
                qs, ks = (a[lv - 1].rearrange("p (n t) -> p n t", t=g)[:, :, h:g] for a in (qlb, klb))
                ks = klb[lv - 1].rearrange("p (n t) -> p n t", t=g)[:, :, 0:h]
                d0 = tt(qs, bg[:, :, h:g], ref, SUB, i_b, zl)
                d1 = tt(ks, ref, bg[:, :, 0:h], SUB)
                e0 = act(qs, qs, ACT.Exp, d0)
                e1 = act(ks, ks, ACT.Exp, d1)
                level[lv] = [qs, ks, e0, e1]
                taps_on_dve(2)
                if lv % 2:
                    proj.step(1)
            b4 = bf.rearrange("p (n t) -> p n t", t=64)
            i_dd = tt(w2.rearrange("p (n t) -> p n t", t=64), b4[:, :, 63:64].broadcast_to([128, 8, 64]), b4, SUB, i_b)
            i_eb = act(w1, bf, ACT.Exp, i_b)
            i_ed = act(w2, w2, ACT.Exp, i_dd)
            i_dl = act(dl.rearrange("p (n t) -> p n t", t=1), b4[:, :, 63:64], ACT.Exp, i_b)
            for lv in range(6, 0, -1):
                g = 1 << lv
                h = g // 2
                qs, ks, e0, e1 = level[lv]
                i0 = tt(qs, qf.rearrange("p (n t) -> p n t", t=g)[:, :, h:g], qs, MUL, e0, qks)
                i1 = tt(ks, kf.rearrange("p (n t) -> p n t", t=g)[:, :, 0:h], ks, MUL, e1, qks)
                level[lv] = [i0, i1]
            i_qd = tt(qd, qf, w1, MUL, i_eb, qks)
            i_kd = tt(kd, kf, w2, MUL, i_ed, qks)

            taps_on_dve(3)
            proj.drain()
            h_read = state["hT"]
            copied = {}
            for lv in range(7):
                qs, ks, dep = (qf, kf, qks) if lv == 0 else (qlb[lv - 1], klb[lv - 1], level[lv])
                qv, kv = chunks(qs, 2), chunks(ks, 2)
                b = 2 * (lv % 4)
                for par in range(2):
                    rows_ = slice(64 * par, 64 * par + 64)
                    for cp in range(2):
                        for hh in range(2):
                            n = 2 * cp + hh
                            last = mm(PS[:, b + par, 128 * n:128 * n + 128], kv[rows_, hh, 128 * cp:128 * cp + 128],
                                      qv[rows_, hh, 128 * cp:128 * cp + 128], True, True,
                                      *([dep, bank_free[b], bank_free[b + 1]] if not (par or n) else []))
                for half in range(2):
                    rows_ = slice(64 * half, 64 * half + 64)
                    mask = C("gm")[rows_, 64 * lv:64 * lv + 64].rearrange("p (o t) -> p o t", o=1)
                    for par in range(2):
                        src = PS[rows_, b + par, :].rearrange("p (n t) -> p n t", n=4)[:, :, 64 * half:64 * half + 64]
                        dst = At[rows_, par, :, 64 * half:64 * half + 64]
                        m = ve(lambda e, dst=dst, src=src, mask=mask: e.copy_predicated(
                            dst, mask.bitcast(U32).broadcast_to([64, 4, 64]), src), last, copied.get((par, half), zA))
                        copied[par, half] = m
                bank_free[b] = bank_free[b + 1] = m
            for c in range(2):
                for t in range(2):
                    b = next_bank(range(8))
                    last = transpose(PS[:, b, 0:128], kd[:, 256 * c + 128 * t:256 * c + 128 * t + 128], i_kd, bank_free[b])
                    i_kr = act(kdrow[:, t, 128 * c:128 * c + 128], PS[:, b, 0:128], ACT.Copy, last)
                    bank_free[b] = i_kr
            taps_on_dve(31)
            ub = {0: 4, 1: 5, 2: 6}
            uins = []
            for n in range(3):
                rows_ = slice(64 * (n % 2), 64 * (n % 2) + 64)
                for h in range(4):
                    last = mm(PS[64 * (h % 2):64 * (h % 2) + 64, ub[n], 128 * (h // 2):128 * (h // 2) + 128],
                              kdrow[rows_, n // 2, 64 * h:64 * h + 64], vrow[rows_, n // 2, 128 * h:128 * h + 128],
                              True, True, *([i_kr, bank_free[ub[n]], vs] if h == 0 else []))
                uins.append(last)
            s_prev = zS
            for n in range(3):
                for c in range(2):
                    s_new = stt(St[:, n + 1, c, :], St[:, n, c, :], dl[:, 4 * c + n:4 * c + n + 1],
                                PS[:, ub[n], 128 * c:128 * c + 128], MUL, ADD, uins[n], i_dl, s_prev)
                s_prev = s_new
                bank_free[ub[n]] = s_new
            mean4 = mean.rearrange("p (o t) -> p o t", o=1).broadcast_to([128, 4, 256])
            for c in range(4):
                last = mm(PS[:, 2, 0:256], ones, y[:, c, :], c == 0, c == 3, conv[c], *([bank_free[2]] if c == 0 else []))
            i_m = act(mean, PS[:, 2, 0:256], ACT.Copy, last, scale=1.0 / 512)
            bank_free[2] = i_m
            i_xc = tt(y, y, mean4, SUB, i_m, last)
            i_s = act(ysq, yf, ACT.Square, i_xc)
            for c in range(4):
                last = mm(PS[:, 3, 0:256], ones, ysq[:, 256 * c:256 * c + 256], c == 0, c == 3,
                          *([i_s, bank_free[3]] if c == 0 else []))
            i_r = act(mean, PS[:, 3, 0:256], ACT.Ln, last, i_xc, scale=1.0 / 512, bias=epst)
            bank_free[3] = i_r
            i_r = act(mean, mean, ACT.Exp, i_r, scale=-0.5)
            i_xn = tt(y, y, mean4, MUL, i_r)
            ya = []
            for c in range(4):
                ya.append(act(yT[:, c, :], y[:, c, :], ACT.Silu, i_xn, scale=P("lng", c), bias=P("lnb", c)))
            y_ok = {0: parts_of(yTf[:, 0:1024], hhi[:, 0:1024], ya, state["hT"])}
            qdv = chunks(qd, 2)
            for par in range(2):
                rows_ = slice(64 * par, 64 * par + 64)
                b = 6 + par
                for hh in range(2):
                    for n in range(4):
                        last = mm(PS[:, b, 256 * hh + 64 * n:256 * hh + 64 * n + 64], St[rows_, n, hh, :],
                                  qdv[rows_, hh, 64 * n:64 * n + 64], hh == 0 and n == 0, False,
                                  *([s_prev, i_qd, bank_free[b]] if not (hh or n) else []), skip=True)
                for hh in range(2):
                    for cp in range(2):
                        h = 2 * hh + par
                        last = mm(PS[:, b, 256 * hh + 128 * cp:256 * hh + 128 * cp + 128],
                                  vrow[:, cp, 128 * h:128 * h + 128], At[:, par, 2 * cp + hh, :], False, True,
                                  *([copied[par, 0], copied[par, 1], vs] if not (hh or cp) else []), skip=True)
                i_o = act(of.rearrange("p (hh par t) -> p par hh t", hh=2, par=2)[:, par, :, :],
                          PS[:, b, :].rearrange("p (hh t) -> p hh t", hh=2), ACT.Copy, last)
                bank_free[b] = i_o
            yhi, ylo = hhiv, R(yTf).rearrange("p (c t) -> p c t", c=8)

            def out():
                loads = [load("ev_out", p) for p in range(2)]
                for half in (0, 1):
                    for n in range(8):
                        slot, w, arrived = loads[n // 4]
                        ks = slice(4 * half, 4 * half + 4)
                        part = chunks(w, 8)[:, ks, 128 * (n % 4):128 * (n % 4) + 128]

                        def prepare(part=part, arrived=arrived, slot=slot, half=half, n=n):
                            sp_ = split(part, arrived)
                            if half == 1 and n % 4 == 3:
                                release(slot, sp_[4])
                            return sp_

                        def run(sp_, half=half, n=n, ks=ks):
                            i, hi, lo, i_h, i_l = sp_
                            last = mm3(PS[:, n, 0:256], hi, lo, yhi[:, ks, :], ylo[:, ks, :], i_h, i_l, half == 0, half == 1,
                                       y_ok[half], *([] if half else [bank_free[n]]))
                            sring["free"][i] = last
                            if half:
                                bank_free[n] = state["x"][n] = tt(xT[:, n, :], PS[:, n, 0:256], xT[:, n, :], ADD, last)
                            state["hT"] = last
                            return last

                        yield prepare, run

            outs = Filler(stream(out()))
            outs.step(3)
            i_sq = act(o2, of, ACT.Square, i_o)
            done = []
            for i in range(2):
                last = mm(PS[:, 4 + i, :], ones, o2[:, 512 * i:512 * i + 512], True, True, i_sq, bank_free[4 + i])
            for i in range(2):
                bank_free[4 + i] = act(o2[:, 512 * i:512 * i + 512], PS[:, 4 + i, :], ACT.Ln, last, scale=1.0 / 128, bias=epst)
                done.append(bank_free[4 + i])
            i_r = act(o2, o2, ACT.Exp, done, scale=-0.5)
            i_n = stt(of, of, P("glag", 0), o2, MUL, MUL, i_r)
            i_rs = act(rTf, rTf, ACT.Silu, rs)
            i_yb = tt(yTf[:, 1024:2048], of, rTf, MUL, i_n, i_rs)
            y_ok[1] = parts_of(yTf[:, 1024:2048], hhi[:, 1024:2048], i_yb, h_read)
            outs.drain()
        def peer_layer(layer):
            start = phase()
            at = {"o": 0}

            def take(n):
                at["o"] += n
                return arena[:, at["o"] - n:at["o"]]

            av = mem[:, 0:32768].rearrange("p (j t) -> p j t", j=128)
            A0 = 32768 - 3 * WSLOT
            LATE = 4096 + 6 * 256 + 1500
            at["o"] = A0 - LATE - 4096
            keysb = take(2048)
            qTb = [take(1024).rearrange("p (c t) -> p c t", c=4) for _ in range(2)]
            late = at["o"]
            j_early, j_late = (3 * WSLOT + late - 4096) // 256, (3 * WSLOT + late) // 256
            scores = take(4096).rearrange("p (t h n) -> p t h n", t=2, h=16)
            SC, EF, GT, E1, E2 = (take(256) for _ in range(5))
            EI = arena_u[:, at["o"]:at["o"] + 256]
            take(256)
            s2 = take(128)
            cand, cand2, ecand = (take(NP + 2)[:, 0:NP] for _ in range(3))
            hot = take(16 * NP)
            v16 = take(32)
            i16 = arena_u[:, at["o"]:at["o"] + 32]
            take(32)
            f16 = take(32)
            p16 = arena_u[:, at["o"]:at["o"] + 16]
            take(16)
            p16f = take(16)
            st = take(32)
            assert at["o"] <= A0, at["o"]
            at["o"] = A0
            cbuf = take(1536)
            assert at["o"] <= AR, at["o"]
            eT = [cbuf[:, 256 * i:256 * i + 256] for i in range(5)]
            CS = [(cbuf[:, 512 * i:512 * i + 256], cbuf[:, 512 * i + 256:512 * i + 512]) for i in range(3)]
            rounded(*[x for pair in CS for x in pair])
            raw = [wring[0][:, 1024 * i:1024 * i + 1024] for i in range(4)]

            sc_ok = {}
            qT_use = [None, None]

            def queries(p):
                def evict(j, ps, last):
                    qs[p].append(act(qTb[p % 2][:, j, :], ps, ACT.Copy, last, qT_use[p % 2], *start))
                    if j == 3 and p >= 1:
                        score(p - 1)
                    return qs[p][-1]
                return tiles_T(f"wq{layer}", p, H3, 8, evict, banks=(0, 1, 2, 3), loaded=wq[p])

            def score(p):
                for t in range(2):
                    b = next_bank((4, 5, 6, 7))
                    for j in range(4):
                        last = mm(PS[:, b, 128 * j:128 * j + 128], qTb[p % 2][:, j, 128 * t:128 * t + 128],
                                  keys[:, 4 * p + j, :], True, True, *([qs[p][3], karr, bank_free[b]] if j == 0 else []))
                    i = act(scores[:, t, 4 * p:4 * p + 4, :].rearrange("p h n -> p (h n)"), PS[:, b, :], ACT.Copy, last, *start)
                    bank_free[b] = i
                    sc_ok[t, 2 * p] = sc_ok[t, 2 * p + 1] = i
                qT_use[p % 2] = last
                return last

            qs = [[] for _ in range(4)]
            wq = [load(f"wq{layer}", p) for p in range(4)]
            karr = sp(lambda e: e.dma_start(keysb[:, :], io[f"keys{layer}"].rearrange("(p f) -> p f", p=128)), *start, dma=s_key)
            keys = keysb.rearrange("p (h n) -> p h n", h=16)
            asked = stream(*[queries(p) for p in range(4)])
            rms_T(lambda c: P(f"f{layer}", c), first=asked)
            run_all(asked)
            ring_was = list(ring["free"])

            n_raw = {"n": 0}
            raw_free = [ring_was[0]] * 4

            def tile(table, j):
                n = n_raw["n"]
                n_raw["n"] += 1
                r = raw[n % 4]
                src = io[f"{table}{layer}"][131072 * j:131072 * j + 131072].rearrange("(p f) -> p f", p=128)
                arrived = sp(lambda e: e.dma_start(r, src), raw_free[n % 4], dma=gsem[n % 4])
                got = split(r.rearrange("p (c e) -> p c e", c=8), arrived, *start)
                raw_free[n % 4] = got[4]
                return got

            def topk(t, h):
                sc16, ef = SC[:, 128 * t + 16 * h:128 * t + 16 * h + 16], EF[:, 128 * t + 16 * h:128 * t + 16 * h + 16]
                first = [sc_ok[t, h], *start]
                for side in range(2):
                    s = scores[:, t, 2 * h + side, :]
                    va, vb = v16[:, 16 * side:16 * side + 8], v16[:, 16 * side + 8:16 * side + 16]
                    ia, ib = i16[:, 16 * side:16 * side + 8], i16[:, 16 * side + 8:16 * side + 16]
                    a = ve(lambda e, va=va, s=s: e.max(va, s), *(first if side == 0 else []))
                    a = ve(lambda e, va=va, s=s: e.match_replace(s2, va, s, -3e38), a)
                    ve(lambda e, ia=ia, va=va, s=s: e.max_index(ia, va, s))
                    a = ve(lambda e, vb=vb: e.max(vb, s2), a)
                    a = ve(lambda e, ib=ib, vb=vb: e.max_index(ib, vb, s2), a)
                    yield a
                a = vcopy(f16, i16, a)
                a = ts(f16[:, 0:16], f16[:, 0:16], 128.0, MUL, a)
                off = 0
                for i0, i1, n in ((0, 1, 16), (1, 2, 8), (2, 3, 5), (3, 4, 4), (4, 5, 3), (5, 8, 2), (8, 16, 1)):
                    m = i1 - i0
                    for dst, src in ((cand, v16), (ecand, f16)):
                        dv = dst[:, off:off + m * n].rearrange("p (i j) -> p i j", i=m)
                        x = src[:, i0:i1].rearrange("p (i o) -> p i o", o=1).broadcast_to([128, m, n])
                        yy = src[:, 16:16 + n].rearrange("p (o j) -> p o j", o=1).broadcast_to([128, m, n])
                        c = tt(dv, x, yy, ADD, a)
                    off += m * n
                yield c
                a = ve(lambda e: e.max(sc16[:, 0:8], cand), c)
                a = ve(lambda e: e.match_replace(cand2, sc16[:, 0:8], cand, -3e38), a)
                ve(lambda e: e.max_index(p16[:, 0:8], sc16[:, 0:8], cand))
                a = ve(lambda e: e.max(sc16[:, 8:16], cand2), a)
                a = ve(lambda e: e.max_index(p16[:, 8:16], sc16[:, 8:16], cand2), a)
                a = vcopy(p16f, p16, a)
                yield a
                hv = hot.rearrange("p (k c) -> p k c", k=16)
                a = tt(hv, p16f.rearrange("p (k o) -> p k o", o=1).broadcast_to([128, 16, NP]),
                       C("iota")[:, 0:NP].rearrange("p (o c) -> p o c", o=1).broadcast_to([128, 16, NP]), EQ, a)
                yield a
                a = tt(hv, hv, ecand.rearrange("p (o c) -> p o c", o=1).broadcast_to([128, 16, NP]), MUL, a)
                yield a
                yield red(ef, hv, ADD, a)

            e_ok = []

            def choices():
                for t in range(2):
                    for h in range(8):
                        for a in topk(t, h):
                            yield a
                g = GT.rearrange("p (h k) -> p h k", h=16)
                s = SC.rearrange("p (h k) -> p h k", h=16)
                x = tt(g, s, s[:, :, 0:1].broadcast_to([128, 16, 16]), SUB, a)
                x = act(GT, GT, ACT.Exp, x)
                a = vcopy(EI, EF, a)
                b1 = ts(E2.bitcast(U32), EI, 127, ALU.bitwise_and, a)
                b2 = ts(E1.bitcast(U32), EI, 7, ALU.logical_shift_right, a)
                b1 = vcopy(E2, E2.bitcast(U32), b1)
                b2 = vcopy(E1, E1.bitcast(U32), b2)
                yield b2
                a = red(st[:, 0:16], g, ADD, x)
                a = recip(st[:, 16:32], st[:, 0:16], a)
                a = tt(g, g, st[:, 16:32].rearrange("p (h o) -> p h o", o=1).broadcast_to([128, 16, 16]), MUL, a)
                yield a
                yield a
                for t in range(2):
                    w = slice(128 * t, 128 * t + 128)
                    b = next_bank((0, 1, 2, 3))
                    for i, m in enumerate((E1, E2, GT)):
                        last = transpose(PS[:, b, 128 * i:128 * i + 128], m[:, w], a, b2, bank_free[b])
                    for i in range(3):
                        act(eT[i][:, w], PS[:, b, 128 * i:128 * i + 128], ACT.Copy, last, *start)
                    for i in range(2):
                        bank_free[b] = act(eT[3 + i][:, w], PS[:, b, 128 * i:128 * i + 128], ACT.Copy, last, *start, scale=-1.0)
                    e_ok.append(bank_free[b])
                    yield last

            picks = Filler(choices())
            cur = tile("u", 0)
            q_done = score(3)
            gelu = None
            for j in range(128):
                nxt = tile("u" if j < 127 else "v", (j + 1) % 128)
                picks.step(2 if j % 4 == 3 else 1)
                if j == j_late - 2:
                    picks.drain()
                sl, hi, lo, i_h, i_l = cur
                b = next_bank((0, 1, 2, 3))
                out = PS[:, b, 0:256]
                last = mm3(out, hi, lo, hhiv, hlov, i_h, i_l, True, True, bank_free[b])
                sring["free"][sl] = last
                before = [ring_was[1 + j // 16]] if j < 48 else [q_done] if j < j_late else [e_ok]
                assert j < j_early or j >= 48
                gelu = act(av[:, j, :], out, ACT.Gelu, last, before, *start)
                bank_free[b] = gelu
                cur = nxt
            state["hT"] = last

            oneA = hhi.rearrange("p (n e) -> p n e", n=16)
            oneB = hTt[:, :].rearrange("p (n e) -> p n e", n=16)
            iota = C("iota")
            prod = {}

            def one_hots(g):
                s = 4 * (g % 4)
                w = [e_ok, last, prod.get(g - 4)]
                done = []
                for i in range(4):
                    n, o = 4 * g + i, oneA[:, s + i, :]
                    if i < 1 + (g % 4 == 0):
                        done.append(po(lambda e, n=n, o=o: e.tensor_scalar(o, iota, eT[0][:, n:n + 1], eT[2][:, n:n + 1], EQ, MUL), *w))
                    elif i < 2 + (g % 4 == 0):
                        done.append(ve(lambda e, n=n, o=o: e.tensor_scalar(o, iota, eT[0][:, n:n + 1], eT[2][:, n:n + 1], EQ, MUL), *w))
                    else:
                        x = act(o, iota, ACT.Abs, *w, bias=eT[3][:, n:n + 1])
                        done.append(act(o, o, ACT.Relu, x, scale=-2.0, bias=eT[2][:, n:n + 1]))
                for i in range(0):
                    x = act(oneB[:, s + i, :], iota, ACT.Abs, *w, bias=eT[4][:, 4 * g + i:4 * g + i + 1])
                if 0:
                    done.append(act(oneB[:, s:s + 0, :], oneB[:, s:s + 0, :], ACT.Relu, x, scale=-1.0, bias=onet))
                nb = 4 - 0
                if nb:
                    done.append(tt(oneB[:, s + 0:s + 4, :], iota.rearrange("p (o e) -> p o e", o=1).broadcast_to([128, nb, 128]),
                                   eT[1][:, 4 * g + 0:4 * g + 4].rearrange("p (t o) -> p t o", o=1).broadcast_to([128, nb, 128]), EQ, *w))
                return done

            hots = [one_hots(g) for g in range(2)]
            for g in range(64):
                b = next_bank((0, 1, 2, 3))
                for i in range(4):
                    prod[g] = mm(PS[:, b, 128 * i:128 * i + 128], oneA[:, 4 * (g % 4) + i, :], oneB[:, 4 * (g % 4) + i, :],
                                 True, True, *([hots[g], bank_free[b]] if i == 0 else []))
                if g < 62:
                    hots.append(one_hots(g + 2))
                m = av[:, :, 4 * g:4 * g + 4]
                a_ok = bank_free[b] = tt(m, m, PS[:, b, :].rearrange("p (t j) -> p j t", t=4), MUL, prod[g], gelu)

            state["hT"] = prod[63]

            c_free, freed = [None] * 3, {}

            def coef(j):
                hi, lo = CS[j % 3]
                i_h = act(R(hi), av[:, j, :], ACT.Copy, a_ok, c_free[j % 3])
                freed[j] = tt(R(lo), av[:, j, :], RF(hi), SUB, i_h)
                return R(hi), R(lo), i_h, freed[j]

            ada_sum, ada_got = small[:, 0:512], {"use": state["barrier"], "sum": None}

            def modulation(j):
                piece, i = (j - 4) // 10, (j - 4) % 10
                if j < 4 or piece >= 12 or i % 2:
                    return
                q = i // 2
                if q < 4:
                    n = n_raw["n"]
                    n_raw["n"] += 1
                    r = raw[n % 4]
                    p0, w = flat(WEIGHTS["ada"])[0][piece]
                    src = io["ada"][p0:p0 + 128 * w].rearrange("(p f) -> p f", p=128)[:, 1024 * q:1024 * q + 1024]
                    arrived = sp(lambda e: e.dma_start(r, src), raw_free[n % 4], dma=gsem[n % 4])
                    k = 2 * q
                    if q == 0:
                        a = ts(ada_sum, r[:, 0:512], cs[:, 0:1], MUL, arrived, state["cs"], ada_got["use"])
                    else:
                        a = stt(ada_sum, r[:, 0:512], cs[:, k:k + 1], ada_sum, MUL, ADD, arrived, ada_got["sum"])
                    ada_got["sum"] = raw_free[n % 4] = stt(ada_sum, r[:, 512:1024], cs[:, k + 1:k + 2], ada_sum, MUL, ADD, a)
                else:
                    b = next_bank((0, 1, 2, 3))
                    for m in range(4):
                        last = mm(PS[:, b, m:m + 1], ada_sum[:, 128 * m:128 * m + 128], ones[:, 0:1], True, True,
                                  *([ada_got["sum"], bank_free[b]] if m == 0 else []))
                    ada_got["use"] = last
                    bank_free[b] = state["mod"] = tt(mod[:, 4 * piece:4 * piece + 4], PS[:, b, 0:4],
                                                     P("adab")[:, 4 * piece:4 * piece + 4], ADD, last)

            ccur, chunk_done = coef(0), {}
            for j in range(128):
                if j < 127:
                    cnxt, nxt = coef(j + 1), tile("v", j + 1)
                sl, hi, lo, i_h, i_l = cur
                chi, clo, j_h, j_l = ccur
                outs = [PS[:, 4 + c // 2, 256 * (c % 2):256 * (c % 2) + 256] for c in range(8)]
                for c in range(8):
                    mm(outs[c], hi[:, c, :], chi, j == 0 and c % 2 == 0, False,
                       *([i_h, j_h] + [bank_free[4 + i] for i in range(4) if j == 0] if c == 0 else []), skip=True)
                    mm(outs[c], hi[:, c, :], clo, False, False, *([j_l] if c == 0 else []), skip=True)
                    if j == 127:
                        chunk_done[c] = mm(outs[c], lo[:, c, :], chi, False, True, i_l, skip=True)
                for c in range(8 if j < 127 else 0):
                    last = mm(outs[c], lo[:, c, :], chi, False, False, *([i_l] if c == 0 else []), skip=True)
                sring["free"][sl] = c_free[j % 3] = last
                if layer == 0:
                    modulation(j)
                cur, ccur = nxt, cnxt
            for c in range(8):
                state["x"][c] = tt(xT[:, c, :], PS[:, 4 + c // 2, 256 * (c % 2):256 * (c % 2) + 256], xT[:, c, :], ADD, chunk_done[c | 1])
                bank_free[4 + c // 2] = state["x"][c]
            ring["free"] = [raw_free] + [freed[16 * i + 15] for i in range(3)]
            ring["n"] = 1

        def softmax_pv(items, logits, bias, v_of, out_of, mult, L, PT, sm, deps, extra, fill):
            n = len(items)
            lg, ex, pn, tr, pt, l_use, pt_use = {}, {}, {}, {}, {}, {}, {}
            filler, rate = fill
            nb = len(L)

            def stage_a(i):
                b = i % 2
                lg[i] = logits(items[i], PS[:, b, 0:256], PS[:, b, 256:384], [deps, bank_free[b]])
                l, s = L[i % nb], sm[i % nb]
                a = tt(l, PS[:, b, 0:384], bias(items[i]), ADD, lg[i], l_use.get(i - nb))
                bank_free[b] = a
                m1 = red(s[:, 0:1], l[:, 0:256], MAX, a, negate=True)
                m0 = red(s[:, 1:2], l[:, 256:384], MAX, a, negate=True)
                act(l[:, 0:256], l[:, 0:256], ACT.Exp, m0, bias=s[:, 0:1], accum_out=s[:, 2:3])
                ex[i] = act(l[:, 256:384], l[:, 256:384], ACT.Exp, m0, bias=s[:, 1:2], accum_out=s[:, 3:4])

            def scale(i):
                l, s = L[i % nb], sm[i % nb]
                a = recip(s[:, 4:6], s[:, 2:4], ex[i])
                if mult is not None:
                    a = tt(s[:, 4:6], s[:, 4:6], mult(items[i]), MUL, a)
                ts(l[:, 0:256], l[:, 0:256], s[:, 4:5], MUL, a)
                pn[i] = ts(l[:, 256:384], l[:, 256:384], s[:, 5:6], MUL, a)

            def stage_b(i):
                l = L[i % nb]
                b = 2 + i % 2
                transpose(PS[:, b, 0:128], l[:, 256:384], pn[i], bank_free[b])
                transpose(PS[:, b, 128:256], l[:, 0:128])
                l_use[i] = tr[i] = transpose(PS[:, b, 256:384], l[:, 128:256])
                p = PT[i % 2]
                pt[i] = act(p, PS[:, b, 0:384], ACT.Copy, tr[i], pt_use.get(i - 2))
                bank_free[b] = pt[i]

            def stage_c(i):
                p = PT[i % 2]
                out, first, stop, waits = out_of(i, items[i])
                mm(out[:, 0:256], v_of(items[i], 0), p[:, 0:256], first, False, pt[i], waits, skip=True)
                pt_use[i] = mm(out[:, 128:256], v_of(items[i], 1), p[:, 256:384], False, stop, skip=True)
                extra(i, items[i], out, pt_use[i])

            for i in range(n + 3):
                if 2 <= i < n + 2:
                    scale(i - 2)
                if i < n:
                    stage_a(i)
                filler.step(rate)
                if 2 <= i < n + 2:
                    stage_b(i - 2)
                if i >= 3:
                    stage_c(i - 3)

        def head_norm(src, n, gcol, sq, r, deps, banks):
            w = n * 256
            i_sq = act(sq[:, 0:w], src, ACT.Square, deps)
            done = []
            for i in range(0, w, 512):
                m = min(512, w - i)
                b = next_bank(banks)
                last = mm(PS[:, b, 0:m], C("bd64"), sq[:, i:i + m], True, True, i_sq, bank_free[b])
                bank_free[b] = act(r[:, i:i + m], PS[:, b, 0:m], ACT.Ln, last, scale=1.0 / 64, bias=epst)
                done.append(bank_free[b])
            a = act(r[:, 0:w], r[:, 0:w], ACT.Exp, done, scale=-0.5)
            return stt(src, src, gcol, r[:, 0:w], MUL, MUL, a)

        def odd_layer():
            start = phase()
            o = 0

            def take(n):
                nonlocal o
                o += n
                return arena[:, o - n:o]

            qf, kf = take(2048), take(2048)
            q, k = (a.rearrange("p (c t) -> p c t", c=8) for a in (qf, kf))
            v = take(2048).rearrange("p (t n) -> p t n", t=2)
            oTf = take(2048)
            rounded(oTf)
            oT = oTf.rearrange("p (c t) -> p c t", c=8)
            sqk, rk, sq, r = (take(1024) for _ in range(4))
            L = [take(384) for _ in range(3)]
            PT = [take(384) for _ in range(2)]
            sm = [take(8) for _ in range(3)]
            fz, f1, f2 = take(256), take(256), take(256)
            qg = take(1)
            assert o <= AR, o
            zf = po(lambda e: e.memset(fz, 0.0), *start)
            i_qg = ts(qg, P("qg", 0), 0.125, MUL, *start)
            dq, dk, dv, df = [], [], [], []

            def ev(dst, p, done):
                return lambda j, ps, last: done.append(act(dst[:, 4 * p + j, :], ps, ACT.Copy, last, *start)) or done[-1]

            def proj(p, **kw):
                yield from tiles_T("od_in", 4 * p, H3, 8, ev(q, p, dq), **kw)
                if p == 0:
                    yield from tiles_T("od_in", 1, H3, 8, lambda j, ps, last: df.append(
                        act(fz[0:16, :], ps, ACT.Identity, last, zf, bias=P("fb", 0)[0:16, :])) or df[-1], **kw)
                yield from tiles_T("od_in", 2 + 3 * p, H3, 8, ev(k, p, dk), **kw)
                yield from rows_T("od_in", 3 + 3 * p, lambda t, ps, last: dv.append(
                    act(v[:, t, 512 * p:512 * p + 512], ps, ACT.Copy, last, *start)) or dv[-1], **kw)

            first = stream(proj(0))
            rms_T(lambda c: P("od_g", c), first=first)
            run_all(first)
            z16 = fz[0:16, :]
            a = act(f1[0:16, :], z16, ACT.Abs, df)
            a = act(f1[0:16, :], f1[0:16, :], ACT.Exp, a, scale=-1.0)
            a = act(f1[0:16, :], f1[0:16, :], ACT.Ln, a, bias=onet[0:16, :])
            a = stt(f2[0:16, :], z16, 0.0, f1[0:16, :], MIN, SUB, a)
            a = ts(f2[0:16, :], f2[0:16, :], -1.0, MUL, a)
            i_c = ve(lambda e: e.tensor_tensor_scan(z16, C("ones", 16)[:, 0:1].broadcast_to([16, 256]),
                                                    f2[0:16, :], 0.0, MUL, ADD), a)
            o_done = []

            def logits(h, t1, t0, waits):
                rows_ = slice(64 * (h % 2), 64 * (h % 2) + 64)
                c = h // 2
                pick = ident[:, h:h + 1].broadcast_to([128, 128])
                mm(t1, q[rows_, c, 128:256], k[rows_, c, :], True, False, waits, norm[h // 8], skip=True)
                mm(t1, pick, fz, False, True, skip=True)
                mm(t0, q[rows_, c, 0:128], k[rows_, c, 0:128], False, False, skip=True)
                return mm(t0, pick, fz[:, 0:128], False, True, skip=True)

            def out_of(i, h):
                b = 4 + (h // 2) % 2
                return (PS[64 * (h % 2):64 * (h % 2) + 64, b, 0:256], True, True, [bank_free[b]])

            def extra(i, h, out, last):
                if h % 2:
                    b = 4 + (h // 2) % 2
                    bank_free[b] = act(oT[:, h // 2, :], PS[:, b, 0:256], ACT.Copy, last, *start)
                    o_done.append(bank_free[b])

            norm = {}

            def norms(p, banks):
                w = slice(1024 * p, 1024 * p + 1024)
                nq = head_norm(qf[:, w], 4, qg, sq, r, [dq, i_qg, *start], banks)
                yield nq
                norm[p] = [nq, head_norm(kf[:, w], 4, P("kg", 0), sqk, rk, [dk, *start], banks)]
                yield norm[p]

            fill = Filler(stream(proj(1, banks=(6, 7))), norms(1, (6, 7)))
            for _ in norms(0, range(8)):
                fill.step(1)
            softmax_pv(list(range(16)), logits, lambda h: C("fmask"),
                       lambda h, st: v[:, st, 64 * h:64 * h + 64], out_of, None, L, PT, sm,
                       [i_c, dv, *start], extra, (fill, 2))
            o_ok = [parts_of(oT[:, c, :], hhi[:, 256 * c:256 * c + 256], o_done[c], state["hT"]) for c in range(8)]
            state["hT"] = residual("od_out", (hhiv, R(oT)), 8, o_ok)

        def last_block():
            start = phase()
            o = 0

            def take(n):
                nonlocal o
                o += n
                return arena[:, o - n:o]

            gs1, gs2 = take(8), take(8)
            B = take(8 * 384).rearrange("p (h n) -> p h n", h=8)
            qaf = take(1024)
            qa = qaf.rearrange("p (c t) -> p c t", c=4)
            kvT = take(1024).rearrange("p (c t) -> p c t", c=4)
            kvTf = arena[:, o - 1024:o]
            vnsa = take(512).rearrange("p (t n) -> p t n", t=2)
            ga = take(48).rearrange("p (t n) -> p t n", t=2)
            qb = take(1024).rearrange("p (c t) -> p c t", c=4)
            kb = take(1024).rearrange("p (c t) -> p c t", c=4)
            vb = take(1024).rearrange("p (t n) -> p t n", t=2)
            onsaf = take(1024)
            onsa = onsaf.rearrange("p (c t) -> p c t", c=4)
            osbf = take(1024)
            osb = osbf.rearrange("p (c t) -> p c t", c=4)
            ma_f, mb_f = take(2048), take(2048)
            ma, mb = (a.rearrange("p (c t) -> p c t", c=8) for a in (ma_f, mb_f))
            sq, r = take(2048), take(1536)
            L = [take(384) for _ in range(3)]
            PT = [take(384) for _ in range(2)]
            sm = [take(8) for _ in range(3)]
            Fv = L[0]
            blk = osbf[:, 0:960].rearrange("p (a i c) -> p a i c", a=2, i=32)
            hid15 = PT[0][:, 0:256]
            hid = take(32)
            kcT = take(16)
            hrep = take(128)
            vblk = take(512).rearrange("p (k g d) -> p k g d", k=2, g=4)
            Lc = r[:, 384:640].rearrange("p (k t g c) -> p k t g c", k=2, t=2, g=4)
            BC = r[:, 640:896].rearrange("p (k t g c) -> p k t g c", k=2, t=2, g=4)
            Pc = r[:, 896:1408].rearrange("p (k t g c) -> p k t g c", k=2, t=2, g=4)
            PcT = take(512).rearrange("p (k t n) -> p k t n", k=2, t=2)
            cm = take(48)
            qg = take(1)
            assert o <= AR, o

            i_g = stt(gs1, mod[:, 8:16], 1.0, P("n1"), ADD, MUL, state["mod"], *start)
            i_g2 = stt(gs2, mod[:, 32:40], 1.0, P("n2"), ADD, MUL)
            in2 = {p: load("in2", p) for p in (1, 0, 2)}
            i_t = vcopy(tbl[32:33, :], C("negrow", 33)[32:33, :], *start)
            last = mm(PS[0:8, 6, 0:384], tbl, C("hot", 33), True, True, i_t, bank_free[6], *READY)
            i_F = act(Fv[0:8, :], PS[0:8, 6, 0:384], ACT.Copy, last, *start)
            bank_free[6] = i_F
            d_w = sp(lambda e: e.dma_start(io["fd"].rearrange("(h n) -> h n", h=8), Fv[0:8, :]), i_F, dma=s_bw)
            src = bass.AP(io["fd_t"], 0, [[1, 128], [384, 8], [1, 256]])
            d_r1 = sp(lambda e: e.dma_start(ma_f.rearrange("p (h n) -> p h n", h=8), src), d_w, *start, dma=s_br)

            i_qg = ts(qg, P("q2", 0), 0.125, MUL, *start)

            def cp(dst, done, *ws, func=ACT.Copy, **kw):
                return lambda j, ps, last: done.append(act(dst(j), ps, func, last, *start, *ws, **kw)) or done[-1]

            dqa, dkv, dvn, dga, dqb, dkb, dvb, dma_, dmb = [], [], [], [], [], [], [], [], []
            def vg(t, ps, last):
                dvn.append(act(vnsa[:, t, :], ps[:, 0:256], ACT.Copy, last, *start))
                dga.append(act(ga[:, t, :], ps[:, 256:280], ACT.Sigmoid, last, *start))
                return dga[-1]

            first = stream(tiles_T("in2", 1, H3, 8, cp(lambda j: kvT[:, j, :], dkv), loaded=in2[1]),
                           tiles_T("in2", 0, H3, 8, cp(lambda j: qa[:, j, :], dqa), loaded=in2[0]),
                           rows_T("in2", 2, vg, loaded=in2[2]))
            rms_T(lambda c: gs1[:, c:c + 1], i_g, first=first, shift=lambda c: mod[:, c:c + 1])
            run_all(first)
            fb = (6, 7)
            pos = P("pos")
            bl = []
            for a in range(2):
                kview = kvT[:, a, :].rearrange("p (c j) -> p j c", j=16)
                for half in range(2):
                    bl.append(tt(blk[:, a, 16 * half:16 * half + 16, :], kview[:, :, half:half + 15],
                                 pos[:, 16 * half:16 * half + 16].rearrange("p (i o) -> p i o", o=1).broadcast_to([128, 16, 15]),
                                 ADD, dkv, *start))
            hid_ok = []
            for a in range(2):
                slot, w, arr = load("cw1", a)
                wi = w.rearrange("p (i n) -> p i n", i=32)
                for i in range(32):
                    last = mm(PS[0:15, a, 0:128], blk[:, a, i, :], wi[:, i, :], i == 0, i == 31,
                              *([arr, bl, bank_free[a]] if i == 0 else []))
                release(slot, last)
                i_h = act(hid15[0:15, 128 * a:128 * a + 128], PS[0:15, a, 0:128], ACT.Silu, last, *start)
                bank_free[a] = i_h
                hid_ok.append(i_h)
            nq = head_norm(qaf, 4, qg, sq, r, [dqa, i_qg, *start], (2, 3, 4, 5))
            nk1 = head_norm(kvTf[:, 512:768], 1, P("k2", 1), sq[:, 1024:1280], r[:, 1024:1280], [dkv, *start], (2, 3, 4, 5))
            nk2 = head_norm(kvTf[:, 768:1024], 1, P("k2", 2), sq[:, 1280:1536], r[:, 1280:1536], [dkv, *start], (2, 3, 4, 5))
            for p in range(4):
                b = 2 + p
                flipped = mm(PS[:, b, :], C("flip"), ma_f[:, 512 * p:512 * p + 512], True, True, d_r1, bank_free[b])
                i_B = vcopy(B[:, 2 * p:2 * p + 2, 0:256], PS[:, b, :].rearrange("p (h n) -> p h n", h=2), flipped, *start)
                bank_free[b] = i_B
            i_B = vcopy(B[:, :, 256:384], B[:, :, 128:256], i_B)
            fill = Filler(stream(
                tiles_T("in2", 3, H3, 8, cp(lambda j: qb[:, j, :], dqb, scale=0.125), banks=fb),
                tiles_T("in2", 4, H3, 8, cp(lambda j: kb[:, j, :], dkb), banks=fb),
                rows_T("in2", 5, lambda t, ps, last: dvb.append(act(vb[:, t, :], ps, ACT.Copy, last, *start)) or dvb[-1], banks=fb),
                *[tiles_T("in2", 6 + p, H3, 8, cp(lambda j, p=p: ma[:, 4 * p + j, :], dma_, flipped), banks=fb)
                  for p in range(2)],
                *[tiles_T("in2", 8 + p, H3, 8, cp(lambda j, p=p: mb[:, 4 * p + j, :], dmb), banks=fb)
                  for p in range(2)]))
            z = ve(lambda e: e.memset(hid, 0.0), *start)
            hv = hid.rearrange("p (a c) -> p a c", a=2)
            for a in range(2):
                last = mm(PS[:, a, 0:15], hid15[0:15, 128 * a:128 * a + 128], ident[0:15, 0:15], True, True,
                          hid_ok[a], bank_free[a])
                i_h = vcopy(hv[:, a, 0:15], PS[:, a, 0:15], last, z)
                bank_free[a] = i_h
            fill.step(1)
            z = ve(lambda e: e.memset(hrep, 0.0), *start)
            i_hr = vcopy(hrep.rearrange("p (g c) -> p g c", g=4)[:, :, 0:16],
                         hid[:, 16:32].rearrange("p (o c) -> p o c", o=1).broadcast_to([128, 4, 16]), i_h, z)
            z = ve(lambda e: e.memset(vblk, 0.0), *start)
            for hk in range(2):
                rows = slice(64 * hk, 64 * hk + 64)
                l1 = mm(PS[rows, hk, 0:15], P("kw2")[rows, :], hid[rows, 0:15], True, True, i_h, bank_free[hk])
                l2 = mm(PS[:, 2 + hk, 0:64], hrep[rows, :], P("vw2")[rows, :], True, True, i_hr, bank_free[2 + hk])
                i_k = vcopy(kcT[rows, 0:15], PS[rows, hk, 0:15], l1, *start)
                bank_free[hk] = i_k
                for g in range(4):
                    i_v = vcopy(vblk[32 * g:32 * g + 32, hk, g, :], PS[32 * g:32 * g + 32, 2 + hk, 0:64], l2, z)
                bank_free[2 + hk] = i_v
            a = act(cm[:, 0:15], kcT[:, 0:15], ACT.Square, i_k, *start)
            last = mm(PS[:, 0, 0:15], C("bd64"), cm[:, 0:15], True, True, a, bank_free[0])
            a = act(cm[:, 16:31], PS[:, 0, 0:15], ACT.Ln, last, scale=1.0 / 64, bias=epst)
            bank_free[0] = a
            a = act(cm[:, 16:31], cm[:, 16:31], ACT.Exp, a, scale=-0.5)
            fill.step(1)
            i_kc = stt(kcT[:, 0:15], kcT[:, 0:15], P("k2", 0), cm[:, 16:31], MUL, MUL, a)

            cn = C("cneg").rearrange("p (t c) -> p t c", t=2)
            cok = C("cok").rearrange("p (t c) -> p t c", t=2)
            for hk in range(2):
                bh = B[:, 4 * hk:4 * hk + 4, :]
                bi = vcopy(BC[:, hk, 1, :, 0:15], bh[:, :, 31:256:16], i_B)
                for g in range(4):
                    vcopy(BC[:, hk, 0, g, :], cn[:, 0, :])
                bi = vcopy(BC[:, hk, 0, :, 0:6], bh[:, :, 287:287 + 96:16], ve.last)
                bi = vcopy(BC[:, hk, 0, :, 6:7], bh[:, :, 383:384])
            for hk in range(2):
                rows = slice(64 * hk, 64 * hk + 64)
                b = 2 + hk
                for t in range(2):
                    for g in range(4):
                        last = mm(PS[:, b, 64 * t + 16 * g:64 * t + 16 * g + 15], qa[rows, g, 128 * t:128 * t + 128],
                                  kcT[rows, 0:15], True, True, *([nq, i_kc, bank_free[b]] if not (t or g) else []))
            fill.step(5)
            zp = ve(lambda e: e.memset(Pc, 0.0), *start)
            for hk in range(2):
                a = tt(Lc[:, hk, :, :, 0:15].rearrange("p t g c -> p (t g) c"),
                       PS[:, 2 + hk, 0:128].rearrange("p (n c) -> p n c", c=16)[:, :, 0:15],
                       BC[:, hk, :, :, 0:15].rearrange("p t g c -> p (t g) c"), ADD, last, bi)
                bank_free[2 + hk] = a
            L3 = Lc.rearrange("p k t g c -> p (k t g) c")[:, :, 0:15]
            P3 = Pc.rearrange("p k t g c -> p (k t g) c")[:, :, 0:15]
            a = red(cm[:, 0:16], L3, MAX, a)
            a = tt(L3, L3, cm[:, 0:16].rearrange("p (n o) -> p n o", o=1).broadcast_to([128, 16, 15]), SUB, a)
            a = act(L3, L3, ACT.Exp, a)
            for hk in range(2):
                for t in range(2):
                    e1 = tt(Lc[:, hk, t, :, 0:15], Lc[:, hk, t, :, 0:15],
                            cok[:, t:t + 1, 0:15].broadcast_to([128, 4, 15]), MUL, a)
            a = red(cm[:, 0:16], L3, ADD, e1)
            a = ts(cm[:, 0:16], cm[:, 0:16], 1e-30, MAX, a)
            a = recip(cm[:, 16:32], cm[:, 0:16], a)
            g5 = ga.rearrange("p t (h b) -> p t h b", b=3)
            for hk in range(2):
                for t in range(2):
                    n = 8 * hk + 4 * t
                    a2 = tt(cm[:, 16 + n:20 + n], cm[:, 16 + n:20 + n], g5[:, t, 4 * hk:4 * hk + 4, 0], MUL, a, dga)
            i_pc = tt(P3, L3, cm[:, 16:32].rearrange("p (n o) -> p n o", o=1).broadcast_to([128, 16, 15]), MUL, a2, zp)
            for hk in range(2):
                b = 4 + hk
                for t in range(2):
                    last = transpose(PS[:, b, 128 * t:128 * t + 128], Pc[:, hk, t, :, :].rearrange("p g c -> p (g c)"),
                                     i_pc, bank_free[b])
                i_pct = act(PcT[:, hk, :, :].rearrange("p t n -> p (t n)"), PS[:, b, 0:256], ACT.Copy, last, *start)
                bank_free[b] = i_pct

            items = [(c, hk, br) for c in range(4) for br in range(2) for hk in range(2)]

            def logits(it, t1, t0, waits):
                c, hk, br = it
                rows = slice(64 * hk, 64 * hk + 64)
                mm(t1, qa[rows, c, 128:256], kvT[rows, 2 + br, :], True, True, waits, skip=True)
                return mm(t0, qa[rows, c, 0:128], kvT[rows, 2 + br, 0:128], False, True, skip=True)

            def out_of(i, it):
                c, hk, br = it
                b = 4 + c % 2
                return (PS[64 * hk:64 * hk + 64, b, 0:256], br == 0, False, [bank_free[b]])

            o_done = []

            def extra(i, it, out, last):
                c, hk, br = it
                if br == 1:
                    for t in range(2):
                        last = mm(out[:, 128 * t:128 * t + 128], vblk[:, hk, c, :], PcT[:, hk, t, :], False, t == 1,
                                  i_pct, i_v, skip=True)
                    if hk == 1:
                        b = 4 + c % 2
                        bank_free[b] = act(onsa[:, c, :], PS[:, b, 0:256], ACT.Copy, last)
                        o_done.append(bank_free[b])

            def mult(it):
                c, hk, br = it
                return g5[:, ::-1, c + 4 * hk, 1 + br]

            softmax_pv(items, logits, lambda it: B[:, it[0] + 4 * it[1], :],
                       lambda it, st: vnsa[:, st, 128 * it[2] + 64 * it[1]:128 * it[2] + 64 * it[1] + 64],
                       out_of, mult, L, PT, sm, [nq, nk1, nk2, dvn, i_B, dga], extra, (fill, 1))

            onsa_hi = kvTf
            rounded(kvTf, qaf, onsaf, osbf)
            n_ok = []

            def onsa_parts():
                for c in range(4):
                    n_ok.append(parts_of(onsa[:, c, :], onsa_hi[:, 256 * c:256 * c + 256], o_done))
                    yield n_ok[-1]

            fill.gens.append(onsa_parts())
            sig = []

            def sigmoids():
                fill.drain()
                sig.append(act(ma_f, ma_f, ACT.Sigmoid, dma_))
                sig.append(act(mb_f, mb_f, ACT.Sigmoid, dmb))

            sb_done = stick(qb, kb, vb, osb, sq, r, [dqb, dkb, dvb, nq, nk1, nk2], fill, sigmoids)
            fill.drain()

            b_ok = [parts_of(osb[:, c, :], qaf[:, 256 * c:256 * c + 256], sb_done[c]) for c in range(4)]
            u_read = state["hT"]
            n3, s3 = ((R(h_).rearrange("p (c t) -> p c t", c=4), R(l_)) for h_, l_ in ((onsa_hi, onsa), (qaf, osb)))
            gated, up_ok = {}, {}

            def up_n(j, ps, last):
                gated[j] = tt(ma[:, j, :], ps, ma[:, j, :], MUL, last, sig[0])
                return gated[j]

            def up_s(j, ps, last):
                i2 = tt(mb[:, j, :], ps, mb[:, j, :], MUL, last, sig[1])
                i3 = po(lambda e: e.tensor_tensor(hT[:, j, :], ma[:, j, :], mb[:, j, :], ADD), gated[j], i2, u_read)
                up_ok[j] = parts_of(hT[:, j, :], hhi[:, 256 * j:256 * j + 256], i3, u_read, q=po)
                return i2

            def by_turns(a, b):
                for x, y in zip(a, b):
                    yield x
                    yield y

            lin(by_turns(tiles_T("upn", 0, n3, 4, up_n, n_ok, banks=(0, 1, 2, 3)),
                         tiles_T("ups", 0, s3, 4, up_s, b_ok, banks=(4, 5, 6, 7))))
            residual("out2", H3, 8, [up_ok[c] for c in range(8)], lambda c: mod[:, 16 + c:17 + c])
            phase()
            hid_hi, hid_lo = arena[:, 1024:9216], arena[:, 9216:17408]
            rounded(*[x[:, 2048 * i:2048 * i + 2048] for x in (hid_hi, hid_lo) for i in range(4)])
            rb = [arena[:, 17408 + 256 * i:17664 + 256 * i] for i in range(4)]
            h_done, squared = [], []

            def hidden(p):
                def evict(j, ps, last):
                    i = 4 * p + j
                    w = slice(256 * i, 256 * i + 256)
                    if squared:
                        n, sq_ = squared.pop()
                        h_done.append(parts_of(hid_lo[:, n], hid_hi[:, n], sq_))
                    rr = act(rb[i % 4], ps, ACT.Relu, last, *state["barrier"], used.get(i - 4))
                    used[i] = tt(hid_lo[:, w], rb[i % 4], rb[i % 4], MUL, rr, *state["barrier"])
                    squared.append((w, used[i]))
                    return rr
                return tiles_T("w1", p, H3, 8, evict)

            used = {}
            first = stream(*[hidden(p) for p in range(8)])
            rms_T(lambda c: gs2[:, c:c + 1], i_g2, first=first, shift=lambda c: mod[:, 24 + c:25 + c])
            run_all(first)
            n, sq_ = squared.pop()
            h_done.append(parts_of(hid_lo[:, n], hid_hi[:, n], sq_))
            hid3 = [tuple(R(x[:, 2048 * i:2048 * i + 2048]).rearrange("p (c t) -> p c t", c=8) for x in (hid_hi, hid_lo))
                    for i in range(4)]
            residual("w2", hid3, 32, h_done, lambda c: mod[:, 40 + c:41 + c])

        def stick(qb, kb, vb, osb, sq, r, deps, fill, after):
            n = 8
            lg, p_ok, o_done = {}, {}, []
            cum_ok, a_use, y_ok = {}, {}, {}
            A1 = [sq[:, 384 * i:384 * i + 384] for i in range(3)]
            A2 = [sq[:, 1152 + 384 * i:1152 + 384 * i + 384] for i in range(2)] + [r[:, 0:384]]
            def stage_a(i):
                rows = slice(64 * (i % 2), 64 * (i % 2) + 64)
                c, b = i // 2, i % 4
                ps = PS[:, b, 0:384]
                mm(ps[:, 0:256], kb[rows, c, 0:128], qb[rows, c, :], True, False, deps, bank_free[b], skip=True)
                mm(ps[:, 256:384], kb[rows, c, 128:256], qb[rows, c, 128:256], False, False, skip=True)
                mm(ps[:, 0:128], ident, C("sbm"), False, False, skip=True)
                lg[i] = mm(ps[:, 256:384], ident, C("sbm"), False, False, skip=True)
                x, y = A1[i % 3], A2[i % 3]
                a = act(x, ps, ACT.Abs, lg[i], cum_ok.get(i - 3), deps)
                a = act(x, x, ACT.Exp, a, scale=-1.0)
                a = act(x, x, ACT.Ln, a, bias=onet)
                p_ok[i] = stt(x, ps, 0.0, x, MAX, ADD, a)

            def stage_b(i):
                b = i % 4
                ps = PS[:, b, 0:384]
                x, y = A1[i % 3], A2[i % 3]
                mm(ps[:, 0:256], C("ntri"), x[:, 0:256], False, False, p_ok[i], skip=True)
                mm(ps[:, 128:256], C("nones"), x[:, 256:384], False, False, skip=True)
                cum_ok[i] = mm(ps[:, 256:384], C("ntri"), x[:, 256:384], False, True, skip=True)
                y_ok[i] = bank_free[b] = act(y, ps, ACT.Exp, cum_ok[i], a_use.get(i - 3), deps)

            def stage_c(i):
                y = A2[i % 3]
                ob = 4 + (i // 2) % 2
                out = PS[64 * (i % 2):64 * (i % 2) + 64, ob, 0:256]
                mm(out, vb[:, 0, 64 * i:64 * i + 64], y[:, 0:256], True, False, y_ok[i], bank_free[ob], skip=True)
                a_use[i] = mm(out[:, 128:256], vb[:, 1, 64 * i:64 * i + 64], y[:, 256:384], False, True, skip=True)
                if i % 2:
                    bank_free[ob] = act(osb[:, i // 2, :], PS[:, ob, 0:256], ACT.Copy, a_use[i])
                    o_done.append(bank_free[ob])

            for i in range(n + 3):
                if i < n:
                    stage_a(i)
                fill.step(1)
                if 2 <= i < n + 2:
                    stage_b(i - 2)
                if i == n + 1:
                    after()
                if i >= 3:
                    stage_c(i - 3)
            return o_done

        steps = [even_layer, lambda: peer_layer(0), odd_layer, lambda: peer_layer(1), last_block]
        for s in steps[:stop]:
            s()
        done = [sp(lambda e, c=c: e.dma_start(io["out"][:, 256 * c:256 * c + 256], xT[:, c, :]), state["x"][c], dma=s_out)
                for c in range(8)]
        sp(lambda e: e.nop(), done[7])

        counts = {}
        for q in (pe, ve, ac, po, sp):
            n = 0
            for ins in q.items:
                if ins.sem is not None:
                    counts[id(ins.sem)] = ins.value = counts.get(id(ins.sem), 0) + 16
                elif ins.signals:
                    n += 1
                    ins.value = n

        def emit(q, e):
            seen = {}
            for ins in q.items:
                for w in ins.waits:
                    s = w.sem if w.sem is not None else w.queue.own
                    if seen.get(id(s), 0) < w.value:
                        seen[id(s)] = w.value
                        e.wait_ge(s, w.value)
                r = ins.fn(e)
                if ins.sem is not None:
                    r.then_inc(ins.sem, 16)
                elif ins.signals:
                    r.then_inc(q.own, 1)

        block = ctx.enter_context(nc.Block())
        block.sync(lambda e: emit(sp, e))
        block.gpsimd(lambda e: emit(po, e))
        block.scalar(lambda e: emit(ac, e))
        block.vector(lambda e: emit(ve, e))
        block.tensor(lambda e: emit(pe, e))


def pack(w, ranges):
    kc = w.shape[0] // 128
    v = w.reshape(kc, 128, w.shape[1])
    return np.concatenate([np.ascontiguousarray(v[:, :, lo:hi].transpose(1, 0, 2)).reshape(-1) for lo, hi in ranges])


def layout(inputs):
    g = {k: np.asarray(v) for k, v in inputs.items()}
    a = {}
    a["cst"] = constants()
    cols = np.zeros((128, NCOL), np.float32)

    def put(name, m):
        lo, hi = COL[name]
        cols[: m.shape[0], lo:hi] = m

    col = lambda v: v.reshape(-1, 128).T
    twice = lambda v: np.concatenate([v, v], 0)
    put("ev_g", col(g["ev_norm_mix"][0]))
    put("od_g", col(g["od_norm_mix"][0]))
    put("f0", col(g["ffn_norm"][0]))
    put("f1", col(g["ffn_norm"][1]))
    put("n1", col(g["norm1_g_2"][0]))
    put("n2", col(g["norm2_g_2"][0]))
    put("cw", g["ev_conv_w"][0].reshape(31, 4, 128).transpose(2, 0, 1).reshape(128, 124))
    put("cb", col(g["ev_conv_b"][0]))
    put("lng", col(g["ev_conv_ln_g"][0]))
    put("lnb", col(g["ev_conv_ln_b"][0]))
    put("gb", col(g["ev_gate_b"][0]))
    put("glag", col(g["ev_gla_norm_g"][0]))
    put("qg", twice(g["od_q_norm_g"][0])[:, None])
    put("kg", twice(g["od_k_norm_g"][0])[:, None])
    put("fb", g["od_fgate_b"][0][:, None])
    put("c", col(g["c_2"][0]))
    put("adab", col(g["ada_b_2"][0]))
    put("q2", twice(g["q_norm_g_2"][0])[:, None])
    put("k2", twice(g["k_norm_g_2"][0].T))
    put("pos", twice(g["cmp_pos_2"][0].T))
    put("kw2", twice(g["cmp_k_w2_2"][0]))
    put("vw2", twice(g["cmp_v_w2_2"][0]))
    a["cols"] = cols
    a["xT"] = np.ascontiguousarray(g["x"][0].T.reshape(8, 128, T).transpose(1, 0, 2)).reshape(128, 8 * T)
    a["gw2"] = g["ev_gate_w2"][0]
    a["rel"] = g["rel_bias_2"]
    a["ev_in"] = pack(g["ev_w_in"][0], EV_RANGES)
    a["ev_out"] = pack(g["ev_w_out"][0], FULL)
    a["od_in"] = pack(g["od_w_in"][0], OD_RANGES)
    a["od_out"] = pack(g["od_w_out"][0], FULL)
    for i in range(2):
        a[f"wq{i}"] = pack(g["peer_wq"][i], WQ_RANGES)
        a[f"keys{i}"] = np.ascontiguousarray(g["peer_keys"][i].reshape(16, 128, 128).transpose(2, 0, 1)).reshape(-1)
        a[f"u{i}"] = np.ascontiguousarray(g["peer_u"][i].reshape(128, 128, 8, 128).transpose(1, 3, 2, 0)).reshape(-1)
        a[f"v{i}"] = np.ascontiguousarray(g["peer_v"][i].reshape(128, 128, 1024).transpose(1, 0, 2)).reshape(-1)
    a["ada"] = pack(g["ada_w_2"][0], ADA_RANGES)
    a["in2"] = pack(g["w_in_2"][0][:, IN_ORDER], IN_RANGES)
    w1 = [g[n][0].reshape(32, 64, 64).transpose(1, 0, 2).reshape(64, 2048) for n in ("cmp_k_w1_2", "cmp_v_w1_2")]
    blocks = np.zeros((2, 2, 64, 32, 2, 64), np.float32)
    for i in range(2):
        for h in range(2):
            blocks[i, h, :, :, h, :] = w1[i].reshape(64, 32, 64)
    a["cw1"] = blocks.reshape(-1)
    a["upn"] = pack(g["w_up_nsa_2"][0][QPERM], UP_RANGES)
    a["ups"] = pack(g["w_up_sb_2"][0], UP_RANGES)
    a["out2"] = pack(g["w_out_2"][0], FULL)
    a["w1"] = pack(g["mlp_w1_2"][0], W1_RANGES)
    a["w2"] = pack(g["mlp_w2_2"][0], W2_RANGES)
    return {k: np.ascontiguousarray(v) for k, v in a.items()}


def kernel(**inputs):
    import concourse.bacc as _bacc
    from concourse.bass_utils import run_bass_kernel_spmd as _run

    arrays = layout(inputs)
    nc = _bacc.Bacc("TRN2", target_bir_lowering=False, num_devices=1)
    program(nc, declare(nc, arrays))
    r = _run(nc, [{f"in_{k}": v for k, v in arrays.items()}], core_ids=[0])
    out = np.asarray(r.results[0]["out_0"]).reshape(128, 8, T)
    return np.ascontiguousarray(out.transpose(2, 1, 0)).reshape(1, T, D)
```
